# Optimizing a Trainium2 kernel written in Bass

```python
import math
import jax, jax.numpy as jnp
from jax import lax
import numpy as np

D_MODEL = 1024
BATCH = 1
SEQ = 512
DEPTH = 2
DEC_BATCH = 8
DEC_SEQ = 1
PAST_LEN = 1024
PAGE_SIZE = 128

DN_HEADS = 4
DN_DK = 128
DN_DV = 128
DN_CONV = 4
DN_CHUNK = 64
DA_HEADS = 4
DA_DH = 64
DA_DV = 2 * DA_DH
FFN_DIM = ((8 * D_MODEL // 3 + 127) // 128) * 128
PLE_DIM = 256
Q_BLOCK = 128
RMS_EPS = 1e-6

DN_QK = DN_HEADS * DN_DK
DN_V = DN_HEADS * DN_DV
DN_CONV_CH = 2 * DN_QK + DN_V
DA_QK = DA_HEADS * 2 * DA_DH
DA_V = DA_HEADS * DA_DV
IN_WIDTHS = (DN_CONV_CH, DN_V, DN_HEADS, DN_HEADS, DA_QK, DA_QK, DA_V, D_MODEL, D_MODEL)
D_IN = DN_CONV_CH + DN_V + 2 * DN_HEADS + 2 * DA_QK + DA_V + 2 * D_MODEL

kernel_name = "hybrid_deltanet_diffattn_macaron_step"

def rmsnorm(x, g):
    xf = x.astype(jnp.float32)
    y = xf * lax.rsqrt(jnp.mean(xf * xf, axis=-1, keepdims=True) + RMS_EPS)
    return (y * g.astype(jnp.float32)).astype(x.dtype)

def l2norm(x):
    xf = x.astype(jnp.float32)
    return xf * lax.rsqrt(jnp.sum(xf * xf, axis=-1, keepdims=True) + 1e-6)

def swiglu(h, w1, w3, w2):
    return (jax.nn.silu(h @ w1) * (h @ w3)) @ w2

def split_in(u):
    idx, acc = [], 0
    for w_ in IN_WIDTHS[:-1]:
        acc += w_
        idx.append(acc)
    return jnp.split(u, idx, axis=-1)

def causal_conv(u, buf, w):
    T = u.shape[1]
    full = jnp.concatenate([buf.astype(u.dtype), u], axis=1)
    out = full[:, 0:T] * w[0]
    for j in range(1, DN_CONV):
        out = out + full[:, j:j + T] * w[j]
    return jax.nn.silu(out), full[:, -(DN_CONV - 1):]

def delta_chunked(q, k, v, g, beta, s0):
    B, T, H, DK = q.shape
    DV = v.shape[-1]
    C = DN_CHUNK
    N = T // C

    def blk(a):
        a = a.reshape((B, N, C, H) + a.shape[3:])
        return a.transpose((1, 0, 3, 2) + tuple(range(4, a.ndim)))

    q, k, v, g, beta = blk(q), blk(k), blk(v), blk(g), blk(beta)
    gc = jnp.cumsum(g, axis=-1)
    idx = jnp.arange(C)
    incl = idx[:, None] >= idx[None, :]
    strict = idx[:, None] > idx[None, :]
    diff = gc[..., :, None] - gc[..., None, :]
    L = jnp.where(incl, jnp.exp(jnp.where(incl, diff, 0.0)), 0.0)
    kb = k * beta[..., None]
    A = jnp.where(strict, jnp.einsum('nbhid,nbhjd->nbhij', kb, k) * L, 0.0)
    M = A + jnp.eye(C, dtype=A.dtype)
    rhs = jnp.concatenate([v * beta[..., None], kb * jnp.exp(gc)[..., None]], axis=-1)
    X = lax.linalg.triangular_solve(M, rhs, left_side=True, lower=True, unit_diagonal=True)
    val, kcd = X[..., :DV], X[..., DV:]
    attn = jnp.einsum('nbhid,nbhjd->nbhij', q, k) * L
    qd = q * jnp.exp(gc)[..., None]
    kd = k * jnp.exp(gc[..., -1:] - gc)[..., None]
    dl = jnp.exp(gc[..., -1])

    def step(S, xs):
        qd_c, kd_c, val_c, kcd_c, attn_c, dl_c = xs
        v_new = val_c - jnp.einsum('bhck,bhkv->bhcv', kcd_c, S)
        o = jnp.einsum('bhck,bhkv->bhcv', qd_c, S) + jnp.einsum('bhij,bhjv->bhiv', attn_c, v_new)
        S = S * dl_c[..., None, None] + jnp.einsum('bhck,bhcv->bhkv', kd_c, v_new)
        return S, o

    S, o = lax.scan(step, s0, (qd, kd, val, kcd, attn, dl))
    o = o.transpose(1, 0, 3, 2, 4).reshape(B, T, H, DV)
    return o, S

def delta_recurrent(q, k, v, g, beta, s0):
    def step(S, xs):
        q_t, k_t, v_t, g_t, b_t = xs
        S = S * jnp.exp(g_t)[..., None, None]
        u = v_t - jnp.einsum('bhk,bhkv->bhv', k_t, S)
        S = S + jnp.einsum('bhk,bhv->bhkv', k_t * b_t[..., None], u)
        o = jnp.einsum('bhk,bhkv->bhv', q_t, S)
        return S, o

    xs = tuple(jnp.moveaxis(a, 1, 0) for a in (q, k, v, g, beta))
    S, o = lax.scan(step, s0, xs)
    return jnp.moveaxis(o, 0, 1), S

def gated_delta_branch(qkv_raw, z, b_raw, a_raw, conv_buf, s0, w_conv, a_log, dt_bias, g_norm, chunked):
    B, T, _ = qkv_raw.shape
    qkv, new_buf = causal_conv(qkv_raw, conv_buf, w_conv)
    q, k, v = jnp.split(qkv, [DN_QK, 2 * DN_QK], axis=-1)
    q = l2norm(q.reshape(B, T, DN_HEADS, DN_DK)) * (DN_DK ** -0.5)
    k = l2norm(k.reshape(B, T, DN_HEADS, DN_DK))
    v = v.reshape(B, T, DN_HEADS, DN_DV).astype(jnp.float32)
    beta = jax.nn.sigmoid(b_raw.astype(jnp.float32))
    g = -jnp.exp(a_log.astype(jnp.float32)) * jax.nn.softplus(a_raw.astype(jnp.float32) + dt_bias.astype(jnp.float32))
    s0 = s0.astype(jnp.float32)
    if chunked:
        o, S = delta_chunked(q, k, v, g, beta, s0)
    else:
        o, S = delta_recurrent(q, k, v, g, beta, s0)
    o = rmsnorm(o, g_norm) * jax.nn.silu(z.reshape(B, T, DN_HEADS, DN_DV).astype(jnp.float32))
    return o.reshape(B, T, DN_V).astype(qkv_raw.dtype), S, new_buf

def alibi_slopes(n):
    return 2.0 ** (-8.0 * jnp.arange(1, n + 1, dtype=jnp.float32) / n)

def diff_attend(q, k, v, q_pos, k_pos, lam):
    scale = DA_DH ** -0.5
    q1, q2 = q[..., :DA_DH], q[..., DA_DH:]
    k1, k2 = k[..., :DA_DH], k[..., DA_DH:]
    dist = (q_pos[:, None] - k_pos[None, :]).astype(jnp.float32)
    slopes = alibi_slopes(DA_HEADS)
    bias = jnp.where(dist >= 0, -slopes[:, None, None] * dist, -jnp.inf)
    s1 = jnp.einsum('bqhd,bkhd->bhqk', q1, k1).astype(jnp.float32) * scale + bias
    s2 = jnp.einsum('bqhd,bkhd->bhqk', q2, k2).astype(jnp.float32) * scale + bias
    attn = jax.nn.softmax(s1, axis=-1) - lam * jax.nn.softmax(s2, axis=-1)
    return jnp.einsum('bhqk,bkhv->bqhv', attn, v.astype(jnp.float32))

def diff_attn_prompt(q, k, v, lam):
    B, T = q.shape[:2]
    nb = T // Q_BLOCK
    qb = q.reshape(B, nb, Q_BLOCK, DA_HEADS, 2 * DA_DH).transpose(1, 0, 2, 3, 4)
    k_pos = jnp.arange(T)

    def one(args):
        q_i, i = args
        q_pos = i * Q_BLOCK + jnp.arange(Q_BLOCK)
        return diff_attend(q_i, k, v, q_pos, k_pos, lam)

    o = lax.map(one, (qb, jnp.arange(nb)))
    return o.transpose(1, 0, 2, 3, 4).reshape(B, T, DA_HEADS, DA_DV)

def diff_attn_sample(q, k_new, v_new, cache_k_l, cache_v_l, page_table, lam):
    DB, T = q.shape[:2]
    past_k = cache_k_l[page_table].reshape(DB, -1, DA_HEADS, 2 * DA_DH)
    past_v = cache_v_l[page_table].reshape(DB, -1, DA_HEADS, DA_DV)
    past_len = past_k.shape[1]
    k_all = jnp.concatenate([past_k, k_new.astype(past_k.dtype)], axis=1)
    v_all = jnp.concatenate([past_v, v_new.astype(past_v.dtype)], axis=1)
    q_pos = past_len + jnp.arange(T)
    k_pos = jnp.arange(past_len + T)
    return diff_attend(q, k_all, v_all, q_pos, k_pos, lam)

def decoder_layer(x, ple, w, layer_idx, conv_buf, s0, cache_k_l, cache_v_l, page_table, is_prompt):
    B, T, _ = x.shape
    h = rmsnorm(x, w['norm_ffn1'])
    x = x + 0.5 * swiglu(h, w['ffn1_w1'], w['ffn1_w3'], w['ffn1_w2'])
    h = rmsnorm(x, w['norm_mix'])
    u = h @ w['w_in']
    dn_qkv, dn_z, dn_b, dn_a, da_q, da_k, da_v, gate_a, gate_b = split_in(u)
    ya, s_new, buf_new = gated_delta_branch(dn_qkv, dn_z, dn_b, dn_a, conv_buf, s0, w['dn_conv_w'],
                                            w['dn_a_log'], w['dn_dt_bias'], w['dn_norm'], is_prompt)
    da_q = da_q.reshape(B, T, DA_HEADS, 2 * DA_DH)
    da_k = da_k.reshape(B, T, DA_HEADS, 2 * DA_DH)
    da_v = da_v.reshape(B, T, DA_HEADS, DA_DV)
    lam_init = 0.8 - 0.6 * math.exp(-0.3 * layer_idx)
    lam = (jnp.exp(jnp.sum(w['lq1'].astype(jnp.float32) * w['lk1'].astype(jnp.float32)))
           - jnp.exp(jnp.sum(w['lq2'].astype(jnp.float32) * w['lk2'].astype(jnp.float32))) + lam_init)
    if is_prompt:
        o = diff_attn_prompt(da_q, da_k, da_v, lam)
    else:
        o = diff_attn_sample(da_q, da_k, da_v, cache_k_l, cache_v_l, page_table, lam)
    yb = (rmsnorm(o, w['da_norm']) * (1.0 - lam_init)).reshape(B, T, DA_V).astype(x.dtype)
    m = jax.nn.sigmoid(gate_a) * (ya @ w['w_a']) + jax.nn.sigmoid(gate_b) * (yb @ w['w_b'])
    x = x + m @ w['w_o']
    h = rmsnorm(x, w['norm_ffn2'])
    x = x + 0.5 * swiglu(h, w['ffn2_w1'], w['ffn2_w3'], w['ffn2_w2'])
    gate = jax.nn.sigmoid(rmsnorm(x, w['norm_ple']) @ w['w_ple_gate'])
    x = x + gate * (ple.astype(x.dtype) @ w['w_ple'])
    return x, da_k, da_v, s_new, buf_new

def setup_inputs(seed: int = 0) -> dict:
    key = jax.random.key(seed)
    ks = iter(jax.random.split(key, 48))

    def nrm(shape, s):
        return jax.random.normal(next(ks), shape, jnp.float32) * s

    def gain(shape):
        return 1.0 + nrm(shape, 0.02)

    n_pages = PAST_LEN // PAGE_SIZE
    used = DEC_BATCH * n_pages
    n_pool = used + (used + 3) // 4
    page_table = jax.random.permutation(next(ks), n_pool)[:used].reshape(DEC_BATCH, n_pages).astype(jnp.int32)
    dt = jnp.exp(jax.random.uniform(next(ks), (DEPTH, DN_HEADS), jnp.float32, math.log(1e-3), math.log(1e-1)))
    dt_bias = dt + jnp.log(-jnp.expm1(-dt))
    a_log = jnp.log(jax.random.uniform(next(ks), (DEPTH, DN_HEADS), jnp.float32, 1.0, 16.0))
    return {
        "x_prompt": nrm((BATCH, SEQ, D_MODEL), 1.0),
        "x_sample": nrm((DEC_BATCH, DEC_SEQ, D_MODEL), 1.0),
        "cache_k": nrm((DEPTH, n_pool, PAGE_SIZE, DA_HEADS, 2 * DA_DH), 1.0),
        "cache_v": nrm((DEPTH, n_pool, PAGE_SIZE, DA_HEADS, DA_DV), 1.0),
        "state_delta": nrm((DEPTH, DEC_BATCH, DN_HEADS, DN_DK, DN_DV), 0.5),
        "state_conv": nrm((DEPTH, DEC_BATCH, DN_CONV - 1, DN_CONV_CH), 1.0),
        "page_table": page_table,
        "p_prompt": nrm((DEPTH, BATCH, SEQ, PLE_DIM), 1.0),
        "p_sample": nrm((DEPTH, DEC_BATCH, DEC_SEQ, PLE_DIM), 1.0),
        "norm_ffn1": gain((DEPTH, D_MODEL)),
        "ffn1_w1": nrm((DEPTH, D_MODEL, FFN_DIM), D_MODEL ** -0.5),
        "ffn1_w3": nrm((DEPTH, D_MODEL, FFN_DIM), D_MODEL ** -0.5),
        "ffn1_w2": nrm((DEPTH, FFN_DIM, D_MODEL), FFN_DIM ** -0.5),
        "norm_mix": gain((DEPTH, D_MODEL)),
        "w_in": nrm((DEPTH, D_MODEL, D_IN), D_MODEL ** -0.5),
        "dn_conv_w": nrm((DEPTH, DN_CONV, DN_CONV_CH), 0.5),
        "dn_a_log": a_log,
        "dn_dt_bias": dt_bias,
        "dn_norm": gain((DEPTH, DN_DV)),
        "da_lambda_q1": nrm((DEPTH, DA_DH), 0.1),
        "da_lambda_k1": nrm((DEPTH, DA_DH), 0.1),
        "da_lambda_q2": nrm((DEPTH, DA_DH), 0.1),
        "da_lambda_k2": nrm((DEPTH, DA_DH), 0.1),
        "da_norm": gain((DEPTH, DA_DV)),
        "w_a": nrm((DEPTH, DN_V, D_MODEL), DN_V ** -0.5),
        "w_b": nrm((DEPTH, DA_V, D_MODEL), DA_V ** -0.5),
        "w_o": nrm((DEPTH, D_MODEL, D_MODEL), D_MODEL ** -0.5),
        "norm_ffn2": gain((DEPTH, D_MODEL)),
        "ffn2_w1": nrm((DEPTH, D_MODEL, FFN_DIM), D_MODEL ** -0.5),
        "ffn2_w3": nrm((DEPTH, D_MODEL, FFN_DIM), D_MODEL ** -0.5),
        "ffn2_w2": nrm((DEPTH, FFN_DIM, D_MODEL), FFN_DIM ** -0.5),
        "norm_ple": gain((DEPTH, D_MODEL)),
        "w_ple_gate": nrm((DEPTH, D_MODEL, D_MODEL), D_MODEL ** -0.5),
        "w_ple": nrm((DEPTH, PLE_DIM, D_MODEL), PLE_DIM ** -0.5),
        "norm_final": gain((D_MODEL,)),
    }

def reference(x_prompt, x_sample, cache_k, cache_v, state_delta, state_conv, page_table, p_prompt, p_sample,
              norm_ffn1, ffn1_w1, ffn1_w3, ffn1_w2, norm_mix, w_in, dn_conv_w, dn_a_log, dn_dt_bias, dn_norm,
              da_lambda_q1, da_lambda_k1, da_lambda_q2, da_lambda_k2, da_norm, w_a, w_b, w_o,
              norm_ffn2, ffn2_w1, ffn2_w3, ffn2_w2, norm_ple, w_ple_gate, w_ple, norm_final):
    xp, xs = x_prompt, x_sample
    kp, vp, sp, cp = [], [], [], []
    ksm, vsm, ssm, csm = [], [], [], []
    for i in range(DEPTH):
        w = dict(norm_ffn1=norm_ffn1[i], ffn1_w1=ffn1_w1[i], ffn1_w3=ffn1_w3[i], ffn1_w2=ffn1_w2[i],
                 norm_mix=norm_mix[i], w_in=w_in[i], dn_conv_w=dn_conv_w[i], dn_a_log=dn_a_log[i],
                 dn_dt_bias=dn_dt_bias[i], dn_norm=dn_norm[i], lq1=da_lambda_q1[i], lk1=da_lambda_k1[i],
                 lq2=da_lambda_q2[i], lk2=da_lambda_k2[i], da_norm=da_norm[i], w_a=w_a[i], w_b=w_b[i],
                 w_o=w_o[i], norm_ffn2=norm_ffn2[i], ffn2_w1=ffn2_w1[i], ffn2_w3=ffn2_w3[i],
                 ffn2_w2=ffn2_w2[i], norm_ple=norm_ple[i], w_ple_gate=w_ple_gate[i], w_ple=w_ple[i])
        B = xp.shape[0]
        zero_buf = jnp.zeros((B, DN_CONV - 1, DN_CONV_CH), xp.dtype)
        zero_s = jnp.zeros((B, DN_HEADS, DN_DK, DN_DV), jnp.float32)
        xp, k_i, v_i, s_i, c_i = decoder_layer(xp, p_prompt[i], w, i, zero_buf, zero_s,
                                               None, None, None, True)
        kp.append(k_i); vp.append(v_i); sp.append(s_i); cp.append(c_i)
        xs, k_i, v_i, s_i, c_i = decoder_layer(xs, p_sample[i], w, i, state_conv[i], state_delta[i],
                                               cache_k[i], cache_v[i], page_table, False)
        ksm.append(k_i); vsm.append(v_i); ssm.append(s_i); csm.append(c_i)
    y_prompt = rmsnorm(xp, norm_final)
    y_sample = rmsnorm(xs, norm_final)
    return (y_prompt, y_sample,
            jnp.stack(kp), jnp.stack(vp), jnp.stack(sp), jnp.stack(cp),
            jnp.stack(ksm), jnp.stack(vsm), jnp.stack(ssm), jnp.stack(csm))


_drawn_inputs = setup_inputs


def setup_inputs(seed=0):
    import zlib

    import numpy as np

    out = dict(_drawn_inputs(seed))
    spreads = {}
    factors = {'norm_ffn1': 3.883,
     'dn_norm': 30.659,
     'da_lambda_k1': 3.523,
     'da_norm': 23.132,
     'norm_ffn2': 6.247,
     'norm_ple': 64.0,
     'norm_final': 8.032}
    for name, (base, spread) in spreads.items():
        noise = np.random.default_rng([zlib.crc32(name.encode()), seed]).standard_normal(out[name].shape)
        drawn = base * np.exp(spread * noise) if base else spread * noise
        out[name] = __import__('jax').numpy.asarray(drawn.astype(out[name].dtype))
    for name, factor in factors.items():
        out[name] = (out[name] * factor).astype(out[name].dtype)
    return out
```

```python
import math
from contextlib import ExitStack

import numpy as np
import concourse.bass as bass
from concourse import mybir

ALU = mybir.AluOpType
ACT = mybir.ActivationFunctionType
AXX = mybir.AxisListType.X
F32 = mybir.dt.float32
R32 = mybir.dt.float32r
I32 = mybir.dt.int32

P = 128
D = 1024
KD = D // P
SEQ = 512
NSEQ = 8
T = SEQ + NSEQ
HT = T // 2
DEPTH = 2
H = 4
FF = 2816
KF = FF // P
PLE = 256
PAGE = 128
NPAGE = 8
PAST = PAGE * NPAGE
CONV = 4
NCONV = 12
HD = 64
EPS = 1e-6
IN_Z = 1536
IN_BA = 2048
IN_Q = 2056
IN_GA = 3592
IN_GB = 4616
U_CONV, U_Z, U_Q, U_K, U_V, NU = 0, 12, 16, 20, 24, 28
SCALE = HD ** -0.5
NEG = -1.0e30

C_ID, C_ONE, C_SLOPE, C_LI, C_OML, C_EPS, NCC = 0, 128, 256, 260, 262, 264, 266
LV = 7
M_INCL, M_STRICT, M_UP, M_LOW0, M_LVT, M_HALF, M_DIST = 0, 128, 256, 384, 512, 512 + 128 * LV, 768 + 128 * LV
M_PAST = M_DIST + 512
NCM = M_PAST + NPAGE * H


def core_constants():
    c = np.zeros((P, NCC), np.float32)
    c[:, C_ID:C_ID + P] = np.eye(P)
    c[:, C_ONE:C_ONE + P] = 1.0
    for h in range(H):
        c[:, C_SLOPE + h] = 2.0 ** (-8.0 * (h + 1) / H) / SCALE
    for l in range(DEPTH):
        li = 0.8 - 0.6 * math.exp(-0.3 * l)
        c[:, C_LI + l] = li
        c[:, C_OML + l] = 1.0 - li
    c[:, C_EPS] = EPS
    return c


def mixer_constants():
    c = np.zeros((P, NCM), np.float32)
    i, j = np.arange(P)[:, None], np.arange(P)[None, :]
    c[:, M_INCL:M_INCL + P] = i >= j
    c[:, M_STRICT:M_STRICT + P] = i > j
    c[:, M_UP:M_UP + P] = i <= j
    for l in range(LV):
        low = (i >> (l + 1) == j >> (l + 1)) & (i >> l & 1 == 1) & (j >> l & 1 == 0)
        if l == 0:
            c[:, M_LOW0:M_LOW0 + P] = low
        c[:, M_LVT + P * l:M_LVT + P * (l + 1)] = low.T
    c[:HD, M_HALF:M_HALF + P] = 1.0
    c[HD:, M_HALF + P:M_HALF + 2 * P] = 1.0
    x = np.arange(SEQ)[None, :] - (SEQ - P)
    c[:, M_DIST:M_DIST + SEQ] = np.where(x <= i, x - i, NEG)
    for g in range(NPAGE):
        for h in range(H):
            slope = 2.0 ** (-8.0 * (h + 1) / H) / SCALE
            c[:, M_PAST + g * H + h] = -slope * (PAST - g * PAGE - np.arange(P))
    return c


class Track:

    def __init__(self, sem, steps, iters, bias):
        self.sem, self.steps, self.iters, self.bias = sem, steps, iters, bias

    def at(self, step, layer, i=0):
        n = len(self.steps)
        return layer * (self.iters * n) + i * n + (self.bias + self.steps.index(step) + 1)

    def begin(self, layer, i=0):
        n = len(self.steps)
        return layer * (self.iters * n) + i * n + self.bias


def hybrid_trunk(nc, A, O):
    ctx = ExitStack()
    with ctx:
        base = [(nc.sbuf_base + 31) // 32 * 32]

        def at(name, shape, dt, offset):
            return nc.alloc_sbuf_tensor_at(name, shape, dt, offset=offset)

        def size(shape):
            return (int(np.prod(shape[1:])) * 4 + 31) // 32 * 32

        class Region:
            def __init__(self, start):
                self.at = start

            def sb(self, name, shape, dt=F32):
                t = at(name, shape, dt, self.at)
                self.at += size(shape)
                return t

        top = Region(base[0])
        sb = top.sb
        X = sb("X", [P, KD, T])
        Hh = sb("Hh", [P, KD, T], R32)
        Hl = sb("Hl", [P, KD, T], R32)
        raw = sb("raw", [P, 2, 2048])
        whi = sb("whi", [P, 2, 2048], R32)
        wlo = sb("wlo", [P, 2, 2048], R32)
        CC = sb("CC", [P, NCC])
        R = sb("R", [P, T])
        acc = sb("acc", [P, T])
        gains = sb("gains", [P, 76])
        convw = sb("convw", [P, 96])
        bcast = sb("bcast", [P, 18])
        gda = sb("gda", [P, 1])
        nlam = sb("nlam", [P, 1])
        pages = sb("pages", [1, NSEQ * NPAGE], I32)
        PT = sb("PT", [P, 2, T])
        PTl = at("PTl", [P, 2, T], R32, top.at - size([P, 2, T]))
        tmp_at = top.at
        ta = sb("ta", [P, 2, T])
        tb = sb("tb", [P, 2, T])
        PTh = at("PTh", [P, 2, T], R32, top.at - size([P, 2, T]))
        g_at = top.at
        Gh = sb("Gh", [P, KF, T], R32)
        Gl = sb("Gl", [P, KF, T], R32)
        assert top.at <= nc.sbuf_usable_end, (top.at, nc.sbuf_usable_end)
        end = nc.sbuf_usable_end

        mix = Region(g_at)
        U = mix.sb("U", [P, NU, T])
        cm_at = mix.at
        CM = mix.sb("CM", [P, NCM])
        beta = mix.sb("beta", [P, 5, H])
        gcs = mix.sb("gcs", [P, 4, H])
        eg = mix.sb("eg", [P, 4, H])
        ekd = mix.sb("ekd", [P, 4, H])
        dl = mix.sb("dl", [P, 4, H])
        sab = mix.sb("sab", [P, 2, H, NSEQ])
        rawtail = mix.sb("rawtail", [P, NCONV, 11])
        scr_at = mix.at
        s0 = Region(scr_at)
        wba = s0.sb("wba", [P, KD, P])
        wbah = s0.sb("wbah", [P, KD, P], R32)
        wbal = s0.sb("wbal", [P, KD, P], R32)
        BA = s0.sb("BA", [2 * H, T])
        assert s0.at <= end
        s1 = Region(scr_at)
        scin = s1.sb("scin", [24, NCONV * P])
        tailtok = s1.sb("tailtok", [11, NCONV * P])
        csam = s1.sb("csam", [P, NCONV, NSEQ])
        ctmp = s1.sb("ctmp", [P, NCONV, NSEQ])
        assert s1.at <= end
        s2 = Region(tmp_at)
        bt = s2.sb("bt", [P, 5, 2 * H])
        ax = s2.sb("ax", [P, 5, H])
        sp = s2.sb("sp", [P, 5, H])
        gg = s2.sb("gg", [P, 5, H])
        kdx = s2.sb("kdx", [P, 4, H])
        sexp = s2.sb("sexp", [NSEQ, 2, H, NSEQ])
        d = Region(scr_at)
        W4 = [P, H, P]
        Qs, Ks, Vs = d.sb("Qs", W4), d.sb("Ks", W4), d.sb("Vs", W4)
        Vt, Ds, At, ATl = d.sb("Vt", W4), d.sb("Ds", W4), d.sb("At", W4), d.sb("ATl", W4)
        ATs, attn, Ti = d.sb("ATs", W4), d.sb("attn", W4), d.sb("Ti", W4)
        assert d.at <= end
        d2 = Region(tmp_at)
        Ui, W1, S, Kt = d2.sb("Ui", W4), d2.sb("W1", W4), d2.sb("S", W4), d2.sb("Kt", W4)
        a = Region(scr_at)
        qs, ks, vs = a.sb("qs", [P, T]), a.sb("ks", [P, T]), a.sb("vs", [P, T])
        ktok, vtok = a.sb("ktok", W4), a.sb("vtok", W4)
        aT = a.sb("aT", [P, 4, SEQ])
        stok = a.sb("stok", [NSEQ, 2, H, P])
        mx, nm, sm, rc = (a.sb(n, [P, 2]) for n in ("mx", "nm", "sm", "rc"))
        assert a.at <= end
        a2 = Region(tmp_at)
        sc = a2.sb("sc", [P, 2, SEQ])
        pr = a2.sb("pr", [P, 2, SEQ])
        f = Region(scr_at)
        dq = f.sb("dq", [P, 2, H, NSEQ])
        dv = f.sb("dv", [P, H, NSEQ])
        qk = f.sb("qk", [P, H, NSEQ])
        bk = f.sb("bk", [P, H, NSEQ])
        aq = f.sb("aq", [P, H, NSEQ])
        Sall = f.sb("Sall", [P, NSEQ, NPAGE, 2 * H])
        own = f.sb("own", [P, 2, H, NSEQ])
        ms, eo, ls = (f.sb(n, [P, NSEQ, 2 * H]) for n in ("ms", "eo", "ls"))
        po = f.sb("po", [P, NSEQ, H])
        Pc = f.sb("Pc", [P, NSEQ, NPAGE, H])
        cm64 = f.sb("cm64", [64, 1])
        dg64 = f.sb("dg64", [64, 64])
        ucol, ocol = f.sb("ucol", [P, H]), f.sb("ocol", [P, H])
        kvp = [f.sb(f"kvp{n}", [P, 4, SEQ]) for n in range(2)]
        assert f.at <= end
        f2 = Region(tmp_at)
        diag = f2.sb("diag", W4)
        st = f2.sb("st", W4)
        stn = f2.sb("stn", W4)
        vsum = f2.sb("vsum", [P, SEQ])
        Yh = at("Yh", [P, KD, T], R32, g_at)
        Yl = at("Yl", [P, KD, T], R32, g_at + U_K * T * 4)
        Mh = at("Mh", [P, KD, T], R32, g_at + 8 * T * 4)
        gt = Region(cm_at)
        Ml = gt.sb("Ml", [P, KD, T], R32)
        sg = gt.sb("sg", [P, 2, 2, T])
        mt = gt.sb("mt", [P, 2, T])
        gt2 = gt.sb("gt2", [P, 2, T])
        ptok = at("ptok", [P, 5, PLE], F32, g_at + U_Q * T * 4)
        assert gt.at <= end, (gt.at, end)
        z = Region(g_at)
        xtok = z.sb("xtok", [P, 5, D])
        grow = z.sb("grow", [76, P])
        crow = z.sb("crow", [96, P])
        lrow = z.sb("lrow", [1, 8 * HD])
        lpr = z.sb("lpr", [1, 4 * HD])
        row = z.sb("row", [1, 24])
        yr = Region(g_at)
        yT = yr.sb("yT", [P, KD, T])
        ytok = yr.sb("ytok", [P, 5, D])

        ps = ctx.enter_context(nc.psum_tensor("ps", [P, 8, 512], F32))
        ident = CC[:, C_ID:C_ID + P]
        ones = CC[:, C_ONE:C_ONE + P]
        eps = CC[:, C_EPS:C_EPS + 1]

        def sem(name):
            return ctx.enter_context(nc.semaphore(name))

        NB = 118
        NE = 102
        NH = 32
        FREE = 2
        raw_ready = [sem("raw_ready0"), sem("raw_ready1")]
        hi_done = sem("hi_done")
        split_done = sem("split_done")
        block_done = sem("block_done")
        evac = sem("evac")
        hh_ready = sem("hh_ready")
        h_ready = sem("h_ready")
        sq_ready = sem("sq_ready")
        acc_ready = sem("acc_ready")
        sum_ready = sem("sum_ready")
        rt_ready = sem("rt_ready")
        ta_ready, silu_done = sem("ta_ready"), sem("silu_done")
        g_ready, gh_done, gl_done = sem("g_ready"), sem("gh_done"), sem("gl_done")
        outs = sem("outs")
        passed = {n: sem(f"passed_{n}") for n in ("sp", "pe", "dve")}
        NORMS = 4

        def stand(eng, name):
            eng.sem_inc(passed[name], 1)

        def pair(b):
            return ps[:, b:b + 2, 0:HT]

        def halves(t):
            return t.rearrange("p (a c) -> p a c", a=2)

        def track(name, steps, iters=1, bias=0):
            return Track(sem(name), steps.split(), iters, bias)

        levels = range(1, LV)
        loads = sem("loads")
        start_pe, start_dve, start_act = sem("start_pe"), sem("start_dve"), sem("start_act")
        cv_ready = sem("cv_ready")
        cv_done = sem("cv_done")
        cm_load, ba_load, sc_load = sem("cm_load"), sem("ba_load"), sem("sc_load")
        tail_out, s_out, tok_out, stok_out, st_out = (sem(n) for n in ("tail_out", "s_out", "tok_out", "stok_out", "st_out"))
        st_load, p_load = sem("st_load"), sem("p_load")
        k_load = [sem(f"k_load{n}") for n in range(2)]
        v_load = [sem(f"v_load{n}") for n in range(2)]
        kfree, vfree = sem("kfree"), sem("vfree")
        fin, fin_pe, fin_dve = sem("fin"), sem("fin_pe"), sem("fin_dve")
        t_pe = track("t_pe", "ba tok gcum sab tails states")
        t_dve = track("t_dve", "ba bt ax g kdx sexp sab csam")
        t_act = track("t_act", "w beta softplus decays asam tailtok csam")
        t_pool = track("t_pool", "w")
        l_act = track("l_act", "sq0 sq1 rt0 rt1", 4)
        l_pe = track("l_pe", "sum0 sum1", 4)
        l_dve = track("l_dve", "n0 n1", 4, bias=1)
        d_pe = track("d_pe", "gram vt at " + " ".join(f"w{l} p{l}" for l in levels) + " ks vnew out state", 4)
        d_dve = track("d_dve", "diag dm attn at " + " ".join(f"w{l} u{l}" for l in levels) + " w vn o state", 4)
        d_act = track("d_act", "exp qd tok", 4)
        a_pe = track("a_pe", "tok " + " ".join(f"score{q} at{q}" for q in range(4)) + " out", 4)
        a_dve = track("a_dve", "staged " + " ".join(f"max{q} attn{q}" for q in range(4)) + " out", 4)
        a_act = track("a_act", "tok " + " ".join(f"exp{q} at{q}" for q in range(4)), 4)
        q_pe = track("q_pe", "own mt mb sum")
        q_dve = track("q_dve", "cols own max col sub done o")
        q_act = track("q_act", "exp")
        k_pe = track("k_pe", "q sm ub", NSEQ)
        k_dve = track("k_dve", "diag ucol sm", NSEQ)
        v_pe = track("v_pe", "o", NSEQ, bias=1)
        v_dve = track("v_dve", "sum", NSEQ, bias=1)
        n_act = track("n_act", "z sq0 sq1 rt0 rt1 h0 h1", 4)
        n_pe = track("n_pe", "sum0 sum1", 4)
        n_dve = track("n_dve", "y0 y1 l0 l1", 4)
        g_act = track("g_act", "sa sb h", 4)
        g_dve = track("g_dve", "m l", 4)
        p_pe = track("p_pe", "t")
        p_act = track("p_act", "hi")
        p_dve = track("p_dve", "t lo")
        e_act = track("e_act", "s", 4)
        e_dve = track("e_dve", "x", 4)

        block = ctx.enter_context(nc.Block())

        @block.sync
        def _(sp_):
            sp_.dma_start(xtok[:, 0:4, :], A["x_prompt"][0].rearrange("(t p) f -> p t f", p=P)).then_inc(loads, 16)
            sp_.dma_start(xtok[0:NSEQ, 4, :], A["x_sample"][:, 0, :]).then_inc(loads, 16)
            sp_.dma_start(CC[:, :], A["const_core"]).then_inc(loads, 16)
            for l in range(DEPTH):
                for n, name in enumerate(("norm_ffn1", "norm_mix", "norm_ffn2", "norm_ple")):
                    r0 = (NORMS * l + n) * KD
                    sp_.dma_start(grow[r0:r0 + KD, :], A[name][l].rearrange("(c p) -> c p", p=P)).then_inc(loads, 16)
            sp_.dma_start(grow[64:72, :], A["norm_final"].rearrange("(c p) -> c p", p=P)).then_inc(loads, 16)
            sp_.dma_start(grow[72:74, :], A["dn_norm"]).then_inc(loads, 16)
            sp_.dma_start(grow[74:76, :], A["da_norm"]).then_inc(loads, 16)
            sp_.dma_start(crow[:, :], A["dn_conv_w"].rearrange("l j (c p) -> (l j c) p", p=P)).then_inc(loads, 16)
            for n, name in enumerate(("da_lambda_q1", "da_lambda_q2", "da_lambda_k1", "da_lambda_k2")):
                sp_.dma_start(lrow[0:1, n * 2 * HD:(n + 1) * 2 * HD],
                              A[name].rearrange("(o l) c -> o (l c)", o=1)).then_inc(loads, 16)
            sp_.dma_start(row[0:1, 2:10], A["dn_a_log"].rearrange("(o l) h -> o (l h)", o=1)).then_inc(loads, 16)
            sp_.dma_start(row[0:1, 10:18], A["dn_dt_bias"].rearrange("(o l) h -> o (l h)", o=1)).then_inc(loads, 16)
            sp_.dma_start(pages[:, :], A["page_table"].rearrange("(o s) g -> o (s g)", o=1)).then_inc(loads, 16)

            def slot(L, n, p):
                sp_.wait_ge(split_done, L * NB + (n + 1))

            def load(p, dst_k, cols, src):
                sp_.dma_start(raw[:, p, dst_k[0] * cols:dst_k[1] * cols].rearrange("p (k c) -> p k c", c=cols),
                              src).then_inc(raw_ready[p], 16)

            def block8(L, n, p, w, c0, k=KD, cols=256):
                slot(L, n, p)
                src = w[L].rearrange("(k p) c -> p k c", p=P)
                for a0, a1 in ((0, k // 2), (k // 2, k)):
                    load(p, (a0, a1), cols, src[:, a0:a1, bass.ds(c0, cols)])

            def ffn(L, nb, w1, w3, w2):
                with sp_.Fori(0, KF // 2) as i:
                    for p in range(2):
                        slot(L, nb + 2 * i + p, p)
                        for s, w in enumerate((w1, w3)):
                            sp_.dma_start(raw[:, p, :].rearrange("p (k s c) -> p s k c", s=2, c=P)[:, s],
                                          w[L].rearrange("(k p) c -> p k c", p=P)[:, :, bass.ds(i * 256 + p * P, P)]
                                          ).then_inc(raw_ready[p], 16)
                with sp_.Fori(0, KD // 2) as i:
                    for j in range(4):
                        m, hf = j // 2, j % 2
                        slot(L, nb + KF + 4 * i + j, j % 2)
                        src = w2[L, hf * 11 * P:(hf + 1) * 11 * P, :].rearrange("(k p) c -> p k c", p=P)
                        for a0, a1 in ((0, 6), (6, 11)):
                            load(j % 2, (a0, a1), P, src[:, a0:a1, bass.ds(i * 256 + m * P, P)])

            def proj(L, nb, n, c0):
                with sp_.Fori(0, n) as i:
                    for p in range(2):
                        block8(L, nb + 2 * i + p, p, A["w_in"], i * 512 + (c0 + 256 * p))

            with sp_.Fori(0, DEPTH) as L:
                ffn(L, 0, A["ffn1_w1"], A["ffn1_w3"], A["ffn1_w2"])
                sp_.wait_ge(evac, L * NE + (FREE + 30))
                sp_.dma_start(CM[:, :], A["const_mix"]).then_inc(cm_load, 16)
                sp_.dma_start(wba[:, :, :], A["w_in"][L].rearrange("(k p) c -> p k c", p=P)[:, :, IN_BA:IN_BA + P]
                              ).then_inc(ba_load, 16)
                proj(L, 38, 3, 0)
                proj(L, 44, 1, IN_Z)
                proj(L, 46, 3, IN_Q)
                block8(L, 52, 0, A["w_in"], IN_GA)
                block8(L, 53, 1, A["w_in"], IN_GB)
                sp_.wait_ge(t_dve.sem, t_dve.at("bt", L))
                sp_.dma_start(scin[:, :], A["state_conv"][L].rearrange("s j c -> (s j) c")).then_inc(sc_load, 16)
                sp_.wait_ge(t_act.sem, t_act.at("tailtok", L))
                sp_.dma_start(O["conv_prompt"][L, 0], tailtok[0:3, :]).then_inc(tail_out, 16)
                sp_.dma_start(O["conv_sample"][L, :, 2, :], tailtok[3:11, :]).then_inc(tail_out, 16)
                sp_.dma_start(O["conv_sample"][L, :, 0:2, :], A["state_conv"][L, :, 1:3, :]).then_inc(tail_out, 16)
                sp_.wait_ge(d_dve.sem, d_dve.at("state", L, 3))
                sp_.dma_start(O["delta_prompt"][L, 0].rearrange("h k v -> k h v"), S[:, :, :]).then_inc(s_out, 16)
                with sp_.Fori(0, H) as h:
                    sp_.wait_ge(a_act.sem, a_act.at("tok", L, h))
                    for o, t in (("k_prompt", ktok), ("v_prompt", vtok)):
                        sp_.dma_start(O[o][L, 0, :, bass.ds(h, 1), :].rearrange("(t p) o c -> p t (o c)", p=P),
                                      t[:, :, :]).then_inc(tok_out, 16)
                sp_.dma_start(O["k_sample"][L, :, 0], stok[:, 0, :, :]).then_inc(stok_out, 16)
                sp_.dma_start(O["v_sample"][L, :, 0], stok[:, 1, :, :]).then_inc(stok_out, 16)
                sp_.wait_ge(q_dve.sem, q_dve.at("cols", L))
                stand(sp_, "sp")
                with sp_.Fori(0, NSEQ) as s:
                    sp_.dma_start(st[:, :, :], A["state_delta"][L, bass.ds(s, 1)].rearrange("o h k v -> k (o h) v")
                                  ).then_inc(st_load, 16)
                    for half in range(2):
                        sp_.wait_ge(kfree, L * 16 + s * 2 + (half + 1))
                        for g in range(4):
                            pg = sp_.value_load(pages[0:1, bass.ds(s * NPAGE + (half * 4 + g), 1)],
                                                min_val=0, max_val=A["cache_k"].shape[1] - 1)
                            sp_.dma_start(kvp[half][:, g, :], A["cache_k"][L, bass.ds(pg, 1)].rearrange("o k h c -> k (o h c)")
                                          ).then_inc(k_load[half], 16)
                    sp_.wait_ge(k_dve.sem, k_dve.at("sm", L, s))
                    sp_.dma_start(O["delta_sample"][L, bass.ds(s, 1)].rearrange("o h k v -> k (o h) v"), stn[:, :, :]
                                  ).then_inc(st_out, 16)
                with sp_.Fori(0, NSEQ) as s:
                    for half in range(2):
                        if half:
                            sp_.wait_ge(v_dve.sem, v_dve.begin(L, s))
                        else:
                            sp_.wait_ge(vfree, L * NSEQ + s + 1)
                        for g in range(4):
                            pg = sp_.value_load(pages[0:1, bass.ds(s * NPAGE + (half * 4 + g), 1)],
                                                min_val=0, max_val=A["cache_v"].shape[1] - 1)
                            sp_.dma_start(kvp[half][:, g, :], A["cache_v"][L, bass.ds(pg, 1)].rearrange("o k h c -> k (o h c)")
                                          ).then_inc(v_load[half], 16)
                sp_.wait_ge(n_dve.sem, n_dve.at("l1", L, 3))
                sp_.dma_start(ptok[:, 0:4, :], A["p_prompt"][L, 0].rearrange("(t p) f -> p t f", p=P)).then_inc(p_load, 16)
                sp_.dma_start(ptok[0:NSEQ, 4, :], A["p_sample"][L, :, 0, :]).then_inc(p_load, 16)

                def pair2(i, n, first=False):
                    if not first:
                        block8(L, n, 0, A["w_in"], i * 256 + IN_GA)
                        block8(L, n + 1, 1, A["w_in"], i * 256 + IN_GB)
                    block8(L, n + 2, 0, A["w_a"], i * 256, k=4)
                    block8(L, n + 3, 1, A["w_b"], i * 256, k=4)

                pair2(0, 52, first=True)
                with sp_.Fori(1, 4) as i:
                    pair2(i, 4 * i + 52)
                with sp_.Fori(0, 2) as i:
                    for p in range(2):
                        block8(L, 68 + 2 * i + p, p, A["w_o"], i * 512 + 256 * p)
                ffn(L, 72, A["ffn2_w1"], A["ffn2_w3"], A["ffn2_w2"])
                with sp_.Fori(0, 4) as i:
                    block8(L, 110 + 2 * i, 0, A["w_ple_gate"], i * 256)
                    block8(L, 111 + 2 * i, 1, A["w_ple"], i * 256, k=2)
            sp_.wait_ge(fin, 1)
            sp_.dma_start(O["y_prompt"][0].rearrange("(t p) f -> p t f", p=P), ytok[:, 0:4, :]).then_inc(outs, 16)
            sp_.dma_start(O["y_sample"][:, 0, :], ytok[0:NSEQ, 4, :]).then_inc(outs, 16)
            sp_.wait_ge(outs, 32)
            sp_.wait_ge(tail_out, DEPTH * 48)
            sp_.wait_ge(s_out, DEPTH * 16)
            sp_.wait_ge(tok_out, DEPTH * H * 32)
            sp_.wait_ge(stok_out, DEPTH * 32)
            sp_.wait_ge(st_out, (DEPTH * NSEQ + 1) * 16)

        def eq(x):
            return x.unsqueeze(2).broadcast_to([x.shape[0], x.shape[1], P])

        def heads(x):
            return x.unsqueeze(1).broadcast_to([P, H, P])

        def bank4(b):
            return ps[:, b, :].rearrange("p (h c) -> p h c", h=H)

        @block.tensor
        def _(pe):
            def product(slot, cols, ks, ms, rh, rl, bank, starts=True, stops=True, before=None, after=None, k0=0):
                for k in range(ks):
                    if before:
                        before(k)
                    for m in range(ms):
                        o = k * cols + m * P
                        h, l = whi[:, slot, o:o + P], wlo[:, slot, o:o + P]
                        for n, (w, x) in enumerate(((h, rh), (h, rl), (l, rh))):
                            for c in range(2):
                                last = nc.tensor.matmul(ps[:, bank + 2 * m + c, 0:HT], w,
                                                        x[:, k0 + k, c * HT:(c + 1) * HT],
                                                        start=starts and k == 0 and n == 0,
                                                        stop=stops and k == ks - 1 and n == 2)
                last.then_inc(block_done, 1)

            def split_ready(L, n):
                pe.wait_ge(split_done, L * NB + n + (FREE + 1))

            def banks_ready(L, u):
                pe.wait_ge(evac, L * NE + u + 1)

            def h_wait(L, nj):
                return lambda k: pe.wait_ge(h_ready, L * NH + (FREE + KD * nj + k + 1))

            def block8(L, n, u, p, nj, k=KD, rh=Hh, rl=Hl, first=False, k0=0):
                split_ready(L, n)
                banks_ready(L, u)
                if p == 1 and nj is not None:
                    pe.wait_ge(rt_ready, L * NORMS + (nj + 1))
                product(p, 256, k, 2, rh, rl, 4 * p, before=h_wait(L, nj) if first else None, k0=k0)

            def norm_sum(L, nj):
                pe.wait_ge(acc_ready, L * NH + KD * (nj + 1))
                for c in range(2):
                    last = nc.tensor.matmul(ps[:, 6 + c, 0:HT], ones, acc[:, c * HT:(c + 1) * HT], start=True, stop=True)
                last.then_inc(sum_ready, 1)

            def ffn(L, nb, ub, nj, hid):
                with pe.Fori(0, KF // 2) as i:
                    for p in range(2):
                        block8(L, nb + 2 * i + p, ub + 2 * i + p, p, nj, first=p == 0)
                with pe.Fori(0, KD // 2) as i:
                    for j in range(4):
                        m, hf = j // 2, j % 2
                        split_ready(L, nb + KF + 4 * i + j)
                        if hf == 0:
                            banks_ready(L, ub + KF + 2 * i + m)
                        pe.wait_ge(gl_done, L * 2 * KF + (hid * KF + 11 * (hf + 1) + FREE))
                        product(hf, P, 11, 1, Gh, Gl, 4 * m, starts=hf == 0, stops=hf == 1, k0=11 * hf)

            def tr(out, in_, rows=P):
                return nc.tensor.transpose(out, in_, CC[0:rows, C_ID:C_ID + rows])

            def to_features(bank, tok, c):
                for t in range(4):
                    tr(ps[:, bank, t * P:(t + 1) * P], tok[:, t, c * P:(c + 1) * P])
                return tr(ps[:, bank + 1, 0:NSEQ], tok[0:NSEQ, 4, c * P:(c + 1) * P], NSEQ)

            pe.wait_ge(loads, 16 * 22)
            tr(ps[:, 0, 0:76], grow[:, :], 76)
            tr(ps[:, 1, 0:96], crow[:, :], 96).then_inc(start_pe, 1)
            pe.wait_ge(start_dve, 2)
            nc.tensor.matmul(ps[:, 2, 0:18], CC[0:1, C_ONE:C_ONE + P], row[0:1, 0:18], start=True, stop=True).then_inc(start_pe, 1)
            for c in range(KD):
                pe.wait_ge(start_dve, 2 + c)
                to_features(4 * (c % 2), xtok, c).then_inc(start_pe, 1)
            pe.wait_ge(start_dve, 2 + KD)
            norm_sum(0, 0)

            with pe.Fori(0, DEPTH) as L:
                ffn(L, 0, 0, 0, 0)
                norm_sum(L, 1)
                with pe.Fori(0, 3) as i:
                    for p in range(2):
                        block8(L, 38 + 2 * i + p, 30 + 2 * i + p, p, 1, first=p == 0)
                for p in range(2):
                    block8(L, 44 + p, 36 + p, p, 1)
                with pe.Fori(0, 3) as i:
                    for p in range(2):
                        block8(L, 46 + 2 * i + p, 38 + 2 * i + p, p, 1)
                pe.wait_ge(t_pool.sem, t_pool.at("w", L))
                pe.wait_ge(evac, L * NE + (44 + FREE))
                for k in range(KD):
                    for n, (w, x) in enumerate(((wbah, Hh), (wbah, Hl), (wbal, Hh))):
                        for c in range(2):
                            last = nc.tensor.matmul(ps[:, c, 0:HT], w[:, k, :], x[:, k, c * HT:(c + 1) * HT],
                                                    start=k == 0 and n == 0, stop=k == KD - 1 and n == 2)
                last.then_inc(t_pe.sem, 1)
                pe.wait_ge(t_dve.sem, t_dve.at("ba", L))
                stand(pe, "pe")
                for t in range(4):
                    tr(ps[:, 2, t * 8:t * 8 + 8], BA[:, t * P:(t + 1) * P], 8)
                tr(ps[0:NSEQ, 2, 32:40], BA[:, SEQ:T], 8).then_inc(t_pe.sem, 1)
                pe.wait_ge(t_dve.sem, t_dve.at("g", L))
                pe.wait_ge(cm_load, L * 16 + 16)
                gv = gg[:, 0:4, :].rearrange("p t h -> p (t h)")
                nc.tensor.matmul(ps[:, 3, 0:16], CM[:, M_UP:M_UP + P], gv, start=True, stop=True)
                nc.tensor.matmul(ps[:, 3, 16:32], ones, gv, start=True, stop=True).then_inc(t_pe.sem, 1)
                pe.wait_ge(t_dve.sem, t_dve.at("sexp", L))
                nc.tensor.matmul(ps[:, 4, 0:64], CC[0:NSEQ, C_ONE:C_ONE + P], sexp[:, :, :, :].rearrange("p a h s -> p (a h s)"),
                                 start=True, stop=True).then_inc(t_pe.sem, 1)
                for c in range(NCONV):
                    last = tr(ps[0:11, 5 + c // 4, (c % 4) * P:(c % 4 + 1) * P], rawtail[:, c, :])
                last.then_inc(t_pe.sem, 1)
                pe.wait_ge(sc_load, L * 16 + 16)
                stand(pe, "pe")
                for c in range(NCONV):
                    last = tr(ps[:, 0, c * 24:(c + 1) * 24], scin[:, c * P:(c + 1) * P], 24)
                last.then_inc(t_pe.sem, 1)
                with pe.Fori(0, H) as i:
                    for p in range(2):
                        pe.wait_ge(l_act.sem, l_act.at(f"sq{p}", L, i))
                        for c in range(2):
                            last = nc.tensor.matmul(ps[:, 2 * p + c, 0:HT], ones, tb[:, p, c * HT:(c + 1) * HT],
                                                    start=True, stop=True)
                        last.then_inc(l_pe.sem, 1)
                with pe.Fori(0, 4) as c:
                    def dve(step):
                        pe.wait_ge(d_dve.sem, d_dve.at(step, L, c))

                    def each(bank, lhs, rhs, start=True, stop=True):
                        for h in range(H):
                            last = nc.tensor.matmul(ps[:, bank, h * P:(h + 1) * P], lhs[:, h, :], rhs[:, h, :],
                                                    start=start, stop=stop)
                        return last

                    def each_tr(bank, x):
                        for h in range(H):
                            last = tr(ps[:, bank, h * P:(h + 1) * P], x[:, h, :])
                        return last

                    dve("diag")
                    nc.tensor.matmul(ps[:, 0, :], ones, Ds[:, :, :].rearrange("p h c -> p (h c)"), start=True, stop=True)
                    each(1, Ks, Ks)
                    each(2, Qs, Ks)
                    each_tr(3, Ks).then_inc(d_pe.sem, 1)
                    each_tr(4, Vs).then_inc(d_pe.sem, 1)
                    dve("attn")
                    each_tr(5, At)
                    each_tr(6, attn).then_inc(d_pe.sem, 1)
                    for l in levels:
                        dve(f"u{l - 1}" if l > 1 else "at")
                        each(7, ATl, Ti).then_inc(d_pe.sem, 1)
                        dve(f"w{l}")
                        last = each(5, W1, Ui)
                        if l < LV - 1:
                            last = each(1, Ui, W1)
                        last.then_inc(d_pe.sem, 1)
                    dve(f"u{LV - 1}")
                    each(0, Ks, S).then_inc(d_pe.sem, 1)
                    dve("w")
                    each(2, Ui, W1).then_inc(d_pe.sem, 1)
                    dve("vn")
                    for h in range(H):
                        nc.tensor.matmul(ps[:, 3, h * P:(h + 1) * P], S[:, h, :], Qs[:, h, :], start=True, stop=False)
                        last = nc.tensor.matmul(ps[:, 3, h * P:(h + 1) * P], ATl[:, h, :], attn[:, h, :], start=False, stop=True)
                    last.then_inc(d_pe.sem, 1)
                    each(7, Kt, ATl).then_inc(d_pe.sem, 1)
                with pe.Fori(0, H) as h:
                    pe.wait_ge(a_dve.sem, a_dve.at("staged", L, h))
                    for t in range(4):
                        tr(ps[:, 0, t * P:(t + 1) * P], ks[:, t * P:(t + 1) * P])
                    for t in range(4):
                        tr(ps[:, 1, t * P:(t + 1) * P], vs[:, t * P:(t + 1) * P])
                    tr(ps[0:NSEQ, 2, 0:P], ks[:, SEQ:T])
                    tr(ps[0:NSEQ, 2, P:2 * P], vs[:, SEQ:T]).then_inc(a_pe.sem, 1)

                    def scores(q):
                        if q >= 2:
                            pe.wait_ge(a_dve.sem, a_dve.at(f"max{q - 2}", L, h))
                        n = (q + 1) * P
                        for m in range(2):
                            r = slice(HD * m, HD * (m + 1))
                            last = nc.tensor.matmul(ps[:, 4 + 2 * (q % 2) + m, 0:n], qs[r, q * P:(q + 1) * P], ks[r, 0:n],
                                                    start=True, stop=True)
                        last.then_inc(a_pe.sem, 1)

                    for q in range(4):
                        scores(q)
                        pe.wait_ge(a_dve.sem, a_dve.at(f"attn{q}", L, h))
                        if q:
                            pe.wait_ge(a_act.sem, a_act.at(f"at{q - 1}", L, h))
                        for t in range(q + 1):
                            last = tr(ps[:, 3, t * P:(t + 1) * P], pr[:, 0, t * P:(t + 1) * P])
                        last.then_inc(a_pe.sem, 1)
                    pe.wait_ge(a_act.sem, a_act.at("at3", L, h))
                    for t in range(4):
                        last = nc.tensor.matmul(ps[:, 0, t * P:SEQ], vtok[:, t, :], aT[:, t, t * P:SEQ], start=t == 0, stop=t == 3)
                    last.then_inc(a_pe.sem, 1)
                pe.wait_ge(q_dve.sem, q_dve.at("cols", L))
                nc.tensor.matmul(ps[:, 0, 0:32], ones, qk[:, :, :].rearrange("p h s -> p (h s)"), start=True, stop=True)
                for m in range(2):
                    last = nc.tensor.matmul(ps[:, 0, 32 * (m + 1):32 * (m + 2)], CM[:, M_HALF + P * m:M_HALF + P * (m + 1)],
                                            aq[:, :, :].rearrange("p h s -> p (h s)"), start=True, stop=True)
                last.then_inc(q_pe.sem, 1)
                dflat = diag[:, :, :].rearrange("p h c -> p (h c)")
                with pe.Fori(0, NSEQ) as s:
                    pe.wait_ge(k_dve.sem, k_dve.at("diag", L, s))
                    nc.tensor.matmul(ps[:, 1, :], ones, dflat, start=True, stop=True).then_inc(k_pe.sem, 1)
                    pe.wait_ge(st_load, L * (NSEQ * 16) + s * 16 + 16)
                    for h in range(H):
                        last = nc.tensor.matmul(ps[:, 2, 2 * h:2 * h + 2], st[:, h, :],
                                                dq[:, :, h, bass.ds(s, 1)].rearrange("p a o -> p (a o)"), start=True, stop=True)
                    last.then_inc(k_pe.sem, 1)
                    pe.wait_ge(k_dve.sem, k_dve.at("ucol", L, s))
                    nc.tensor.matmul(ps[:, 3, :], ones, dflat, start=True, stop=True).then_inc(k_pe.sem, 1)
                pe.wait_ge(q_dve.sem, q_dve.at("max", L))
                stand(pe, "pe")
                tr(ps[0:64, 4, 0:P], ms[:, :, :].rearrange("p s m -> p (s m)")).then_inc(q_pe.sem, 1)
                pe.wait_ge(q_dve.sem, q_dve.at("col", L))
                nc.tensor.matmul(ps[:, 5, 0:64], CC[0:64, C_ONE:C_ONE + P], dg64[:, :], start=True, stop=True).then_inc(q_pe.sem, 1)
                pe.wait_ge(q_act.sem, q_act.at("exp", L))
                nc.tensor.matmul(ps[:, 6, :], ones, Sall[:, :, :, :].rearrange("p s g m -> p (s g m)"), start=True, stop=True
                                 ).then_inc(q_pe.sem, 1)
                with pe.Fori(0, NSEQ) as s:
                    pe.wait_ge(v_dve.sem, v_dve.at("sum", L, s))
                    for h in range(H):
                        last = nc.tensor.matmul(ps[:, 7, bass.ds(s + h * NSEQ, 1)], vsum[:, h * P:(h + 1) * P],
                                                CC[:, C_ONE:C_ONE + 1], start=True, stop=True)
                    last.then_inc(v_pe.sem, 1)
                with pe.Fori(0, H) as i:
                    for p in range(2):
                        pe.wait_ge(n_act.sem, n_act.at(f"sq{p}", L, i))
                        for c in range(2):
                            last = nc.tensor.matmul(ps[:, 2 * p + c, 0:HT], ones, tb[:, p, c * HT:(c + 1) * HT],
                                                    start=True, stop=True)
                        last.then_inc(n_pe.sem, 1)
                pe.wait_ge(n_dve.sem, n_dve.at("l1", L, 3))
                stand(pe, "pe")
                with pe.Fori(0, 4) as i:
                    for j in range(4):
                        y = j >= 2
                        block8(L, 52 + 4 * i + j, 44 + 4 * i + j, j % 2, None if y else 1, k=4 if y else KD,
                               rh=Yh if y else Hh, rl=Yl if y else Hl, k0=4 * (j == 3))
                pe.wait_ge(p_load, L * 32 + 32)
                pe.wait_ge(evac, L * NE + (60 + FREE))
                to_features(0, ptok, 0)
                to_features(2, ptok, 1).then_inc(p_pe.sem, 1)
                pe.wait_ge(p_dve.sem, p_dve.at("t", L))
                pe.wait_ge(g_dve.sem, g_dve.at("l", L, 3))
                stand(pe, "pe")
                with pe.Fori(0, 2) as i:
                    for p in range(2):
                        block8(L, 68 + 2 * i + p, 60 + 2 * i + p, p, 1, rh=Mh, rl=Ml)
                norm_sum(L, 2)
                ffn(L, 72, 64, 2, 1)
                norm_sum(L, 3)
                pe.wait_ge(p_dve.sem, p_dve.at("lo", L))
                stand(pe, "pe")
                with pe.Fori(0, 4) as i:
                    block8(L, 110 + 2 * i, 94 + 2 * i, 0, 3, first=True)
                    block8(L, 111 + 2 * i, 95 + 2 * i, 1, 3, k=2, rh=PTh, rl=PTl)
                norm_sum(L, 4)
            pe.wait_ge(fin_dve, 1)
            for t in range(4):
                for c in range(KD):
                    last = tr(ps[:, 2 * t + c // 4, (c % 4) * P:(c % 4 + 1) * P], yT[:, c, t * P:(t + 1) * P])
            last.then_inc(fin_pe, 1)
            pe.wait_ge(fin_dve, 2)
            for c in range(KD):
                last = tr(ps[0:NSEQ, c // 4, (c % 4) * P:(c % 4 + 1) * P], yT[:, c, SEQ:T])
            last.then_inc(fin_pe, 1)

        def split_chunk_act(act, L, nj, m, par, ready):
            ready()
            act.wait_ge(h_ready, L * NH + KD * nj + m + 1)
            nc.scalar.activation(ta[:, par, :], Xc(m), ACT.Square).then_inc(sq_ready, 1)
            nc.scalar.activation(col(Hh, m), Xc(m), ACT.Copy, scale=gain(L, nj, m)).then_inc(hh_ready, 1)

        def split_chunk_dve(dve, L, nj, m, par):
            dve.drain()
            dve.wait_ge(sq_ready, L * NH + KD * nj + m + 1)
            nc.vector.tensor_tensor(acc[:, :], acc[:, :], ta[:, par, :], ALU.add).then_inc(acc_ready, 1)
            dve.wait_ge(hh_ready, L * NH + KD * nj + m + 1)
            nc.vector.scalar_tensor_tensor(out=col(Hl, m), in0=Xc(m), scalar=gain(L, nj, m), in1=col(Hh, m).bitcast(F32),
                                           op0=ALU.mult, op1=ALU.subtract).then_inc(h_ready, 1)

        def col(t, m):
            return t[:, bass.ds(m, 1), :].rearrange("p o t -> p (o t)")

        def Xc(m):
            return col(X, m)

        def gain(L, nj, m):
            return gains[:, bass.ds((L * NORMS + nj) * KD + m, 1)]

        @block.scalar
        def _(act):
            def A_(out, in_, func, **kw):
                return nc.scalar.activation(out, in_, func, **kw)

            def hi(L, n, p, i_half):
                act.wait_ge(block_done, L * NB + n + 1)
                act.wait_ge(raw_ready[p], L * (NB // 2 * 32) + i_half * 32 + 32)
                A_(whi[:, p, :], raw[:, p, :], ACT.Copy).then_inc(hi_done, 1)

            def norm_root(L, nj):
                act.wait_ge(sum_ready, L * NORMS + (nj + 1))
                A_(halves(R[:, :]), pair(6), ACT.Sqrt, scale=1.0 / D, bias=eps).then_inc(rt_ready, 1)

            def x_ready(L, u):
                return lambda: act.wait_ge(evac, L * NE + u + (FREE + 1))

            def ffn(L, nb, ub, nj, hid):
                with act.Fori(0, KF // 2) as i:
                    for p in range(2):
                        m = 2 * i + p
                        hi(L, nb + m + 2, p, i + (nb // 2 + 1))
                        act.wait_ge(ta_ready, L * 2 * KF + m + (hid * KF + 1))
                        A_(ta[:, p, :], ta[:, p, :], ACT.Silu).then_inc(silu_done, 1)
                        act.wait_ge(g_ready, L * 2 * KF + m + (hid * KF + 1))
                        A_(col(Gh, m), tb[:, p, :], ACT.Copy).then_inc(gh_done, 1)
                with act.Fori(0, KD // 2) as i:
                    for j in range(4):
                        hi(L, nb + KF + 4 * i + j + 2, j % 2, 2 * i + (nb // 2 + 11 + j // 2 + 1))
                        if j % 2:
                            m = 2 * i + j // 2
                            split_chunk_act(act, L, nj + 1, m, j // 2, x_ready(L, ub + KF + m))
                norm_root(L, nj + 1)

            act.wait_ge(loads, 16 * 22)
            A_(row[0:1, 2:10], row[0:1, 2:10], ACT.Exp)
            act.wait_ge(start_dve, 1)
            A_(row[0:1, 18:22], row[0:1, 18:22], ACT.Exp).then_inc(start_act, 1)
            for m in range(KD):
                split_chunk_act(act, 0, 0, m, m % 2, lambda: act.wait_ge(start_dve, 3 + m))
            norm_root(0, 0)

            with act.Fori(0, DEPTH) as L:
                hi(L, 0, 0, 0)
                hi(L, 1, 1, 0)
                ffn(L, 0, 0, 0, 0)
                with act.Fori(0, 3) as i:
                    for p in range(2):
                        hi(L, 40 + 2 * i + p, p, i + 20)
                        for q in range(2):
                            act.wait_ge(cv_ready, L * NCONV + (4 * i + 2 * p + q) + 1)
                            A_(U[:, bass.ds(4 * i + 2 * p + q, 1), 0:SEQ].rearrange("p o t -> p (o t)"), ta[:, q, 0:SEQ],
                               ACT.Silu).then_inc(cv_done, 1)
                for p in range(2):
                    hi(L, 46 + p, p, 23)
                act.wait_ge(ba_load, L * 16 + 16)
                A_(wbah[:, :, :], wba[:, :, :], ACT.Copy).then_inc(t_act.sem, 1)
                with act.Fori(0, 3) as i:
                    for p in range(2):
                        hi(L, 48 + 2 * i + p, p, i + 24)
                act.wait_ge(t_dve.sem, t_dve.at("bt", L))
                A_(beta[:, :, :], bt[:, :, 0:H], ACT.Sigmoid).then_inc(t_act.sem, 1)
                act.wait_ge(t_dve.sem, t_dve.at("ax", L))
                A_(sp[:, :, :], ax[:, :, :], ACT.Abs)
                act.drain()
                A_(sp[:, :, :], sp[:, :, :], ACT.Exp, scale=-1.0)
                act.drain()
                A_(sp[:, :, :], sp[:, :, :], ACT.Ln, bias=1.0).then_inc(t_act.sem, 1)
                act.wait_ge(t_dve.sem, t_dve.at("kdx", L))
                A_(eg[:, :, :], gcs[:, :, :], ACT.Exp)
                A_(ekd[:, :, :], kdx[:, :, :], ACT.Exp)
                A_(dl[:, :, :], ps[:, 3, 16:32].rearrange("p (c h) -> p c h", h=H), ACT.Exp).then_inc(t_act.sem, 1)
                A_(sp[0:NSEQ, 4, :], gg[0:NSEQ, 4, :], ACT.Exp).then_inc(t_act.sem, 1)
                act.wait_ge(t_pe.sem, t_pe.at("tails", L))
                A_(tailtok[:, :].rearrange("p (b c) -> p b c", b=3), ps[0:11, 5:8, :], ACT.Copy).then_inc(t_act.sem, 1)
                act.wait_ge(t_dve.sem, t_dve.at("csam", L))
                A_(U[:, 0:NCONV, SEQ:T], csam[:, :, :], ACT.Silu).then_inc(t_act.sem, 1)
                act.drain()
                with act.Fori(0, H) as i:
                    for p in range(2):
                        A_(tb[:, p, :], col(U, i + 4 * p), ACT.Square).then_inc(l_act.sem, 1)
                    for p in range(2):
                        act.wait_ge(l_pe.sem, l_pe.at(f"sum{p}", L, i))
                        act.wait_ge(l_dve.sem, l_dve.begin(L, i))
                        A_(halves(ta[:, p, :]), pair(2 * p), ACT.Sqrt, bias=eps).then_inc(l_act.sem, 1)
                with act.Fori(0, 4) as c:
                    act.wait_ge(d_dve.sem, d_dve.at("dm", L, c))
                    A_(Ds[:, :, :], W1[:, :, :], ACT.Exp, scale=-1.0).then_inc(d_act.sem, 1)
                    A_(ATs[:, :, :], bank4(0), ACT.Exp).then_inc(d_act.sem, 1)
                    act.wait_ge(d_pe.sem, d_pe.at("vt", L, c))
                    A_(Kt[:, :, :], bank4(3), ACT.Copy)
                    A_(Vt[:, :, :], bank4(4), ACT.Copy).then_inc(d_act.sem, 1)
                with act.Fori(0, H) as h:
                    act.wait_ge(tok_out, L * (H * 32) + h * 32 + 32)
                    act.wait_ge(a_pe.sem, a_pe.at("tok", L, h))
                    A_(ktok[:, :, :], bank4(0), ACT.Copy)
                    A_(vtok[:, :, :], bank4(1), ACT.Copy)
                    A_(stok[:, :, bass.ds(h, 1), :].rearrange("p a o c -> p a (o c)"),
                       ps[0:NSEQ, 2, 0:2 * P].rearrange("p (a c) -> p a c", a=2), ACT.Copy).then_inc(a_act.sem, 1)
                    for q in range(4):
                        n = (q + 1) * P
                        act.wait_ge(a_dve.sem, a_dve.at(f"max{q}", L, h))
                        for m in range(2):
                            last = A_(pr[:, m, 0:n], sc[:, m, 0:n], ACT.Exp, scale=SCALE, bias=nm[:, m:m + 1],
                                      accum_out=sm[:, m:m + 1])
                        last.then_inc(a_act.sem, 1)
                        act.wait_ge(a_pe.sem, a_pe.at(f"at{q}", L, h))
                        A_(aT[:, 0:q + 1, q * P:(q + 1) * P], ps[:, 3, 0:n].rearrange("p (t c) -> p t c", c=P), ACT.Copy
                           ).then_inc(a_act.sem, 1)
                act.wait_ge(q_dve.sem, q_dve.at("sub", L))
                A_(Sall[:, :, :, :], Sall[:, :, :, :], ACT.Exp, scale=SCALE)
                A_(eo[:, :, :], eo[:, :, :], ACT.Exp, scale=SCALE).then_inc(q_act.sem, 1)
                act.wait_ge(q_dve.sem, q_dve.at("o", L))
                act.wait_ge(st_out, L * (NSEQ * 16) + (NSEQ * 16 + 16))
                with act.Fori(0, H) as i:
                    A_(col(U, i + U_Z), col(U, i + U_Z), ACT.Silu).then_inc(n_act.sem, 1)
                    for p, c in enumerate((8, U_Q)):
                        A_(tb[:, p, :], col(U, i + c), ACT.Square).then_inc(n_act.sem, 1)
                    for p in range(2):
                        act.wait_ge(n_pe.sem, n_pe.at(f"sum{p}", L, i))
                        A_(halves(ta[:, p, :]), pair(2 * p), ACT.Sqrt, scale=1.0 / P, bias=eps).then_inc(n_act.sem, 1)
                    for p, c in enumerate((8, U_Q)):
                        act.wait_ge(n_dve.sem, n_dve.at(f"y{p}", L, i))
                        A_(col(Yh, i + 4 * p), col(U, i + c), ACT.Copy).then_inc(n_act.sem, 1)
                with act.Fori(0, 4) as i:
                    for j in range(4):
                        hi(L, 54 + 4 * i + j, j % 2, 2 * i + (27 + j // 2))
                        if j < 2:
                            act.wait_ge(evac, L * NE + (44 + 4 * i + j) + (FREE + 1))
                            A_(sg[:, j, :, :], sg[:, j, :, :], ACT.Sigmoid).then_inc(g_act.sem, 1)
                    act.wait_ge(g_dve.sem, g_dve.at("m", L, i))
                    A_(Mh[:, bass.ds(2 * i, 2), :], mt[:, :, :], ACT.Copy).then_inc(g_act.sem, 1)
                with act.Fori(0, 2) as i:
                    for p in range(2):
                        hi(L, 70 + 2 * i + p, p, i + 35)
                        for q in range(2):
                            split_chunk_act(act, L, 2, 4 * i + 2 * p + q, q, x_ready(L, 60 + 2 * i + p))
                norm_root(L, 2)
                ffn(L, 72, 64, 2, 1)
                A_(PTh[:, :, :], PT[:, :, :], ACT.Copy).then_inc(p_act.sem, 1)
                with act.Fori(0, 3) as i:
                    hi(L, 112 + 2 * i, 0, i + 56)
                    act.wait_ge(evac, L * NE + (94 + 2 * i) + (FREE + 1))
                    A_(ta[:, :, :], ta[:, :, :], ACT.Sigmoid).then_inc(e_act.sem, 1)
                    hi(L, 113 + 2 * i, 1, i + 56)
                act.wait_ge(evac, L * NE + (100 + FREE + 1))
                A_(ta[:, :, :], ta[:, :, :], ACT.Sigmoid).then_inc(e_act.sem, 1)
                act.wait_ge(e_dve.sem, e_dve.at("x", L, 3))
                with act.Fori(0, 4) as i:
                    for p in range(2):
                        split_chunk_act(act, L, 4, 2 * i + p, p, lambda: None)
                norm_root(L, 4)
            act.wait_ge(fin_pe, 1)
            for t in range(4):
                last = A_(ytok[:, t, :].rearrange("p (b c) -> p b c", b=2), ps[:, 2 * t:2 * t + 2, :], ACT.Copy)
            last.then_inc(start_act, 1)

        @block.gpsimd
        def _(pool):
            for s_, v in ((split_done, FREE), (block_done, FREE), (evac, FREE), (h_ready, FREE), (gl_done, FREE),
                          (l_dve.sem, 1), (v_pe.sem, 1), (kfree, 2), (vfree, 1), (v_dve.sem, 1), (tok_out, 32), (st_out, 16), (cv_done, 2)):
                pool.sem_inc(s_, v)

            def lo(L, n, p):
                pool.wait_ge(hi_done, L * NB + n + 1)
                nc.gpsimd.tensor_tensor(wlo[:, p, :], raw[:, p, :], whi[:, p, :].bitcast(F32), ALU.subtract
                                        ).then_inc(split_done, 1)

            def blocks(L, n0, pairs):
                with pool.Fori(0, pairs) as i:
                    for p in range(2):
                        lo(L, n0 + 2 * i + p, p)

            def ffn(L, nb, hid):
                with pool.Fori(0, KF // 2) as i:
                    for p in range(2):
                        lo(L, nb + 2 + 2 * i + p, p)
                        pool.wait_ge(gh_done, L * 2 * KF + 2 * i + (hid * KF + p + 1))
                        nc.gpsimd.tensor_tensor(col(Gl, 2 * i + p), tb[:, p, :], col(Gh, 2 * i + p).bitcast(F32), ALU.subtract
                                                ).then_inc(gl_done, 1)

            with pool.Fori(0, DEPTH) as L:
                lo(L, 0, 0)
                lo(L, 1, 1)
                ffn(L, 0, 0)
                blocks(L, 24, 12)
                pool.wait_ge(t_act.sem, t_act.at("w", L))
                nc.gpsimd.tensor_tensor(wbal[:, :, :], wba[:, :, :], wbah[:, :, :].bitcast(F32), ALU.subtract
                                        ).then_inc(t_pool.sem, 1)
                blocks(L, 48, 13)
                ffn(L, 72, 1)
                blocks(L, 96, 11)

        @block.vector
        def _(dve):
            V = nc.vector

            def TT(out, a_, b_, op):
                return V.tensor_tensor(out, a_, b_, op)

            def done(L, n):
                dve.wait_ge(block_done, L * NB + n + (FREE + 1))

            def norm_rec(L, nj):
                dve.wait_ge(rt_ready, L * NORMS + (nj + 1))
                V.reciprocal(R[:, :], R[:, :])
                V.memset(acc[:, :], 0.0)
                dve.drain()

            def ffn(L, nb, ub, nj, hid):
                with dve.Fori(0, KF // 2) as i:
                    for p in range(2):
                        m = 2 * i + p
                        done(L, nb + m)
                        dve.wait_ge(gl_done, L * 2 * KF + m + (hid * KF + 1))
                        TT(halves(ta[:, p, :]), pair(4 * p), halves(R[:, :]), ALU.mult).then_inc(ta_ready, 1)
                        TT(halves(tb[:, p, :]), pair(4 * p + 2), halves(R[:, :]), ALU.mult).then_inc(evac, 1)
                        dve.drain()
                        dve.wait_ge(silu_done, L * 2 * KF + m + (hid * KF + 1))
                        TT(tb[:, p, :], tb[:, p, :], ta[:, p, :], ALU.mult).then_inc(g_ready, 1)
                with dve.Fori(0, KD // 2) as i:
                    for p in range(2):
                        m = 2 * i + p
                        done(L, nb + KF + 1 + 4 * i + 2 * p)
                        V.scalar_tensor_tensor(out=halves(Xc(m)), in0=pair(4 * p), scalar=0.5, in1=halves(Xc(m)),
                                               op0=ALU.mult, op1=ALU.add).then_inc(evac, 1)
                        split_chunk_dve(dve, L, nj + 1, m, p)
                norm_rec(L, nj + 1)

            def to_u(L, n, c, p):
                done(L, n)
                for q in range(2):
                    last = TT(halves(col(U, c + q)), pair(4 * p + 2 * q), halves(R[:, :]), ALU.mult)
                last.then_inc(evac, 1)

            dve.wait_ge(loads, 16 * 22)
            V.memset(acc[:, :], 0.0)
            TT(lpr[0:1, :], lrow[0:1, 0:4 * HD], lrow[0:1, 4 * HD:8 * HD], ALU.mult)
            dve.drain()
            V.reduce_sum(row[0:1, 18:22], lpr[0:1, :].rearrange("p (a c) -> p a c", c=HD), AXX).then_inc(start_dve, 1)
            dve.wait_ge(start_pe, 1)
            V.tensor_copy(gains[:, :], ps[:, 0, 0:76])
            V.tensor_copy(convw[:, :], ps[:, 1, 0:96])
            dve.wait_ge(start_act, 1)
            TT(row[0:1, 0:2], row[0:1, 18:20], row[0:1, 20:22], ALU.subtract)
            dve.drain()
            TT(row[0:1, 0:2], row[0:1, 0:2], CC[0:1, C_LI:C_LI + 2], ALU.add).then_inc(start_dve, 1)
            dve.wait_ge(start_pe, 2)
            V.tensor_copy(bcast[:, :], ps[:, 2, 0:18])
            for c in range(KD):
                dve.wait_ge(start_pe, 3 + c)
                V.tensor_copy(X[:, c, 0:SEQ], ps[:, 4 * (c % 2), :])
                V.tensor_copy(X[:, c, SEQ:T], ps[:, 4 * (c % 2) + 1, 0:NSEQ]).then_inc(start_dve, 1)
            for m in range(KD):
                split_chunk_dve(dve, 0, 0, m, m % 2)
            norm_rec(0, 0)

            with dve.Fori(0, DEPTH) as L:
                ffn(L, 0, 0, 0, 0)

                with dve.Fori(0, 3) as i:
                    for p in range(2):
                        c0 = 4 * i + 2 * p
                        to_u(L, 38 + 2 * i + p, c0, p)
                        dve.drain()

                        def tap(j, c):
                            return convw[:, bass.ds(L * (CONV * NCONV) + (j * NCONV) + c, 1)]

                        for j in (3, 2, 1, 0):
                            o = 3 - j
                            for q in range(2):
                                u = col(U, c0 + q)
                                if j == 3:
                                    V.tensor_copy(rawtail[:, bass.ds(c0 + q, 1), :].rearrange("p o t -> p (o t)"), u[:, SEQ - 3:T])
                                    dve.wait_ge(cv_done, L * NCONV + c0 + (q + 1))
                                    V.tensor_scalar(ta[:, q, 0:SEQ], u[:, 0:SEQ], tap(j, c0 + q), None, ALU.mult)
                                else:
                                    last = V.scalar_tensor_tensor(out=ta[:, q, o:SEQ], in0=u[:, 0:SEQ - o], scalar=tap(j, c0 + q),
                                                                  in1=ta[:, q, o:SEQ], op0=ALU.mult, op1=ALU.add)
                                    if j == 0:
                                        last.then_inc(cv_ready, 1)
                            if j:
                                dve.drain()
                for p in range(2):
                    to_u(L, 44 + p, U_Z + 2 * p, p)
                with dve.Fori(0, 3) as i:
                    for p in range(2):
                        to_u(L, 46 + 2 * i + p, U_Q + 4 * i + 2 * p, p)
                dve.wait_ge(t_pe.sem, t_pe.at("ba", L))
                TT(halves(BA[:, :]), ps[0:2 * H, 0:2, 0:HT], halves(R[0:2 * H, :]), ALU.mult).then_inc(t_dve.sem, 1)
                dve.wait_ge(cv_done, L * NCONV + (NCONV + 2))
                V.memset(bt[:, :, :], 0.0)
                dve.drain()
                dve.wait_ge(t_pe.sem, t_pe.at("tok", L))
                V.tensor_copy(bt[:, 0:4, :], ps[:, 2, 0:32].rearrange("p (t c) -> p t c", c=8))
                V.tensor_copy(bt[0:NSEQ, 4, :], ps[0:NSEQ, 2, 32:40]).then_inc(t_dve.sem, 1)
                dve.drain()

                def rowb(o):
                    return bcast[:, bass.ds(L * H + o, H)].unsqueeze(1).broadcast_to([P, 5, H])

                TT(ax[:, :, :], bt[:, :, H:2 * H], rowb(10), ALU.add).then_inc(t_dve.sem, 1)
                dve.drain()
                V.tensor_scalar(gg[:, :, :], ax[:, :, :], 0.0, None, ALU.max)
                dve.drain()
                dve.wait_ge(t_act.sem, t_act.at("softplus", L))
                TT(gg[:, :, :], gg[:, :, :], sp[:, :, :], ALU.add)
                dve.drain()
                V.scalar_tensor_tensor(out=gg[:, :, :], in0=gg[:, :, :], scalar=-1.0, in1=rowb(2), op0=ALU.mult, op1=ALU.mult
                                       ).then_inc(t_dve.sem, 1)
                dve.wait_ge(t_pe.sem, t_pe.at("gcum", L))
                V.tensor_copy(gcs[:, :, :], ps[:, 3, 0:16].rearrange("p (c h) -> p c h", h=H))
                dve.drain()
                TT(kdx[:, :, :], ps[:, 3, 16:32].rearrange("p (c h) -> p c h", h=H), gcs[:, :, :], ALU.subtract
                   ).then_inc(t_dve.sem, 1)
                dve.wait_ge(t_act.sem, t_act.at("asam", L))
                id8 = CC[0:NSEQ, C_ID:C_ID + NSEQ].unsqueeze(1).broadcast_to([NSEQ, H, NSEQ])
                for n, x in enumerate((sp, beta)):
                    last = TT(sexp[:, n, :, :], x[0:NSEQ, 4, :].unsqueeze(2).broadcast_to([NSEQ, H, NSEQ]), id8, ALU.mult)
                last.then_inc(t_dve.sem, 1)
                dve.wait_ge(t_pe.sem, t_pe.at("sab", L))
                V.tensor_copy(sab[:, :, :, :].rearrange("p a h s -> p (a h s)"), ps[:, 4, 0:64]).then_inc(t_dve.sem, 1)

                def taps(j):
                    return convw[:, bass.ds(L * (CONV * NCONV) + j * NCONV, NCONV)].unsqueeze(2).broadcast_to([P, NCONV, NSEQ])

                dve.wait_ge(t_pe.sem, t_pe.at("states", L))
                TT(csam[:, :, :], rawtail[:, :, 3:11], taps(3), ALU.mult)
                dve.drain()
                for j in range(3):
                    TT(ctmp[:, :, :], ps[:, 0, 0:24 * NCONV].rearrange("p (c s j) -> p c s j", c=NCONV, j=3)[:, :, :, j],
                       taps(j), ALU.mult)
                    dve.drain()
                    last = TT(csam[:, :, :], csam[:, :, :], ctmp[:, :, :], ALU.add)
                    if j < 2:
                        dve.drain()
                last.then_inc(t_dve.sem, 1)
                V.tensor_tensor(gda[:, :], gains[:, bass.ds(L + 74, 1)], CC[:, bass.ds(L + C_OML, 1)], ALU.mult)
                V.tensor_scalar(nlam[:, :], bcast[:, bass.ds(L, 1)], -1.0, None, ALU.mult)
                with dve.Fori(0, H) as i:
                    for p in range(2):
                        dve.wait_ge(l_act.sem, l_act.at(f"rt{p}", L, i))
                        V.reciprocal(ta[:, p, :], ta[:, p, :])
                        dve.drain()
                        V.scalar_tensor_tensor(out=col(U, i + 4 * p), in0=col(U, i + 4 * p), scalar=1.0 if p else P ** -0.5,
                                               in1=ta[:, p, :], op0=ALU.mult, op1=ALU.mult).then_inc(l_dve.sem, 1)
                dve.drain()
                dve.wait_ge(tail_out, L * 48 + 48)
                V.memset(S[:, :, :], 0.0)
                dve.drain()
                with dve.Fori(0, 4) as c:
                    def pe_(step):
                        dve.wait_ge(d_pe.sem, d_pe.at(step, L, c))

                    def cc(x):
                        return x[:, bass.ds(c, 1), :].rearrange("p o h -> p (o h)").unsqueeze(2).broadcast_to([P, H, P])

                    def con(o):
                        return heads(CM[:, o:o + P])

                    for t_, o in ((Qs, 0), (Ks, 4), (Vs, 8)):
                        V.tensor_copy(t_[:, :, :], U[:, o:o + 4, bass.ds(c * P, P)])
                    TT(Ds[:, :, :], heads(ident), cc(gcs), ALU.mult).then_inc(d_dve.sem, 1)
                    pe_("gram")
                    TT(W1[:, :, :], bank4(0), cc(gcs), ALU.subtract)
                    dve.drain()
                    V.tensor_scalar(W1[:, :, :], W1[:, :, :], 0.0, None, ALU.max).then_inc(d_dve.sem, 1)
                    dve.wait_ge(d_act.sem, d_act.at("exp", L, c))
                    TT(attn[:, :, :], Ds[:, :, :], con(M_INCL), ALU.mult)
                    TT(At[:, :, :], Ds[:, :, :], con(M_STRICT), ALU.mult)
                    dve.drain()
                    TT(attn[:, :, :], attn[:, :, :], bank4(2), ALU.mult)
                    TT(At[:, :, :], At[:, :, :], bank4(1), ALU.mult)
                    dve.drain()
                    TT(At[:, :, :], At[:, :, :], cc(beta), ALU.mult).then_inc(d_dve.sem, 1)
                    dve.drain()
                    dve.wait_ge(d_act.sem, d_act.at("tok", L, c))
                    TT(Qs[:, :, :], Qs[:, :, :], ATs[:, :, :], ALU.mult)
                    TT(Ti[:, :, :], At[:, :, :], con(M_LOW0), ALU.mult)
                    dve.drain()
                    TT(Ti[:, :, :], heads(ident), Ti[:, :, :], ALU.subtract)
                    pe_("at")
                    V.tensor_copy(ATs[:, :, :], bank4(5))
                    V.tensor_copy(attn[:, :, :], bank4(6))
                    dve.drain()
                    TT(Ui[:, :, :], ATs[:, :, :], con(M_LVT), ALU.mult)
                    TT(ATl[:, :, :], ATs[:, :, :], con(M_LVT + P), ALU.mult)
                    dve.drain()
                    TT(Ui[:, :, :], heads(ident), Ui[:, :, :], ALU.subtract).then_inc(d_dve.sem, 1)
                    for l in levels:
                        pe_(f"w{l}")
                        V.tensor_copy(W1[:, :, :], bank4(7)).then_inc(d_dve.sem, 1)
                        if l < LV - 1:
                            TT(ATl[:, :, :], ATs[:, :, :], con(M_LVT + P * (l + 1)), ALU.mult)
                        pe_(f"p{l}")
                        if l < LV - 1:
                            TT(Ti[:, :, :], Ti[:, :, :], bank4(1), ALU.subtract)
                        TT(Ui[:, :, :], Ui[:, :, :], bank4(5), ALU.subtract).then_inc(d_dve.sem, 1)
                    pe_("ks")
                    TT(W1[:, :, :], bank4(0), cc(eg), ALU.mult)
                    dve.drain()
                    TT(W1[:, :, :], Vt[:, :, :], W1[:, :, :], ALU.subtract)
                    dve.drain()
                    TT(W1[:, :, :], W1[:, :, :], cc(beta), ALU.mult).then_inc(d_dve.sem, 1)
                    TT(Kt[:, :, :], Kt[:, :, :], cc(ekd), ALU.mult)
                    pe_("vnew")
                    V.tensor_copy(ATl[:, :, :], bank4(2)).then_inc(d_dve.sem, 1)
                    pe_("out")
                    stand(dve, "dve")
                    V.tensor_copy(U[:, 8:12, bass.ds(c * P, P)], bank4(3)).then_inc(d_dve.sem, 1)
                    TT(S[:, :, :], S[:, :, :], cc(dl), ALU.mult)
                    dve.drain()
                    pe_("state")
                    TT(S[:, :, :], S[:, :, :], bank4(7), ALU.add).then_inc(d_dve.sem, 1)
                dve.wait_ge(s_out, L * 16 + 16)
                stand(dve, "dve")
                with dve.Fori(0, H) as h:
                    for t_, o in ((qs, U_Q), (ks, U_K), (vs, U_V)):
                        last = V.tensor_copy(t_[:, :], col(U, h + o))
                    last.then_inc(a_dve.sem, 1)
                    slope = CC[:, bass.ds(h + C_SLOPE, 1)]
                    for q in range(4):
                        n = (q + 1) * P
                        dve.wait_ge(a_pe.sem, a_pe.at(f"score{q}", L, h))
                        for m in range(2):
                            V.scalar_tensor_tensor(out=sc[:, m, 0:n], in0=CM[:, M_DIST + SEQ - n:M_DIST + SEQ], scalar=slope,
                                                   in1=ps[:, 4 + 2 * (q % 2) + m, 0:n], op0=ALU.mult, op1=ALU.add)
                        dve.drain()
                        V.reduce_max(mx[:, :], sc[:, :, 0:n], AXX)
                        dve.drain()
                        V.tensor_scalar(nm[:, :], mx[:, :], -SCALE, None, ALU.mult).then_inc(a_dve.sem, 1)
                        dve.wait_ge(a_act.sem, a_act.at(f"exp{q}", L, h))
                        V.reciprocal(rc[:, :], sm[:, :])
                        dve.drain()
                        TT(rc[:, 1:2], rc[:, 1:2], nlam[:, :], ALU.mult)
                        V.tensor_scalar(pr[:, 0, 0:n], pr[:, 0, 0:n], rc[:, 0:1], None, ALU.mult)
                        dve.drain()
                        V.scalar_tensor_tensor(out=pr[:, 0, 0:n], in0=pr[:, 1, 0:n], scalar=rc[:, 1:2], in1=pr[:, 0, 0:n],
                                               op0=ALU.mult, op1=ALU.add).then_inc(a_dve.sem, 1)
                    dve.wait_ge(a_pe.sem, a_pe.at("out", L, h))
                    stand(dve, "dve")
                    V.tensor_copy(U[:, bass.ds(h + U_Q, 1), 0:SEQ].rearrange("p o t -> p (o t)"), ps[:, 0, :]).then_inc(a_dve.sem, 1)
                dve.drain()
                dve.wait_ge(tok_out, L * (H * 32) + (H * 32 + 32))
                dve.wait_ge(stok_out, L * 32 + 32)
                V.tensor_copy(dq[:, 0, :, :], U[:, 0:4, SEQ:T])
                V.tensor_copy(dq[:, 1, :, :], U[:, 4:8, SEQ:T])
                V.tensor_copy(dv[:, :, :], U[:, 8:12, SEQ:T])
                TT(aq[:, :, :], U[:, U_Q:U_Q + 4, SEQ:T], U[:, U_K:U_K + 4, SEQ:T], ALU.mult)
                dve.drain()
                TT(bk[:, :, :], dq[:, 1, :, :], sab[:, 1, :, :], ALU.mult)
                TT(qk[:, :, :], dq[:, 0, :, :], dq[:, 1, :, :], ALU.mult).then_inc(q_dve.sem, 1)
                dve.wait_ge(q_pe.sem, q_pe.at("own", L))
                TT(qk[:, :, :], ps[:, 0, 0:32].rearrange("p (h s) -> p h s", h=H), sab[:, 1, :, :], ALU.mult)
                V.tensor_copy(own[:, :, :, :].rearrange("p m h s -> p (m h s)"), ps[:, 0, 32:96]).then_inc(q_dve.sem, 1)
                with dve.Fori(0, NSEQ) as s:
                    def at_s(x):
                        return x[:, :, bass.ds(s, 1)].rearrange("p h o -> p (h o)")

                    TT(diag[:, :, :], heads(ident), eq(U[:, U_Q:U_Q + 4, bass.ds(s + SEQ, 1)].rearrange("p h o -> p (h o)")),
                       ALU.mult).then_inc(k_dve.sem, 1)
                    dve.wait_ge(k_pe.sem, k_pe.at("q", L, s))
                    for half in range(2):
                        kv = kvp[half]
                        dve.wait_ge(k_load[half], L * (NSEQ * 64) + s * 64 + 64)
                        TT(kv[:, :, :], kv[:, :, :], ps[:, 1, :].unsqueeze(1).broadcast_to([P, 4, SEQ]), ALU.mult)
                        dve.drain()
                        V.reduce_sum(Sall[:, bass.ds(s, 1), 4 * half:4 * half + 4, :].rearrange("p o g m -> p (o g m)"),
                                     kv[:, :, :].rearrange("p g (m d) -> p (g m) d", d=HD), AXX).then_inc(kfree, 1)
                    dve.wait_ge(k_pe.sem, k_pe.at("sm", L, s))
                    skq = ps[:, 2, 0:2 * H].rearrange("p (h a) -> p h a", a=2)
                    TT(ucol[:, :], skq[:, :, 1], at_s(sab[:, 0]), ALU.mult)
                    TT(ocol[:, :], skq[:, :, 0], at_s(sab[:, 0]), ALU.mult)
                    dve.drain()
                    TT(ucol[:, :], at_s(dv), ucol[:, :], ALU.subtract)
                    dve.drain()
                    TT(diag[:, :, :], heads(ident), eq(ucol[:, :]), ALU.mult).then_inc(k_dve.sem, 1)
                    dve.drain()
                    TT(ucol[:, :], ucol[:, :], at_s(qk), ALU.mult)
                    dve.wait_ge(st_out, L * (NSEQ * 16) + s * 16 + 16)
                    TT(stn[:, :, :], st[:, :, :], eq(at_s(sab[:, 0])), ALU.mult)
                    dve.drain()
                    dve.wait_ge(k_pe.sem, k_pe.at("ub", L, s))
                    TT(U[:, 8:12, bass.ds(s + SEQ, 1)].rearrange("p h o -> p (h o)"), ocol[:, :], ucol[:, :], ALU.add)
                    TT(diag[:, :, :], bank4(3), eq(at_s(bk)), ALU.mult)
                    dve.drain()
                    TT(stn[:, :, :], stn[:, :, :], diag[:, :, :], ALU.add).then_inc(k_dve.sem, 1)
                    dve.drain()
                bias = CM[:, M_PAST:M_PAST + NPAGE * H].unsqueeze(1).unsqueeze(3)
                for s in range(NSEQ):
                    TT(Sall[:, s, :, :].rearrange("p g (h m) -> p (g h) m", m=2),
                       Sall[:, s, :, :].rearrange("p g (h m) -> p (g h) m", m=2),
                       CM[:, M_PAST:M_PAST + NPAGE * H].unsqueeze(2).broadcast_to([P, NPAGE * H, 2]), ALU.add)
                dve.drain()
                V.reduce_max(ms[:, :, :], Sall[:, :, :, :].rearrange("p s g m -> p s m g"), AXX).then_inc(q_dve.sem, 1)
                dve.wait_ge(q_pe.sem, q_pe.at("mt", L))
                V.reduce_max(cm64[:, :], ps[0:64, 4, 0:P], AXX)
                dve.drain()
                V.tensor_scalar(dg64[:, :], CC[0:64, C_ID:C_ID + 64], cm64[:, 0:1], None, ALU.mult).then_inc(q_dve.sem, 1)
                dve.wait_ge(q_pe.sem, q_pe.at("mb", L))

                def hm(x):
                    return x[:, :, :].rearrange("p s (h m) -> p s h m", m=2)

                ow = own[:, :, :, :].rearrange("p m h s -> p s h m")
                TT(hm(ms), ps[:, 5, 0:64].rearrange("p (s h m) -> p s h m", s=NSEQ, m=2), ow, ALU.max)
                dve.drain()

                def pages_(x):
                    return x[:, :, :].unsqueeze(2).broadcast_to([P, NSEQ, NPAGE, 2 * H])

                TT(Sall[:, :, :, :], Sall[:, :, :, :], pages_(ms), ALU.subtract)
                TT(hm(eo), ow, hm(ms), ALU.subtract).then_inc(q_dve.sem, 1)
                dve.wait_ge(q_pe.sem, q_pe.at("sum", L))
                V.reduce_sum(ls[:, :, :], ps[:, 6, :].rearrange("p (s g m) -> p s m g", s=NSEQ, g=NPAGE), AXX)
                dve.drain()
                TT(ls[:, :, :], ls[:, :, :], eo[:, :, :], ALU.add)
                dve.drain()
                V.reciprocal(ls[:, :, :], ls[:, :, :])
                dve.drain()
                V.tensor_scalar(hm(ls)[:, :, :, 1], hm(ls)[:, :, :, 1], nlam[:, 0:1], None, ALU.mult)
                dve.drain()
                TT(Sall[:, :, :, :], Sall[:, :, :, :], pages_(ls), ALU.mult)
                TT(eo[:, :, :], eo[:, :, :], ls[:, :, :], ALU.mult)
                dve.drain()
                sv = Sall[:, :, :, :].rearrange("p s g (h m) -> p (s g) h m", m=2)
                TT(Pc[:, :, :, :].rearrange("p s g h -> p (s g) h"), sv[:, :, :, 0], sv[:, :, :, 1], ALU.add)
                TT(po[:, :, :], hm(eo)[:, :, :, 0], hm(eo)[:, :, :, 1], ALU.add).then_inc(q_dve.sem, 1)
                dve.drain()
                with dve.Fori(0, NSEQ) as s:
                    for half in range(2):
                        kv = kvp[half]
                        dve.wait_ge(v_load[half], L * (NSEQ * 64) + s * 64 + 64)
                        w = Pc[:, bass.ds(s, 1), 4 * half:4 * half + 4, :].rearrange("p o g h -> p (o g h)")
                        kh = kv[:, :, :].rearrange("p g (h d) -> p (g h) d", d=P)
                        TT(kh, kh, w.unsqueeze(2).broadcast_to([P, 4 * H, P]), ALU.mult)
                        dve.drain()
                        TT(kv[:, 0:2, :], kv[:, 0:2, :], kv[:, 2:4, :], ALU.add)
                        dve.drain()
                        if half == 0:
                            dve.wait_ge(v_pe.sem, v_pe.begin(L, s))
                            TT(vsum[:, :], kv[:, 0, :], kv[:, 1, :], ALU.add).then_inc(vfree, 1)
                        else:
                            TT(kv[:, 0, :], kv[:, 0, :], kv[:, 1, :], ALU.add)
                            dve.drain()
                            TT(kv[:, 1, :], kv[:, 0, :], vsum[:, :], ALU.add)
                            dve.drain()
                            V.tensor_copy(vsum[:, :], kv[:, 1, :]).then_inc(v_dve.sem, 1)
                dve.drain()
                dve.wait_ge(v_pe.sem, v_pe.at("o", L, NSEQ - 1))
                TT(aq[:, :, :], U[:, U_V:U_V + 4, SEQ:T], po[:, :, :].rearrange("p s h -> p h s"), ALU.mult)
                dve.drain()
                TT(U[:, U_Q:U_Q + 4, SEQ:T], aq[:, :, :], ps[:, 7, 0:32].rearrange("p (h s) -> p h s", h=H), ALU.add
                   ).then_inc(q_dve.sem, 1)
                with dve.Fori(0, H) as i:
                    for p, (c, g_) in enumerate(((8, gains[:, bass.ds(L + 72, 1)]), (U_Q, gda[:, 0:1]))):
                        dve.wait_ge(n_act.sem, n_act.at(f"rt{p}", L, i))
                        V.reciprocal(ta[:, p, :], ta[:, p, :])
                        dve.drain()
                        last = V.scalar_tensor_tensor(out=col(U, i + c), in0=col(U, i + c), scalar=g_, in1=ta[:, p, :],
                                                      op0=ALU.mult, op1=ALU.mult)
                        if p == 0:
                            dve.drain()
                            last = TT(col(U, i + c), col(U, i + c), col(U, i + U_Z), ALU.mult)
                        last.then_inc(n_dve.sem, 1)
                    for p, c in enumerate((8, U_Q)):
                        dve.wait_ge(n_act.sem, n_act.at(f"h{p}", L, i))
                        TT(col(Yl, i + 4 * p), col(U, i + c), col(Yh, i + 4 * p).bitcast(F32), ALU.subtract).then_inc(n_dve.sem, 1)
                with dve.Fori(0, 4) as i:
                    for j in range(4):
                        done(L, 52 + 4 * i + j)
                        if j >= 2:
                            dve.wait_ge(g_act.sem, g_act.at("sa" if j == 2 else "sb", L, i))
                        for q in range(2):
                            b = halves(R[:, :]) if j < 2 else halves(sg[:, j - 2, q, :])
                            o = (sg[:, j % 2, q, :], sg[:, j % 2, q, :], mt[:, q, :], gt2[:, q, :])[j]
                            last = TT(halves(o), pair(4 * (j % 2) + 2 * q), b, ALU.mult)
                        last.then_inc(evac, 1)
                    dve.drain()
                    TT(mt[:, :, :], mt[:, :, :], gt2[:, :, :], ALU.add).then_inc(g_dve.sem, 1)
                    dve.wait_ge(g_act.sem, g_act.at("h", L, i))
                    TT(Ml[:, bass.ds(2 * i, 2), :], mt[:, :, :], Mh[:, bass.ds(2 * i, 2), :].bitcast(F32), ALU.subtract
                       ).then_inc(g_dve.sem, 1)
                dve.wait_ge(p_pe.sem, p_pe.at("t", L))
                V.tensor_copy(PT[:, 0, 0:SEQ], ps[:, 0, :])
                V.tensor_copy(PT[:, 1, 0:SEQ], ps[:, 2, :])
                V.tensor_copy(PT[:, 0, SEQ:T], ps[:, 1, 0:NSEQ])
                V.tensor_copy(PT[:, 1, SEQ:T], ps[:, 3, 0:NSEQ]).then_inc(p_dve.sem, 1)
                with dve.Fori(0, 2) as i:
                    for p in range(2):
                        done(L, 68 + 2 * i + p)
                        for q in range(2):
                            m = 4 * i + 2 * p + q
                            last = TT(halves(Xc(m)), pair(4 * p + 2 * q), halves(Xc(m)), ALU.add)
                        last.then_inc(evac, 1)
                        for q in range(2):
                            split_chunk_dve(dve, L, 2, 4 * i + 2 * p + q, q)
                norm_rec(L, 2)
                ffn(L, 72, 64, 2, 1)
                dve.wait_ge(p_act.sem, p_act.at("hi", L))
                TT(PTl[:, :, :], PT[:, :, :], PTh[:, :, :].bitcast(F32), ALU.subtract).then_inc(p_dve.sem, 1)
                with dve.Fori(0, 4) as i:
                    done(L, 110 + 2 * i)
                    for q in range(2):
                        last = TT(halves(ta[:, q, :]), pair(2 * q), halves(R[:, :]), ALU.mult)
                    last.then_inc(evac, 1)
                    done(L, 111 + 2 * i)
                    dve.wait_ge(e_act.sem, e_act.at("s", L, i))
                    for q in range(2):
                        last = TT(halves(ta[:, q, :]), pair(4 + 2 * q), halves(ta[:, q, :]), ALU.mult)
                    last.then_inc(evac, 1)
                    dve.drain()
                    TT(X[:, bass.ds(2 * i, 2), :], X[:, bass.ds(2 * i, 2), :], ta[:, :, :], ALU.add).then_inc(e_dve.sem, 1)
                    dve.drain()
                with dve.Fori(0, 4) as i:
                    for p in range(2):
                        split_chunk_dve(dve, L, 4, 2 * i + p, p)
                norm_rec(L, 4)
            for m in range(KD):
                last = V.scalar_tensor_tensor(out=yT[:, m, :], in0=X[:, m, :], scalar=gains[:, 64 + m:65 + m], in1=R[:, :],
                                              op0=ALU.mult, op1=ALU.mult)
            last.then_inc(fin_dve, 1)
            dve.wait_ge(start_act, 2)
            dve.wait_ge(fin_pe, 1)
            V.memset(acc[:, :], 0.0).then_inc(fin_dve, 1)
            dve.wait_ge(fin_pe, 2)
            V.tensor_copy(ytok[0:NSEQ, 4, :].rearrange("p (b c) -> p b c", b=2), ps[0:NSEQ, 0:2, :]).then_inc(fin, 1)


_CONST = dict(const_core=core_constants, const_mix=mixer_constants)
_OUTS = [
    ("y_prompt", (1, SEQ, D)), ("y_sample", (NSEQ, 1, D)),
    ("k_prompt", (DEPTH, 1, SEQ, H, P)), ("v_prompt", (DEPTH, 1, SEQ, H, P)),
    ("delta_prompt", (DEPTH, 1, H, P, P)), ("conv_prompt", (DEPTH, 1, CONV - 1, NCONV * P)),
    ("k_sample", (DEPTH, NSEQ, 1, H, P)), ("v_sample", (DEPTH, NSEQ, 1, H, P)),
    ("delta_sample", (DEPTH, NSEQ, H, P, P)), ("conv_sample", (DEPTH, NSEQ, CONV - 1, NCONV * P)),
]


def kernel(**inputs):
    import concourse.bacc as bacc
    from concourse.bass_utils import run_bass_kernel_spmd

    nc = bacc.Bacc("TRN2", target_bir_lowering=False, num_devices=1)
    arrays, ins, outs = {}, {}, {}
    for name, a in [*inputs.items(), *((n, f()) for n, f in _CONST.items())]:
        a = np.ascontiguousarray(a)
        arrays[f"in_{name}"] = a
        ins[name] = nc.dram_tensor(f"in_{name}", a.shape, mybir.dt.from_np(a.dtype), kind="ExternalInput").ap()
    for name, shape in _OUTS:
        outs[name] = nc.dram_tensor(f"out_{name}", shape, F32, kind="ExternalOutput").ap()
    hybrid_trunk(nc, ins, outs)
    r = run_bass_kernel_spmd(nc, [arrays], core_ids=[0])
    return tuple(r.results[0][f"out_{name}"] for name, _ in _OUTS)
```

```python
import math
from contextlib import ExitStack

import numpy as np
import concourse.bass as bass
from concourse import mybir

ALU = mybir.AluOpType
ACT = mybir.ActivationFunctionType
AXX = mybir.AxisListType.X
F32 = mybir.dt.float32
R32 = mybir.dt.float32r
I32 = mybir.dt.int32

P = 128
D = 1024
KD = D // P
SEQ = 512
NSEQ = 8
T = SEQ + NSEQ
HT = T // 2
DEPTH = 2
H = 4
FF = 2816
KF = FF // P
PLE = 256
PAGE = 128
NPAGE = 8
PAST = PAGE * NPAGE
CONV = 4
NCONV = 12
HD = 64
EPS = 1e-6
IN_Z = 1536
IN_BA = 2048
IN_Q = 2056
IN_GA = 3592
IN_GB = 4616
U_CONV, U_Z, U_Q, U_K, U_V, NU = 0, 12, 16, 20, 24, 28
SCALE = HD ** -0.5
NEG = -1.0e30

C_ID, C_ONE, C_SLOPE, C_LI, C_OML, C_EPS, NCC = 0, 128, 256, 260, 262, 264, 266
LV = 7
M_INCL, M_STRICT, M_UP, M_LOW0, M_LVT, M_HALF, M_DIST = 0, 128, 256, 384, 512, 512 + 128 * LV, 768 + 128 * LV
M_PAST = M_DIST + 512
NCM = M_PAST + NPAGE * H


def core_constants():
    c = np.zeros((P, NCC), np.float32)
    c[:, C_ID:C_ID + P] = np.eye(P)
    c[:, C_ONE:C_ONE + P] = 1.0
    for h in range(H):
        c[:, C_SLOPE + h] = 2.0 ** (-8.0 * (h + 1) / H) / SCALE
    for l in range(DEPTH):
        li = 0.8 - 0.6 * math.exp(-0.3 * l)
        c[:, C_LI + l] = li
        c[:, C_OML + l] = 1.0 - li
    c[:, C_EPS] = EPS
    return c


def mixer_constants():
    c = np.zeros((P, NCM), np.float32)
    i, j = np.arange(P)[:, None], np.arange(P)[None, :]
    c[:, M_INCL:M_INCL + P] = i >= j
    c[:, M_STRICT:M_STRICT + P] = i > j
    c[:, M_UP:M_UP + P] = i <= j
    for l in range(LV):
        low = (i >> (l + 1) == j >> (l + 1)) & (i >> l & 1 == 1) & (j >> l & 1 == 0)
        if l == 0:
            c[:, M_LOW0:M_LOW0 + P] = low
        c[:, M_LVT + P * l:M_LVT + P * (l + 1)] = low.T
    c[:HD, M_HALF:M_HALF + P] = 1.0
    c[HD:, M_HALF + P:M_HALF + 2 * P] = 1.0
    x = np.arange(SEQ)[None, :] - (SEQ - P)
    c[:, M_DIST:M_DIST + SEQ] = np.where(x <= i, x - i, NEG)
    for g in range(NPAGE):
        for h in range(H):
            slope = 2.0 ** (-8.0 * (h + 1) / H) / SCALE
            c[:, M_PAST + g * H + h] = -slope * (PAST - g * PAGE - np.arange(P))
    return c


class Track:

    def __init__(self, sem, steps, iters, bias):
        self.sem, self.steps, self.iters, self.bias = sem, steps, iters, bias

    def at(self, step, layer, i=0):
        n = len(self.steps)
        return layer * (self.iters * n) + i * n + (self.bias + self.steps.index(step) + 1)

    def begin(self, layer, i=0):
        n = len(self.steps)
        return layer * (self.iters * n) + i * n + self.bias


def hybrid_trunk(nc, A, O):
    ctx = ExitStack()
    with ctx:
        base = [(nc.sbuf_base + 31) // 32 * 32]

        def at(name, shape, dt, offset):
            return nc.alloc_sbuf_tensor_at(name, shape, dt, offset=offset)

        def size(shape):
            return (int(np.prod(shape[1:])) * 4 + 31) // 32 * 32

        class Region:
            def __init__(self, start):
                self.at = start

            def sb(self, name, shape, dt=F32):
                t = at(name, shape, dt, self.at)
                self.at += size(shape)
                return t

        top = Region(base[0])
        sb = top.sb
        X = sb("X", [P, KD, T])
        Hh = sb("Hh", [P, KD, T], R32)
        Hl = sb("Hl", [P, KD, T], R32)
        ring_at = top.at
        raw = sb("raw", [P, 2, 2048])
        whi = sb("whi", [P, 2, 2048], R32)
        wlo = sb("wlo", [P, 2, 2048], R32)
        ring_end = top.at
        CC = sb("CC", [P, NCC])
        R = sb("R", [P, T])
        acc = sb("acc", [P, T])
        gains = sb("gains", [P, 76])
        convw = sb("convw", [P, 96])
        bcast = sb("bcast", [P, 18])
        gda = sb("gda", [P, 1])
        nlam = sb("nlam", [P, 1])
        pages = sb("pages", [1, NSEQ * NPAGE], I32)
        PT = sb("PT", [P, 2, T])
        PTl = at("PTl", [P, 2, T], R32, top.at - size([P, 2, T]))
        tmp_at = top.at
        ta = sb("ta", [P, 2, T])
        tb = sb("tb", [P, 2, T])
        PTh = at("PTh", [P, 2, T], R32, top.at - size([P, 2, T]))
        g_at = top.at
        Gh = sb("Gh", [P, KF, T], R32)
        Gl = sb("Gl", [P, KF, T], R32)
        assert top.at <= nc.sbuf_usable_end, (top.at, nc.sbuf_usable_end)
        end = nc.sbuf_usable_end

        mix = Region(g_at)
        U = mix.sb("U", [P, NU, T])
        cm_at = mix.at
        CM = mix.sb("CM", [P, NCM])
        beta = mix.sb("beta", [P, 5, H])
        gcs = mix.sb("gcs", [P, 4, H])
        eg = mix.sb("eg", [P, 4, H])
        ekd = mix.sb("ekd", [P, 4, H])
        dl = mix.sb("dl", [P, 4, H])
        sab = mix.sb("sab", [P, 2, H, NSEQ])
        rawtail = mix.sb("rawtail", [P, NCONV, 11])
        scr_at = mix.at
        s0 = Region(scr_at)
        wba = s0.sb("wba", [P, KD, P])
        wbah = s0.sb("wbah", [P, KD, P], R32)
        wbal = s0.sb("wbal", [P, KD, P], R32)
        BA = s0.sb("BA", [2 * H, T])
        assert s0.at <= end
        s1 = Region(scr_at)
        scin = s1.sb("scin", [24, NCONV * P])
        tailtok = s1.sb("tailtok", [11, NCONV * P])
        csam = s1.sb("csam", [P, NCONV, NSEQ])
        ctmp = s1.sb("ctmp", [P, NCONV, NSEQ])
        assert s1.at <= end
        s2 = Region(tmp_at)
        bt = s2.sb("bt", [P, 5, 2 * H])
        ax = s2.sb("ax", [P, 5, H])
        sp = s2.sb("sp", [P, 5, H])
        gg = s2.sb("gg", [P, 5, H])
        kdx = s2.sb("kdx", [P, 4, H])
        sexp = s2.sb("sexp", [NSEQ, 2, H, NSEQ])
        d = Region(scr_at)
        W4 = [P, H, P]
        Qs, Ks, Vs = d.sb("Qs", W4), d.sb("Ks", W4), d.sb("Vs", W4)
        Vt, Ds, At, ATl = d.sb("Vt", W4), d.sb("Ds", W4), d.sb("At", W4), d.sb("ATl", W4)
        ATs, attn, Ti = d.sb("ATs", W4), d.sb("attn", W4), d.sb("Ti", W4)
        assert d.at <= end
        d2 = Region(tmp_at)
        Ui, W1, S, Kt = d2.sb("Ui", W4), d2.sb("W1", W4), d2.sb("S", W4), d2.sb("Kt", W4)
        a = Region(ring_at)
        qs, ks, vs = a.sb("qs", [P, T]), a.sb("ks", [P, T]), a.sb("vs", [P, T])
        ktok, vtok = a.sb("ktok", W4), a.sb("vtok", W4)
        aT = a.sb("aT", [P, 4, SEQ])
        stok = a.sb("stok", [NSEQ, 2, P])
        mx, nm, sm, rc = (a.sb(n, [P, 2]) for n in ("mx", "nm", "sm", "rc"))
        sc = a.sb("sc", [P, 2, SEQ])
        kp = [a.sb(f"kp{n}", [P, 4, SEQ]) for n in range(2)]
        diag = a.sb("diag", W4)
        st = a.sb("st", W4)
        stn = a.sb("stn", W4)
        qb = a.sb("qb", [P, SEQ])
        assert a.at <= ring_end, (a.at, ring_end)
        f = Region(d.at)
        dq = f.sb("dq", [P, 2, H, NSEQ])
        dv = f.sb("dv", [P, H, NSEQ])
        qk = f.sb("qk", [P, H, NSEQ])
        bk = f.sb("bk", [P, H, NSEQ])
        aq = f.sb("aq", [P, H, NSEQ])
        Sall = f.sb("Sall", [P, NSEQ, NPAGE, 2 * H])
        own = f.sb("own", [P, 2, H, NSEQ])
        ms, eo, ls = (f.sb(n, [P, NSEQ, 2 * H]) for n in ("ms", "eo", "ls"))
        po = f.sb("po", [P, NSEQ, H])
        Pc = f.sb("Pc", [P, NSEQ, NPAGE, H])
        cm64 = f.sb("cm64", [64, 1])
        dg64 = f.sb("dg64", [64, 64])
        ucol, ocol = f.sb("ucol", [P, H]), f.sb("ocol", [P, H])
        assert f.at <= end, (f.at, end)
        vr = Region(scr_at)
        vu = Region(g_at)
        vp = [[r.sb(f"vp{j}{n}", [P, 4, SEQ]) for n in range(2)] for j, r in enumerate((vr, vu))]
        assert vr.at <= d.at and vu.at <= g_at + 8 * T * 4
        Yh = at("Yh", [P, KD, T], R32, g_at)
        Yl = at("Yl", [P, KD, T], R32, g_at + U_K * T * 4)
        Mh = at("Mh", [P, KD, T], R32, g_at + 8 * T * 4)
        gt = Region(cm_at)
        Ml = gt.sb("Ml", [P, KD, T], R32)
        sg = gt.sb("sg", [P, 2, 2, T])
        mt = gt.sb("mt", [P, 2, T])
        gt2 = gt.sb("gt2", [P, 2, T])
        ptok = at("ptok", [P, 5, PLE], F32, g_at + U_Q * T * 4)
        assert gt.at <= end, (gt.at, end)
        z = Region(g_at)
        xtok = z.sb("xtok", [P, 5, D])
        grow = z.sb("grow", [76, P])
        crow = z.sb("crow", [96, P])
        lrow = z.sb("lrow", [1, 8 * HD])
        lpr = z.sb("lpr", [1, 4 * HD])
        row = z.sb("row", [1, 24])
        pg = at("pg", [P, 2, T], F32, g_at)
        yr = Region(g_at)
        yT = yr.sb("yT", [P, KD, T])
        ytok = yr.sb("ytok", [P, 5, D])

        ps = ctx.enter_context(nc.psum_tensor("ps", [P, 8, 512], F32))
        ident = CC[:, C_ID:C_ID + P]
        ones = CC[:, C_ONE:C_ONE + P]
        eps = CC[:, C_EPS:C_EPS + 1]

        def sem(name):
            return ctx.enter_context(nc.semaphore(name))

        NB = 118
        NE = 102
        NH = 32
        FREE = 2
        raw_ready = [sem("raw_ready0"), sem("raw_ready1")]
        hi_done = sem("hi_done")
        split_done = sem("split_done")
        block_done = sem("block_done")
        evac = sem("evac")
        hh_ready = sem("hh_ready")
        h_ready = sem("h_ready")
        sq_ready = sem("sq_ready")
        acc_ready = sem("acc_ready")
        sum_ready = sem("sum_ready")
        rt_ready = sem("rt_ready")
        ta_ready, silu_done = sem("ta_ready"), sem("silu_done")
        g_ready, gh_done, gl_done = sem("g_ready"), sem("gh_done"), sem("gl_done")
        outs = sem("outs")
        passed = {n: sem(f"passed_{n}") for n in ("sp", "pe", "dve", "act", "pool")}
        NORMS = 4

        def stand(eng, name):
            eng.sem_inc(passed[name], 1)

        def pair(b):
            return ps[:, b:b + 2, 0:HT]

        def halves(t):
            return t.rearrange("p (a c) -> p a c", a=2)

        def track(name, steps, iters=1, bias=0):
            return Track(sem(name), steps.split(), iters, bias)

        levels = range(1, LV)
        loads = sem("loads")
        start_pe, start_dve, start_act = sem("start_pe"), sem("start_dve"), sem("start_act")
        cv_ready = sem("cv_ready")
        cv_done = sem("cv_done")
        cm_load, ba_load, sc_load = sem("cm_load"), sem("ba_load"), sem("sc_load")
        tail_out, s_out, tok_out, st_out = (sem(n) for n in ("tail_out", "s_out", "tok_out", "st_out"))
        st_load, p_load = sem("st_load"), sem("p_load")
        k_load = [sem(f"k_load{n}") for n in range(2)]
        v_load = [[sem(f"v_load{j}{n}") for n in range(2)] for j in range(2)]
        kfree = sem("kfree")
        fin, fin_pe, fin_dve = sem("fin"), sem("fin_pe"), sem("fin_dve")
        t_pe = track("t_pe", "ba tok gcum sab tails states")
        t_dve = track("t_dve", "ba bt ax g kdx sexp sab csam")
        t_act = track("t_act", "w beta softplus decays asam tailtok csam")
        t_pool = track("t_pool", "w")
        l_act = track("l_act", "sq0 sq1 rt0 rt1", 4)
        l_pe = track("l_pe", "sum0 sum1", 4)
        l_dve = track("l_dve", "n0 n1", 4, bias=1)
        d_pe = track("d_pe", "gram vt at " + " ".join(f"w{l} p{l}" for l in levels) + " ks vnew out state", 4)
        d_dve = track("d_dve", "diag dm attn at " + " ".join(f"w{l} u{l}" for l in levels) + " w vn o state", 4)
        d_act = track("d_act", "exp qd kt vt", 4)
        a_pe = track("a_pe", "tok " + " ".join(f"score{q} at{q}" for q in range(4)) + " out", 4)
        a_dve = track("a_dve", "staged " + " ".join(f"max{q} attn{q}" for q in range(4)) + " out", 4)
        a_act = track("a_act", "tok " + " ".join(f"exp{q} at{q}" for q in range(4)), 4)
        q_pe = track("q_pe", "own mt mb sum")
        q_dve = track("q_dve", "cols own max col sub done o")
        q_act = track("q_act", "exp")
        k_pe = track("k_pe", "sm ub q", NSEQ)
        k_dve = track("k_dve", "ucol st diag", NSEQ, bias=1)
        k_act = track("k_act", "qb", NSEQ, bias=1)
        k_pool = track("k_pool", "half0 half1", NSEQ, bias=1)
        v_pool = track("v_pool", "half0", NSEQ)
        v_dve = track("v_dve", "half1 sum", NSEQ, bias=3)
        v_pe = track("v_pe", "o", NSEQ, bias=2)
        n_act = track("n_act", "z sq0 sq1 rt0 rt1 h0 h1", 4)
        n_pe = track("n_pe", "sum0 sum1", 4)
        n_dve = track("n_dve", "y0 y1 l0 l1", 4)
        g_act = track("g_act", "sa sb h", 4)
        g_dve = track("g_dve", "m l", 4)
        p_pe = track("p_pe", "t")
        p_act = track("p_act", "hi")
        p_dve = track("p_dve", "t lo")
        e_act = track("e_act", "s", 4)
        e_dve = track("e_dve", "x", 4)

        block = ctx.enter_context(nc.Block())

        @block.sync
        def _(sp_):
            def slot(L, n, p):
                sp_.wait_ge(split_done, L * NB + (n + 1))

            def load(p, dst_k, cols, src):
                sp_.dma_start(raw[:, p, dst_k[0] * cols:dst_k[1] * cols].rearrange("p (k c) -> p k c", c=cols),
                              src).then_inc(raw_ready[p], 16)

            def block8(L, n, p, w, c0, k=KD, cols=256):
                slot(L, n, p)
                src = w[L].rearrange("(k p) c -> p k c", p=P)
                for a0, a1 in ((0, k // 2), (k // 2, k)):
                    load(p, (a0, a1), cols, src[:, a0:a1, bass.ds(c0, cols)])

            def up(L, n, p, w1, w3, layer, c0):
                slot(L, n, p)
                for s, w in enumerate((w1, w3)):
                    sp_.dma_start(raw[:, p, :].rearrange("p (k s c) -> p s k c", s=2, c=P)[:, s],
                                  w[layer].rearrange("(k p) c -> p k c", p=P)[:, :, c0]).then_inc(raw_ready[p], 16)

            def ffn(L, nb, w1, w3, w2, first=0):
                with sp_.Fori(first, KF // 2) as i:
                    for p in range(2):
                        up(L, nb + 2 * i + p, p, w1, w3, L, bass.ds(i * 256 + p * P, P))
                with sp_.Fori(0, KD // 2) as i:
                    for j in range(4):
                        m, hf = j // 2, j % 2
                        slot(L, nb + KF + 4 * i + j, j % 2)
                        src = w2[L, hf * 11 * P:(hf + 1) * 11 * P, :].rearrange("(k p) c -> p k c", p=P)
                        for a0, a1 in ((0, 6), (6, 11)):
                            load(j % 2, (a0, a1), P, src[:, a0:a1, bass.ds(i * 256 + m * P, P)])

            def proj(L, nb, n, c0, first=0):
                with sp_.Fori(first, n) as i:
                    for p in range(2):
                        block8(L, nb + 2 * i + p, p, A["w_in"], i * 512 + (c0 + 256 * p))

            sp_.dma_start(xtok[:, 0:4, :], A["x_prompt"][0].rearrange("(t p) f -> p t f", p=P)).then_inc(loads, 16)
            sp_.dma_start(xtok[0:NSEQ, 4, :], A["x_sample"][:, 0, :]).then_inc(loads, 16)
            sp_.dma_start(CC[:, :], A["const_core"]).then_inc(loads, 16)
            for l in range(DEPTH):
                for n, name in enumerate(("norm_ffn1", "norm_mix", "norm_ffn2", "norm_ple")):
                    r0 = (NORMS * l + n) * KD
                    sp_.dma_start(grow[r0:r0 + KD, :], A[name][l].rearrange("(c p) -> c p", p=P)).then_inc(loads, 16)
            sp_.dma_start(grow[64:72, :], A["norm_final"].rearrange("(c p) -> c p", p=P)).then_inc(loads, 16)
            sp_.dma_start(grow[72:74, :], A["dn_norm"]).then_inc(loads, 16)
            sp_.dma_start(grow[74:76, :], A["da_norm"]).then_inc(loads, 16)
            sp_.dma_start(crow[:, :], A["dn_conv_w"].rearrange("l j (c p) -> (l j c) p", p=P)).then_inc(loads, 16)
            for n, name in enumerate(("da_lambda_q1", "da_lambda_q2", "da_lambda_k1", "da_lambda_k2")):
                sp_.dma_start(lrow[0:1, n * 2 * HD:(n + 1) * 2 * HD],
                              A[name].rearrange("(o l) c -> o (l c)", o=1)).then_inc(loads, 16)
            sp_.dma_start(row[0:1, 2:10], A["dn_a_log"].rearrange("(o l) h -> o (l h)", o=1)).then_inc(loads, 16)
            sp_.dma_start(row[0:1, 10:18], A["dn_dt_bias"].rearrange("(o l) h -> o (l h)", o=1)).then_inc(loads, 16)
            sp_.dma_start(pages[:, :], A["page_table"].rearrange("(o s) g -> o (s g)", o=1)).then_inc(loads, 16)
            for p in range(2):
                up(0, p, p, A["ffn1_w1"], A["ffn1_w3"], 0, slice(p * P, (p + 1) * P))
            with sp_.Fori(0, DEPTH) as L:
                ffn(L, 0, A["ffn1_w1"], A["ffn1_w3"], A["ffn1_w2"], first=1)
                block8(L, 38, 0, A["w_in"], 0)
                block8(L, 39, 1, A["w_in"], 256)
                sp_.wait_ge(evac, L * NE + (FREE + 30))
                sp_.dma_start(CM[:, :], A["const_mix"]).then_inc(cm_load, 16)
                sp_.dma_start(wba[:, :, :], A["w_in"][L].rearrange("(k p) c -> p k c", p=P)[:, :, IN_BA:IN_BA + P]
                              ).then_inc(ba_load, 16)
                proj(L, 38, 3, 0, first=1)
                proj(L, 44, 1, IN_Z)
                proj(L, 46, 3, IN_Q)
                sp_.wait_ge(t_dve.sem, t_dve.at("bt", L))
                sp_.dma_start(scin[:, :], A["state_conv"][L].rearrange("s j c -> (s j) c")).then_inc(sc_load, 16)
                sp_.wait_ge(t_act.sem, t_act.at("tailtok", L))
                sp_.dma_start(O["conv_prompt"][L, 0], tailtok[0:3, :]).then_inc(tail_out, 16)
                sp_.dma_start(O["conv_sample"][L, :, 2, :], tailtok[3:11, :]).then_inc(tail_out, 16)
                sp_.dma_start(O["conv_sample"][L, :, 0:2, :], A["state_conv"][L, :, 1:3, :]).then_inc(tail_out, 16)
                sp_.wait_ge(q_dve.sem, q_dve.at("cols", L))
                stand(sp_, "sp")
                with sp_.Fori(0, H) as c:
                    for j in range(2):
                        s = 2 * c + j
                        sp_.wait_ge(k_dve.sem, k_dve.begin(L, s))
                        sp_.dma_start(st[:, :, :], A["state_delta"][L, bass.ds(s, 1)].rearrange("o h k v -> k (o h) v")
                                      ).then_inc(st_load, 16)
                        for half in range(2):
                            sp_.wait_ge(kfree, L * 16 + s * 2 + (half + 1))
                            stand(sp_, "sp")
                            for g in range(4):
                                pg = sp_.value_load(pages[0:1, bass.ds(s * NPAGE + (half * 4 + g), 1)],
                                                    min_val=0, max_val=A["cache_k"].shape[1] - 1)
                                sp_.dma_start(kp[half][:, g, :],
                                              A["cache_k"][L, bass.ds(pg, 1)].rearrange("o k h c -> k (o h c)")
                                              ).then_inc(k_load[half], 16)
                        if j == 0:
                            sp_.wait_ge(a_act.sem, a_act.at("tok", L, c))
                            for n, (o, t) in enumerate((("k", ktok), ("v", vtok))):
                                sp_.dma_start(O[o + "_prompt"][L, 0, :, bass.ds(c, 1), :].rearrange("(t p) o c -> p t (o c)", p=P),
                                              t[:, :, :]).then_inc(tok_out, 16)
                                sp_.dma_start(O[o + "_sample"][L, :, 0, bass.ds(c, 1), :].rearrange("s o c -> s (o c)"),
                                              stok[:, n, :]).then_inc(tok_out, 16)
                        sp_.wait_ge(k_dve.sem, k_dve.at("st", L, s))
                        sp_.dma_start(O["delta_sample"][L, bass.ds(s, 1)].rearrange("o h k v -> k (o h) v"), stn[:, :, :]
                                      ).then_inc(st_out, 16)
                sp_.wait_ge(d_dve.sem, d_dve.at("state", L, 3))
                sp_.dma_start(O["delta_prompt"][L, 0].rearrange("h k v -> k h v"), S[:, :, :]).then_inc(s_out, 16)

                def values(i):
                    for j in range(2):
                        s = 2 * i + j
                        for half in range(2):
                            if half:
                                sp_.wait_ge(v_dve.sem, v_dve.begin(L, s - 1))
                            else:
                                sp_.wait_ge(v_pe.sem, v_pe.begin(L, s - 1))
                            stand(sp_, "sp")
                            for g in range(4):
                                pg = sp_.value_load(pages[0:1, bass.ds(s * NPAGE + (half * 4 + g), 1)],
                                                    min_val=0, max_val=A["cache_v"].shape[1] - 1)
                                sp_.dma_start(vp[j][half][:, g, :],
                                              A["cache_v"][L, bass.ds(pg, 1)].rearrange("o k h c -> k (o h c)")
                                              ).then_inc(v_load[j][half], 16)

                with sp_.Fori(0, 1) as i:
                    values(i)
                sp_.wait_ge(kfree, L * 16 + (16 + 2))
                sp_.wait_ge(a_dve.sem, a_dve.at("out", L, 3))
                sp_.wait_ge(st_out, L * (NSEQ * 16) + (NSEQ * 16 + 16))
                sp_.wait_ge(tok_out, L * (H * 64) + (H * 64 + 64))
                stand(sp_, "sp")
                block8(L, 52, 0, A["w_in"], IN_GA)
                block8(L, 53, 1, A["w_in"], IN_GB)
                with sp_.Fori(1, NSEQ // 2) as i:
                    values(i)
                sp_.wait_ge(n_dve.sem, n_dve.at("l1", L, 3))
                sp_.dma_start(ptok[:, 0:4, :], A["p_prompt"][L, 0].rearrange("(t p) f -> p t f", p=P)).then_inc(p_load, 16)
                sp_.dma_start(ptok[0:NSEQ, 4, :], A["p_sample"][L, :, 0, :]).then_inc(p_load, 16)

                def pair2(i, n, first=False):
                    if not first:
                        block8(L, n, 0, A["w_in"], i * 256 + IN_GA)
                        block8(L, n + 1, 1, A["w_in"], i * 256 + IN_GB)
                    block8(L, n + 2, 0, A["w_a"], i * 256, k=4)
                    block8(L, n + 3, 1, A["w_b"], i * 256, k=4)

                pair2(0, 52, first=True)
                with sp_.Fori(1, 4) as i:
                    pair2(i, 4 * i + 52)
                with sp_.Fori(0, 2) as i:
                    for p in range(2):
                        block8(L, 68 + 2 * i + p, p, A["w_o"], i * 512 + 256 * p)
                ffn(L, 72, A["ffn2_w1"], A["ffn2_w3"], A["ffn2_w2"])
                with sp_.Fori(0, 4) as i:
                    block8(L, 110 + 2 * i, 0, A["w_ple_gate"], i * 256)
                    block8(L, 111 + 2 * i, 1, A["w_ple"], i * 256, k=2)
                for p in range(2):
                    slot(L, NB + p, p)
                    stand(sp_, "sp")
                    for n, w in enumerate((A["ffn1_w1"], A["ffn1_w3"])):
                        sp_.dma_start(raw[:, p, :].rearrange("p (k s c) -> p s k c", s=2, c=P)[:, n],
                                      w[bass.ds(1 - L, 1)].rearrange("o (k p) c -> p (o k) c", p=P)[:, :, p * P:(p + 1) * P]
                                      ).then_inc(raw_ready[p], 16)
            sp_.wait_ge(fin, 1)
            sp_.dma_start(O["y_prompt"][0].rearrange("(t p) f -> p t f", p=P), ytok[:, 0:4, :]).then_inc(outs, 16)
            sp_.dma_start(O["y_sample"][:, 0, :], ytok[0:NSEQ, 4, :]).then_inc(outs, 16)
            sp_.wait_ge(outs, 32)
            sp_.wait_ge(tail_out, DEPTH * 48)
            sp_.wait_ge(s_out, DEPTH * 16)
            sp_.wait_ge(tok_out, (DEPTH * H + 1) * 64)
            sp_.wait_ge(st_out, (DEPTH * NSEQ + 1) * 16)

        def eq(x):
            return x.unsqueeze(2).broadcast_to([x.shape[0], x.shape[1], P])

        def heads(x):
            return x.unsqueeze(1).broadcast_to([P, H, P])

        def bank4(b):
            return ps[:, b, :].rearrange("p (h c) -> p h c", h=H)

        @block.tensor
        def _(pe):
            def product(slot, cols, ks, ms, rh, rl, bank, starts=True, stops=True, before=None, after=None, k0=0):
                for k in range(ks):
                    if before:
                        before(k)
                    for m in range(ms):
                        o = k * cols + m * P
                        h, l = whi[:, slot, o:o + P], wlo[:, slot, o:o + P]
                        for n, (w, x) in enumerate(((h, rh), (h, rl), (l, rh))):
                            for c in range(2):
                                last = nc.tensor.matmul(ps[:, bank + 2 * m + c, 0:HT], w,
                                                        x[:, k0 + k, c * HT:(c + 1) * HT],
                                                        start=starts and k == 0 and n == 0,
                                                        stop=stops and k == ks - 1 and n == 2)
                last.then_inc(block_done, 1)

            def split_ready(L, n):
                pe.wait_ge(split_done, L * NB + n + (FREE + 1))

            def banks_ready(L, u):
                pe.wait_ge(evac, L * NE + u + 1)

            def h_wait(L, nj):
                return lambda k: pe.wait_ge(h_ready, L * NH + (FREE + KD * nj + k + 1))

            def block8(L, n, u, p, nj, k=KD, rh=Hh, rl=Hl, first=False, k0=0):
                split_ready(L, n)
                banks_ready(L, u)
                if p == 1 and nj is not None:
                    pe.wait_ge(rt_ready, L * NORMS + (nj + 1))
                product(p, 256, k, 2, rh, rl, 4 * p, before=h_wait(L, nj) if first else None, k0=k0)

            def norm_sum(L, nj):
                pe.wait_ge(acc_ready, L * NH + KD * (nj + 1))
                for c in range(2):
                    last = nc.tensor.matmul(ps[:, 6 + c, 0:HT], ones, acc[:, c * HT:(c + 1) * HT], start=True, stop=True)
                last.then_inc(sum_ready, 1)

            def first_pair(L, n, u, nj, **second):
                block8(L, n, u, 0, nj, first=True)
                norm_sum(L, nj)
                block8(L, n + 1, u + 1, 1, nj, **second)

            def ffn(L, nb, ub, nj, hid):
                first_pair(L, nb, ub, nj)
                with pe.Fori(1, KF // 2) as i:
                    for p in range(2):
                        block8(L, nb + 2 * i + p, ub + 2 * i + p, p, nj)
                with pe.Fori(0, KD // 2) as i:
                    for j in range(4):
                        m, hf = j // 2, j % 2
                        split_ready(L, nb + KF + 4 * i + j)
                        if hf == 0:
                            banks_ready(L, ub + KF + 2 * i + m)
                        pe.wait_ge(gl_done, L * 2 * KF + (hid * KF + 11 * (hf + 1) + FREE))
                        product(hf, P, 11, 1, Gh, Gl, 4 * m, starts=hf == 0, stops=hf == 1, k0=11 * hf)

            def tr(out, in_, rows=P):
                return nc.tensor.transpose(out, in_, CC[0:rows, C_ID:C_ID + rows])

            def to_features(bank, tok, c):
                for t in range(4):
                    tr(ps[:, bank, t * P:(t + 1) * P], tok[:, t, c * P:(c + 1) * P])
                return tr(ps[:, bank + 1, 0:NSEQ], tok[0:NSEQ, 4, c * P:(c + 1) * P], NSEQ)

            pe.wait_ge(loads, 16 * 22)
            tr(ps[:, 0, 0:76], grow[:, :], 76)
            tr(ps[:, 1, 0:96], crow[:, :], 96).then_inc(start_pe, 1)
            pe.wait_ge(start_dve, 2)
            nc.tensor.matmul(ps[:, 2, 0:18], CC[0:1, C_ONE:C_ONE + P], row[0:1, 0:18], start=True, stop=True).then_inc(start_pe, 1)
            for c in range(KD):
                pe.wait_ge(start_dve, max(2, 1 + c))
                to_features(4 * (c % 2), xtok, c).then_inc(start_pe, 1)

            pe.wait_ge(start_dve, 2 + KD)
            with pe.Fori(0, DEPTH) as L:
                ffn(L, 0, 0, 0, 0)
                first_pair(L, 38, 30, 1)
                with pe.Fori(1, 3) as i:
                    for p in range(2):
                        block8(L, 38 + 2 * i + p, 30 + 2 * i + p, p, 1)
                for p in range(2):
                    block8(L, 44 + p, 36 + p, p, 1)
                with pe.Fori(0, 3) as i:
                    for p in range(2):
                        block8(L, 46 + 2 * i + p, 38 + 2 * i + p, p, 1)
                pe.wait_ge(t_pool.sem, t_pool.at("w", L))
                pe.wait_ge(evac, L * NE + (44 + FREE))
                for k in range(KD):
                    for n, (w, x) in enumerate(((wbah, Hh), (wbah, Hl), (wbal, Hh))):
                        for c in range(2):
                            last = nc.tensor.matmul(ps[:, c, 0:HT], w[:, k, :], x[:, k, c * HT:(c + 1) * HT],
                                                    start=k == 0 and n == 0, stop=k == KD - 1 and n == 2)
                last.then_inc(t_pe.sem, 1)
                pe.wait_ge(t_dve.sem, t_dve.at("ba", L))
                stand(pe, "pe")
                for t in range(4):
                    tr(ps[:, 2, t * 8:t * 8 + 8], BA[:, t * P:(t + 1) * P], 8)
                tr(ps[0:NSEQ, 2, 32:40], BA[:, SEQ:T], 8).then_inc(t_pe.sem, 1)
                pe.wait_ge(t_dve.sem, t_dve.at("g", L))
                pe.wait_ge(cm_load, L * 16 + 16)
                gv = gg[:, 0:4, :].rearrange("p t h -> p (t h)")
                nc.tensor.matmul(ps[:, 3, 0:16], CM[:, M_UP:M_UP + P], gv, start=True, stop=True)
                nc.tensor.matmul(ps[:, 3, 16:32], ones, gv, start=True, stop=True).then_inc(t_pe.sem, 1)
                pe.wait_ge(t_dve.sem, t_dve.at("sexp", L))
                nc.tensor.matmul(ps[:, 4, 0:64], CC[0:NSEQ, C_ONE:C_ONE + P], sexp[:, :, :, :].rearrange("p a h s -> p (a h s)"),
                                 start=True, stop=True).then_inc(t_pe.sem, 1)
                for c in range(NCONV):
                    last = tr(ps[0:11, 5 + c // 4, (c % 4) * P:(c % 4 + 1) * P], rawtail[:, c, :])
                last.then_inc(t_pe.sem, 1)
                pe.wait_ge(sc_load, L * 16 + 16)
                stand(pe, "pe")
                for c in range(NCONV):
                    last = tr(ps[:, 0, c * 24:(c + 1) * 24], scin[:, c * P:(c + 1) * P], 24)
                last.then_inc(t_pe.sem, 1)
                with pe.Fori(0, H) as i:
                    for p in range(2):
                        pe.wait_ge(l_act.sem, l_act.at(f"sq{p}", L, i))
                        for c in range(2):
                            last = nc.tensor.matmul(ps[:, 2 * p + c, 0:HT], ones, tb[:, p, c * HT:(c + 1) * HT],
                                                    start=True, stop=True)
                        last.then_inc(l_pe.sem, 1)
                pe.wait_ge(q_dve.sem, q_dve.at("cols", L))
                nc.tensor.matmul(ps[:, 7, 0:32], ones, qk[:, :, :].rearrange("p h s -> p (h s)"), start=True, stop=True)
                for m in range(2):
                    last = nc.tensor.matmul(ps[:, 7, 32 * (m + 1):32 * (m + 2)], CM[:, M_HALF + P * m:M_HALF + P * (m + 1)],
                                            aq[:, :, :].rearrange("p h s -> p (h s)"), start=True, stop=True)
                last.then_inc(q_pe.sem, 1)
                dflat = diag[:, :, :].rearrange("p h c -> p (h c)")
                with pe.Fori(0, 4) as c:
                    def dve(step):
                        pe.wait_ge(d_dve.sem, d_dve.at(step, L, c))

                    def each(bank, lhs, rhs):
                        for h in range(H):
                            last = nc.tensor.matmul(ps[:, bank, h * P:(h + 1) * P], lhs[:, h, :], rhs[:, h, :],
                                                    start=True, stop=True)
                        return last

                    def each_tr(bank, x):
                        for h in range(H):
                            last = tr(ps[:, bank, h * P:(h + 1) * P], x[:, h, :])
                        return last

                    def att_tok():
                        pe.wait_ge(a_dve.sem, a_dve.at("staged", L, c))
                        for t in range(4):
                            tr(ps[:, 4, t * P:(t + 1) * P], ks[:, t * P:(t + 1) * P])
                        for t in range(4):
                            tr(ps[:, 5, t * P:(t + 1) * P], vs[:, t * P:(t + 1) * P])
                        tr(ps[0:NSEQ, 6, 0:P], ks[:, SEQ:T])
                        tr(ps[0:NSEQ, 6, P:2 * P], vs[:, SEQ:T]).then_inc(a_pe.sem, 1)

                    def att_scores(q):
                        if q == 0:
                            pe.wait_ge(a_act.sem, a_act.at("tok", L, c))
                        n = (q + 1) * P
                        for m in range(2):
                            r = slice(HD * m, HD * (m + 1))
                            last = nc.tensor.matmul(ps[:, 4 + m, 0:n], qs[r, q * P:(q + 1) * P], ks[r, 0:n],
                                                    start=True, stop=True)
                        last.then_inc(a_pe.sem, 1)

                    def att_tr(q):
                        pe.wait_ge(a_dve.sem, a_dve.at(f"attn{q}", L, c))
                        if q:
                            pe.wait_ge(a_act.sem, a_act.at(f"at{q - 1}", L, c))
                        for t in range(q + 1):
                            last = tr(ps[:, 6, t * P:(t + 1) * P], sc[:, 0, t * P:(t + 1) * P])
                        last.then_inc(a_pe.sem, 1)

                    def att_out():
                        pe.wait_ge(a_act.sem, a_act.at("at3", L, c))
                        for t in range(4):
                            last = nc.tensor.matmul(ps[:, 4, t * P:SEQ], vtok[:, t, :], aT[:, t, t * P:SEQ],
                                                    start=t == 0, stop=t == 3)
                        last.then_inc(a_pe.sem, 1)

                    def state_cols(s):
                        pe.wait_ge(st_load, L * (NSEQ * 16) + s * 16 + 16)
                        pe.wait_ge(k_act.sem, k_act.begin(L, s))
                        for h in range(H):
                            last = nc.tensor.matmul(ps[:, 7, 2 * h:2 * h + 2], st[:, h, :],
                                                    dq[:, :, h, bass.ds(s, 1)].rearrange("p a o -> p (a o)"), start=True, stop=True)
                        last.then_inc(k_pe.sem, 1)

                    def spread(s, step):
                        pe.wait_ge(k_dve.sem, k_dve.at(step, L, s))
                        nc.tensor.matmul(ps[:, 7, :], ones, dflat, start=True, stop=True).then_inc(k_pe.sem, 1)

                    def invert(l):
                        dve(f"w{l}")
                        last = each(0, W1, Ui)
                        if l < LV - 1:
                            last = each(1, Ui, W1)
                        last.then_inc(d_pe.sem, 1)

                    def invert_low(l):
                        dve(f"u{l - 1}" if l > 1 else "at")
                        each(3, ATl, Ti).then_inc(d_pe.sem, 1)

                    dve("diag")
                    nc.tensor.matmul(ps[:, 0, :], ones, Ds[:, :, :].rearrange("p h c -> p (h c)"), start=True, stop=True)
                    each(1, Ks, Ks)
                    each(2, Qs, Ks)
                    each_tr(3, Ks).then_inc(d_pe.sem, 1)
                    att_tok()
                    pe.wait_ge(d_act.sem, d_act.at("qd", L, c))
                    dve("dm")
                    each_tr(0, Vs).then_inc(d_pe.sem, 1)
                    att_scores(0)
                    state_cols(2 * c)
                    dve("attn")
                    each_tr(1, At)
                    each_tr(2, attn).then_inc(d_pe.sem, 1)
                    pe.wait_ge(d_act.sem, d_act.at("vt", L, c))
                    invert_low(1)
                    spread(2 * c, "ucol")
                    invert(1)
                    att_tr(0)
                    att_scores(1)
                    invert_low(2)
                    spread(2 * c, "diag")
                    invert(2)
                    att_tr(1)
                    att_scores(2)
                    invert_low(3)
                    invert(3)
                    att_tr(2)
                    att_scores(3)
                    invert_low(4)
                    state_cols(2 * c + 1)
                    invert(4)
                    att_tr(3)
                    invert_low(5)
                    spread(2 * c + 1, "ucol")
                    invert(5)
                    att_out()
                    invert_low(6)
                    spread(2 * c + 1, "diag")
                    invert(6)
                    dve(f"u{LV - 1}")
                    each(0, Ks, S).then_inc(d_pe.sem, 1)
                    dve("w")
                    each(2, Ui, W1).then_inc(d_pe.sem, 1)
                    dve("vn")
                    for h in range(H):
                        nc.tensor.matmul(ps[:, 3, h * P:(h + 1) * P], S[:, h, :], Qs[:, h, :], start=True, stop=False)
                        last = nc.tensor.matmul(ps[:, 3, h * P:(h + 1) * P], ATl[:, h, :], attn[:, h, :], start=False, stop=True)
                    last.then_inc(d_pe.sem, 1)
                    each(1, Kt, ATl).then_inc(d_pe.sem, 1)
                pe.wait_ge(q_dve.sem, q_dve.at("max", L))
                stand(pe, "pe")
                tr(ps[0:64, 4, 0:P], ms[:, :, :].rearrange("p s m -> p (s m)")).then_inc(q_pe.sem, 1)
                pe.wait_ge(q_dve.sem, q_dve.at("col", L))
                nc.tensor.matmul(ps[:, 5, 0:64], CC[0:64, C_ONE:C_ONE + P], dg64[:, :], start=True, stop=True).then_inc(q_pe.sem, 1)
                pe.wait_ge(q_act.sem, q_act.at("exp", L))
                nc.tensor.matmul(ps[:, 6, :], ones, Sall[:, :, :, :].rearrange("p s g m -> p (s g m)"), start=True, stop=True
                                 ).then_inc(q_pe.sem, 1)
                with pe.Fori(0, NSEQ // 2) as i:
                    for j in range(2):
                        s = 2 * i + j
                        pe.wait_ge(v_dve.sem, v_dve.at("sum", L, s))
                        for h in range(H):
                            for g in range(2):
                                last = nc.tensor.matmul(ps[:, 7, bass.ds(s + h * NSEQ, 1)], vp[j][0][:, g, h * P:(h + 1) * P],
                                                        CC[:, C_ONE:C_ONE + 1], start=g == 0, stop=g == 1)
                        last.then_inc(v_pe.sem, 1)
                with pe.Fori(0, H) as i:
                    for p in range(2):
                        pe.wait_ge(n_act.sem, n_act.at(f"sq{p}", L, i))
                        for c in range(2):
                            last = nc.tensor.matmul(ps[:, 2 * p + c, 0:HT], ones, tb[:, p, c * HT:(c + 1) * HT],
                                                    start=True, stop=True)
                        last.then_inc(n_pe.sem, 1)
                pe.wait_ge(n_dve.sem, n_dve.at("l1", L, 3))
                stand(pe, "pe")
                with pe.Fori(0, 4) as i:
                    for j in range(4):
                        y = j >= 2
                        block8(L, 52 + 4 * i + j, 44 + 4 * i + j, j % 2, None if y else 1, k=4 if y else KD,
                               rh=Yh if y else Hh, rl=Yl if y else Hl, k0=4 * (j == 3))
                pe.wait_ge(p_load, L * 32 + 32)
                pe.wait_ge(evac, L * NE + (59 + FREE))
                to_features(0, ptok, 0)
                to_features(2, ptok, 1).then_inc(p_pe.sem, 1)
                pe.wait_ge(p_dve.sem, p_dve.at("t", L))
                pe.wait_ge(g_dve.sem, g_dve.at("l", L, 3))
                stand(pe, "pe")
                with pe.Fori(0, 2) as i:
                    for p in range(2):
                        block8(L, 68 + 2 * i + p, 60 + 2 * i + p, p, 1, rh=Mh, rl=Ml)
                ffn(L, 72, 64, 2, 1)
                pe.wait_ge(p_dve.sem, p_dve.at("lo", L))
                stand(pe, "pe")
                first_pair(L, 110, 94, 3, k=2, rh=PTh, rl=PTl)
                with pe.Fori(1, 4) as i:
                    block8(L, 110 + 2 * i, 94 + 2 * i, 0, 3)
                    block8(L, 111 + 2 * i, 95 + 2 * i, 1, 3, k=2, rh=PTh, rl=PTl)
            norm_sum(DEPTH - 1, 4)
            pe.wait_ge(fin_dve, 1)
            for t in range(4):
                for c in range(KD):
                    last = tr(ps[:, 2 * t + c // 4, (c % 4) * P:(c % 4 + 1) * P], yT[:, c, t * P:(t + 1) * P])
            last.then_inc(fin_pe, 1)
            pe.wait_ge(fin_dve, 2)
            for c in range(KD):
                last = tr(ps[0:NSEQ, c // 4, (c % 4) * P:(c % 4 + 1) * P], yT[:, c, SEQ:T])
            last.then_inc(fin_pe, 1)

        def split_chunk_act(act, L, nj, m, par, ready):
            ready()
            act.wait_ge(h_ready, L * NH + KD * nj + m + 1)
            nc.scalar.activation(ta[:, par, :], Xc(m), ACT.Square).then_inc(sq_ready, 1)
            nc.scalar.activation(col(Hh, m), Xc(m), ACT.Copy, scale=gain(L, nj, m)).then_inc(hh_ready, 1)

        def split_chunk_dve(dve, L, nj, m, par):
            dve.drain()
            dve.wait_ge(sq_ready, L * NH + KD * nj + m + 1)
            nc.vector.tensor_tensor(acc[:, :], acc[:, :], ta[:, par, :], ALU.add).then_inc(acc_ready, 1)
            dve.wait_ge(hh_ready, L * NH + KD * nj + m + 1)
            nc.vector.scalar_tensor_tensor(out=col(Hl, m), in0=Xc(m), scalar=gain(L, nj, m), in1=col(Hh, m).bitcast(F32),
                                           op0=ALU.mult, op1=ALU.subtract).then_inc(h_ready, 1)

        def col(t, m):
            return t[:, bass.ds(m, 1), :].rearrange("p o t -> p (o t)")

        def Xc(m):
            return col(X, m)

        def at_s(x, s):
            return x[:, :, bass.ds(s, 1)].rearrange("p h o -> p (h o)")

        def gain(L, nj, m):
            return gains[:, bass.ds((L * NORMS + nj) * KD + m, 1)]

        @block.scalar
        def _(act):
            def A_(out, in_, func, **kw):
                return nc.scalar.activation(out, in_, func, **kw)

            def hi(L, n, p, i_half):
                act.wait_ge(block_done, L * NB + n + 1)
                act.wait_ge(raw_ready[p], L * (NB // 2 * 32) + i_half * 32 + 32)
                A_(whi[:, p, :], raw[:, p, :], ACT.Copy).then_inc(hi_done, 1)

            def norm_root(L, nj):
                act.wait_ge(sum_ready, L * NORMS + (nj + 1))
                A_(halves(R[:, :]), pair(6), ACT.Sqrt, scale=1.0 / D, bias=eps).then_inc(rt_ready, 1)

            def x_ready(L, u):
                return lambda: act.wait_ge(evac, L * NE + u + (FREE + 1))

            def ffn(L, nb, ub, nj, hid):
                with act.Fori(0, KF // 2) as i:
                    for p in range(2):
                        m = 2 * i + p
                        hi(L, nb + m + 2, p, i + (nb // 2 + 1))
                        act.wait_ge(ta_ready, L * 2 * KF + m + (hid * KF + 1))
                        A_(ta[:, p, :], ta[:, p, :], ACT.Silu).then_inc(silu_done, 1)
                        act.wait_ge(g_ready, L * 2 * KF + m + (hid * KF + 1))
                        A_(col(Gh, m), tb[:, p, :], ACT.Copy).then_inc(gh_done, 1)
                with act.Fori(0, KD // 2 - 1) as i:
                    for j in range(4):
                        hi(L, nb + KF + 4 * i + j + 2, j % 2, 2 * i + (nb // 2 + 11 + j // 2 + 1))
                        if j % 2:
                            m = 2 * i + j // 2
                            split_chunk_act(act, L, nj + 1, m, j // 2, x_ready(L, ub + KF + m))
                if hid:
                    A_(PTh[:, :, :], PT[:, :, :], ACT.Copy).then_inc(p_act.sem, 1)
                for j in range(3):
                    hi(L, nb + KF + 14 + j, j % 2, nb // 2 + 18 + j // 2)
                    if j == 1:
                        split_chunk_act(act, L, nj + 1, KD - 2, 0, x_ready(L, ub + KF + KD - 2))
                split_chunk_act(act, L, nj + 1, KD - 1, 1, x_ready(L, ub + KF + KD - 1))
                hi(L, nb + KF + 17, 1, nb // 2 + 19)
                norm_root(L, nj + 1)

            act.wait_ge(loads, 16 * 22)
            A_(row[0:1, 2:10], row[0:1, 2:10], ACT.Exp)
            act.wait_ge(start_dve, 1)
            A_(row[0:1, 18:22], row[0:1, 18:22], ACT.Exp).then_inc(start_act, 1)
            hi(0, 0, 0, 0)
            for m in range(KD):
                split_chunk_act(act, 0, 0, m, m % 2, lambda: act.wait_ge(start_dve, 3 + m))
            hi(0, 1, 1, 0)
            norm_root(0, 0)

            with act.Fori(0, DEPTH) as L:
                ffn(L, 0, 0, 0, 0)
                with act.Fori(0, 3) as i:
                    for p in range(2):
                        hi(L, 40 + 2 * i + p, p, i + 20)
                        for q in range(2):
                            act.wait_ge(cv_ready, L * NCONV + (4 * i + 2 * p + q) + 1)
                            A_(U[:, bass.ds(4 * i + 2 * p + q, 1), 0:SEQ].rearrange("p o t -> p (o t)"), ta[:, q, 0:SEQ],
                               ACT.Silu).then_inc(cv_done, 1)
                for p in range(2):
                    hi(L, 46 + p, p, 23)
                act.wait_ge(ba_load, L * 16 + 16)
                A_(wbah[:, :, :], wba[:, :, :], ACT.Copy).then_inc(t_act.sem, 1)
                with act.Fori(0, 2) as i:
                    for p in range(2):
                        hi(L, 48 + 2 * i + p, p, i + 24)
                act.wait_ge(t_dve.sem, t_dve.at("bt", L))
                A_(beta[:, :, :], bt[:, :, 0:H], ACT.Sigmoid).then_inc(t_act.sem, 1)
                act.wait_ge(t_dve.sem, t_dve.at("ax", L))
                A_(sp[:, :, :], ax[:, :, :], ACT.Abs)
                act.drain()
                A_(sp[:, :, :], sp[:, :, :], ACT.Exp, scale=-1.0)
                act.drain()
                A_(sp[:, :, :], sp[:, :, :], ACT.Ln, bias=1.0).then_inc(t_act.sem, 1)
                act.wait_ge(t_dve.sem, t_dve.at("kdx", L))
                A_(eg[:, :, :], gcs[:, :, :], ACT.Exp)
                A_(ekd[:, :, :], kdx[:, :, :], ACT.Exp)
                A_(dl[:, :, :], ps[:, 3, 16:32].rearrange("p (c h) -> p c h", h=H), ACT.Exp).then_inc(t_act.sem, 1)
                A_(sp[0:NSEQ, 4, :], gg[0:NSEQ, 4, :], ACT.Exp).then_inc(t_act.sem, 1)
                act.wait_ge(t_pe.sem, t_pe.at("tails", L))
                A_(tailtok[:, :].rearrange("p (b c) -> p b c", b=3), ps[0:11, 5:8, :], ACT.Copy).then_inc(t_act.sem, 1)
                act.wait_ge(t_dve.sem, t_dve.at("csam", L))
                A_(U[:, 0:NCONV, SEQ:T], csam[:, :, :], ACT.Silu).then_inc(t_act.sem, 1)
                act.drain()
                with act.Fori(0, H) as i:
                    for p in range(2):
                        A_(tb[:, p, :], col(U, i + 4 * p), ACT.Square).then_inc(l_act.sem, 1)
                    for p in range(2):
                        act.wait_ge(l_pe.sem, l_pe.at(f"sum{p}", L, i))
                        act.wait_ge(l_dve.sem, l_dve.begin(L, i))
                        A_(halves(ta[:, p, :]), pair(2 * p), ACT.Sqrt, bias=eps).then_inc(l_act.sem, 1)
                with act.Fori(0, 4) as c:
                    def att_tok():
                        act.wait_ge(tok_out, L * (H * 64) + c * 64 + 64)
                        act.wait_ge(a_pe.sem, a_pe.at("tok", L, c))
                        A_(ktok[:, :, :], bank4(4), ACT.Copy)
                        A_(vtok[:, :, :], bank4(5), ACT.Copy)
                        A_(stok[:, :, :], ps[0:NSEQ, 6, 0:2 * P].rearrange("p (a c) -> p a c", a=2), ACT.Copy
                           ).then_inc(a_act.sem, 1)

                    def att_exp(q):
                        n = (q + 1) * P
                        act.wait_ge(a_dve.sem, a_dve.at(f"max{q}", L, c))
                        for m in range(2):
                            last = A_(sc[:, m, 0:n], sc[:, m, 0:n], ACT.Exp, scale=SCALE, bias=nm[:, m:m + 1],
                                      accum_out=sm[:, m:m + 1])
                        last.then_inc(a_act.sem, 1)

                    def att_tr(q):
                        act.wait_ge(a_pe.sem, a_pe.at(f"at{q}", L, c))
                        A_(aT[:, 0:q + 1, q * P:(q + 1) * P], ps[:, 6, 0:(q + 1) * P].rearrange("p (t c) -> p t c", c=P), ACT.Copy
                           ).then_inc(a_act.sem, 1)

                    def query(s):
                        act.wait_ge(k_pool.sem, k_pool.begin(L, s))
                        act.wait_ge(k_pe.sem, k_pe.at("q", L, s))
                        A_(qb[:, :], ps[:, 7, :], ACT.Copy).then_inc(k_act.sem, 1)

                    att_tok()
                    act.wait_ge(d_dve.sem, d_dve.at("dm", L, c))
                    A_(Ds[:, :, :], W1[:, :, :], ACT.Exp, scale=-1.0).then_inc(d_act.sem, 1)
                    A_(ATs[:, :, :], bank4(0), ACT.Exp).then_inc(d_act.sem, 1)
                    A_(Kt[:, :, :], bank4(3), ACT.Copy).then_inc(d_act.sem, 1)
                    att_exp(0)
                    act.wait_ge(d_pe.sem, d_pe.at("vt", L, c))
                    A_(Vt[:, :, :], bank4(0), ACT.Copy).then_inc(d_act.sem, 1)
                    att_tr(0)
                    att_exp(1)
                    query(2 * c)
                    att_tr(1)
                    att_exp(2)
                    att_tr(2)
                    att_exp(3)
                    att_tr(3)
                    query(2 * c + 1)
                act.wait_ge(q_dve.sem, q_dve.at("sub", L))
                A_(Sall[:, :, :, :], Sall[:, :, :, :], ACT.Exp, scale=SCALE)
                A_(eo[:, :, :], eo[:, :, :], ACT.Exp, scale=SCALE).then_inc(q_act.sem, 1)
                hi(L, 52, 0, 26)
                hi(L, 53, 1, 26)
                act.wait_ge(q_dve.sem, q_dve.at("o", L))
                with act.Fori(0, H) as i:
                    A_(col(U, i + U_Z), col(U, i + U_Z), ACT.Silu).then_inc(n_act.sem, 1)
                    for p, c in enumerate((8, U_Q)):
                        A_(tb[:, p, :], col(U, i + c), ACT.Square).then_inc(n_act.sem, 1)
                    for p in range(2):
                        act.wait_ge(n_pe.sem, n_pe.at(f"sum{p}", L, i))
                        A_(halves(ta[:, p, :]), pair(2 * p), ACT.Sqrt, scale=1.0 / P, bias=eps).then_inc(n_act.sem, 1)
                    for p, c in enumerate((8, U_Q)):
                        act.wait_ge(n_dve.sem, n_dve.at(f"y{p}", L, i))
                        A_(col(Yh, i + 4 * p), col(U, i + c), ACT.Copy).then_inc(n_act.sem, 1)
                with act.Fori(0, 4) as i:
                    for j in range(4):
                        hi(L, 54 + 4 * i + j, j % 2, 2 * i + (27 + j // 2))
                        if j < 2:
                            act.wait_ge(evac, L * NE + (44 + 4 * i + j) + (FREE + 1))
                            A_(sg[:, j, :, :], sg[:, j, :, :], ACT.Sigmoid).then_inc(g_act.sem, 1)
                    act.wait_ge(g_dve.sem, g_dve.at("m", L, i))
                    A_(Mh[:, bass.ds(2 * i, 2), :], mt[:, :, :], ACT.Copy).then_inc(g_act.sem, 1)
                with act.Fori(0, 2) as i:
                    for p in range(2):
                        hi(L, 70 + 2 * i + p, p, i + 35)
                        for q in range(2):
                            split_chunk_act(act, L, 2, 4 * i + 2 * p + q, q, x_ready(L, 60 + 2 * i + p))
                norm_root(L, 2)
                ffn(L, 72, 64, 2, 1)
                def gate(i):
                    hi(L, 112 + 2 * i, 0, i + 56)
                    act.wait_ge(evac, L * NE + (94 + 2 * i) + (FREE + 1))
                    A_(pg[:, :, :], pg[:, :, :], ACT.Sigmoid).then_inc(e_act.sem, 1)

                def squares(i):
                    act.wait_ge(e_dve.sem, e_dve.at("x", L, i))
                    for q in range(2):
                        A_(ta[:, q, :], Xc(2 * i + q), ACT.Square).then_inc(sq_ready, 1)

                with act.Fori(0, 3) as i:
                    gate(i)
                    hi(L, 113 + 2 * i, 1, i + 56)
                    squares(i)
                gate(3)
                for m in range(KD):
                    if m == KD - 2:
                        squares(3)
                    A_(Hh[:, m, :], X[:, m, :], ACT.Copy, scale=gain(L, 4, m)).then_inc(hh_ready, 1)
                hi(L, 119, 1, 59)
                norm_root(L, 4)
            act.wait_ge(fin_pe, 1)
            for t in range(4):
                last = A_(ytok[:, t, :].rearrange("p (b c) -> p b c", b=2), ps[:, 2 * t:2 * t + 2, :], ACT.Copy)
            last.then_inc(start_act, 1)

        @block.gpsimd
        def _(pool):
            for s_, v in ((split_done, FREE), (block_done, FREE), (evac, FREE), (h_ready, FREE), (gl_done, FREE),
                          (l_dve.sem, 1), (v_pe.sem, 2), (kfree, 2), (v_dve.sem, 3), (tok_out, 64), (st_out, 16), (cv_done, 2),
                          (k_dve.sem, 1), (k_act.sem, 1), (k_pool.sem, 1)):
                pool.sem_inc(s_, v)

            def lo(L, n, p):
                pool.wait_ge(hi_done, L * NB + n + 1)
                nc.gpsimd.tensor_tensor(wlo[:, p, :], raw[:, p, :], whi[:, p, :].bitcast(F32), ALU.subtract
                                        ).then_inc(split_done, 1)

            def blocks(L, n0, pairs):
                with pool.Fori(0, pairs) as i:
                    for p in range(2):
                        lo(L, n0 + 2 * i + p, p)

            def ffn(L, nb, hid):
                with pool.Fori(0, KF // 2) as i:
                    for p in range(2):
                        lo(L, nb + 2 + 2 * i + p, p)
                        pool.wait_ge(gh_done, L * 2 * KF + 2 * i + (hid * KF + p + 1))
                        nc.gpsimd.tensor_tensor(col(Gl, 2 * i + p), tb[:, p, :], col(Gh, 2 * i + p).bitcast(F32), ALU.subtract
                                                ).then_inc(gl_done, 1)

            lo(0, 0, 0)
            lo(0, 1, 1)
            with pool.Fori(0, DEPTH) as L:
                ffn(L, 0, 0)
                blocks(L, 24, 12)
                pool.wait_ge(t_act.sem, t_act.at("w", L))
                nc.gpsimd.tensor_tensor(wbal[:, :, :], wba[:, :, :], wbah[:, :, :].bitcast(F32), ALU.subtract
                                        ).then_inc(t_pool.sem, 1)
                blocks(L, 48, 2)
                with pool.Fori(0, NSEQ) as s:
                    for half in range(2):
                        pool.wait_ge(k_load[half], L * (NSEQ * 64) + s * 64 + 64)
                        if half == 0:
                            pool.wait_ge(k_act.sem, k_act.at("qb", L, s))
                        nc.gpsimd.tensor_tensor(kp[half][:, :, :], kp[half][:, :, :],
                                                qb[:, :].unsqueeze(1).broadcast_to([P, 4, SEQ]), ALU.mult).then_inc(k_pool.sem, 1)
                lo(L, 52, 0)
                lo(L, 53, 1)
                pool.wait_ge(q_dve.sem, q_dve.at("done", L))
                stand(pool, "pool")
                with pool.Fori(0, NSEQ // 2) as i:
                    for j in range(2):
                        s = 2 * i + j
                        pool.wait_ge(v_load[j][0], L * (NSEQ * 32) + i * 64 + 64)
                        kh = vp[j][0][:, :, :].rearrange("p g (h d) -> p (g h) d", d=P)
                        w = Pc[:, bass.ds(s, 1), 0:4, :].rearrange("p o g h -> p (o g h)")
                        nc.gpsimd.tensor_tensor(kh, kh, w.unsqueeze(2).broadcast_to([P, 4 * H, P]), ALU.mult
                                                ).then_inc(v_pool.sem, 1)
                blocks(L, 54, 10)
                ffn(L, 72, 1)
                blocks(L, 96, 12)

        @block.vector
        def _(dve):
            V = nc.vector

            def TT(out, a_, b_, op):
                return V.tensor_tensor(out, a_, b_, op)

            def done(L, n):
                dve.wait_ge(block_done, L * NB + n + (FREE + 1))

            def norm_rec(L, nj):
                dve.wait_ge(rt_ready, L * NORMS + (nj + 1))
                V.reciprocal(R[:, :], R[:, :])
                V.memset(acc[:, :], 0.0)
                dve.drain()

            def ffn(L, nb, ub, nj, hid):
                with dve.Fori(0, KF // 2) as i:
                    for p in range(2):
                        m = 2 * i + p
                        done(L, nb + m)
                        dve.wait_ge(gl_done, L * 2 * KF + m + (hid * KF + 1))
                        TT(halves(ta[:, p, :]), pair(4 * p), halves(R[:, :]), ALU.mult).then_inc(ta_ready, 1)
                        TT(halves(tb[:, p, :]), pair(4 * p + 2), halves(R[:, :]), ALU.mult).then_inc(evac, 1)
                        dve.drain()
                        dve.wait_ge(silu_done, L * 2 * KF + m + (hid * KF + 1))
                        TT(tb[:, p, :], tb[:, p, :], ta[:, p, :], ALU.mult).then_inc(g_ready, 1)
                def down(i):
                    for p in range(2):
                        m = 2 * i + p
                        done(L, nb + KF + 1 + 4 * i + 2 * p)
                        V.scalar_tensor_tensor(out=halves(Xc(m)), in0=pair(4 * p), scalar=0.5, in1=halves(Xc(m)),
                                               op0=ALU.mult, op1=ALU.add).then_inc(evac, 1)
                        split_chunk_dve(dve, L, nj + 1, m, p)

                with dve.Fori(0, KD // 2 - 1) as i:
                    down(i)
                if hid:
                    dve.wait_ge(p_act.sem, p_act.at("hi", L))
                    TT(PTl[:, :, :], PT[:, :, :], PTh[:, :, :].bitcast(F32), ALU.subtract).then_inc(p_dve.sem, 1)
                down(KD // 2 - 1)
                norm_rec(L, nj + 1)

            def to_u(L, n, c, p):
                done(L, n)
                for q in range(2):
                    last = TT(halves(col(U, c + q)), pair(4 * p + 2 * q), halves(R[:, :]), ALU.mult)
                last.then_inc(evac, 1)

            dve.wait_ge(loads, 16 * 22)
            V.memset(acc[:, :], 0.0)
            TT(lpr[0:1, :], lrow[0:1, 0:4 * HD], lrow[0:1, 4 * HD:8 * HD], ALU.mult)
            dve.drain()
            V.reduce_sum(row[0:1, 18:22], lpr[0:1, :].rearrange("p (a c) -> p a c", c=HD), AXX).then_inc(start_dve, 1)
            dve.wait_ge(start_pe, 1)
            V.tensor_copy(gains[:, :], ps[:, 0, 0:76])
            V.tensor_copy(convw[:, :], ps[:, 1, 0:96])
            dve.wait_ge(start_act, 1)
            TT(row[0:1, 0:2], row[0:1, 18:20], row[0:1, 20:22], ALU.subtract)
            dve.drain()
            TT(row[0:1, 0:2], row[0:1, 0:2], CC[0:1, C_LI:C_LI + 2], ALU.add).then_inc(start_dve, 1)
            dve.wait_ge(start_pe, 2)
            V.tensor_copy(bcast[:, :], ps[:, 2, 0:18])
            for c in range(KD):
                dve.wait_ge(start_pe, 3 + c)
                V.tensor_copy(X[:, c, 0:SEQ], ps[:, 4 * (c % 2), :])
                V.tensor_copy(X[:, c, SEQ:T], ps[:, 4 * (c % 2) + 1, 0:NSEQ]).then_inc(start_dve, 1)
                if c:
                    split_chunk_dve(dve, 0, 0, c - 1, (c - 1) % 2)
            split_chunk_dve(dve, 0, 0, KD - 1, 1)
            norm_rec(0, 0)

            with dve.Fori(0, DEPTH) as L:
                ffn(L, 0, 0, 0, 0)

                with dve.Fori(0, 3) as i:
                    for p in range(2):
                        c0 = 4 * i + 2 * p
                        to_u(L, 38 + 2 * i + p, c0, p)
                        dve.drain()

                        def tap(j, c):
                            return convw[:, bass.ds(L * (CONV * NCONV) + (j * NCONV) + c, 1)]

                        for j in (3, 2, 1, 0):
                            o = 3 - j
                            for q in range(2):
                                u = col(U, c0 + q)
                                if j == 3:
                                    V.tensor_copy(rawtail[:, bass.ds(c0 + q, 1), :].rearrange("p o t -> p (o t)"), u[:, SEQ - 3:T])
                                    dve.wait_ge(cv_done, L * NCONV + c0 + (q + 1))
                                    V.tensor_scalar(ta[:, q, 0:SEQ], u[:, 0:SEQ], tap(j, c0 + q), None, ALU.mult)
                                else:
                                    last = V.scalar_tensor_tensor(out=ta[:, q, o:SEQ], in0=u[:, 0:SEQ - o], scalar=tap(j, c0 + q),
                                                                  in1=ta[:, q, o:SEQ], op0=ALU.mult, op1=ALU.add)
                                    if j == 0:
                                        last.then_inc(cv_ready, 1)
                            if j:
                                dve.drain()
                for p in range(2):
                    to_u(L, 44 + p, U_Z + 2 * p, p)
                with dve.Fori(0, 3) as i:
                    for p in range(2):
                        to_u(L, 46 + 2 * i + p, U_Q + 4 * i + 2 * p, p)
                dve.wait_ge(t_pe.sem, t_pe.at("ba", L))
                TT(halves(BA[:, :]), ps[0:2 * H, 0:2, 0:HT], halves(R[0:2 * H, :]), ALU.mult).then_inc(t_dve.sem, 1)
                dve.wait_ge(cv_done, L * NCONV + (NCONV + 2))
                V.memset(bt[:, :, :], 0.0)
                dve.drain()
                dve.wait_ge(t_pe.sem, t_pe.at("tok", L))
                V.tensor_copy(bt[:, 0:4, :], ps[:, 2, 0:32].rearrange("p (t c) -> p t c", c=8))
                V.tensor_copy(bt[0:NSEQ, 4, :], ps[0:NSEQ, 2, 32:40]).then_inc(t_dve.sem, 1)
                dve.drain()

                def rowb(o):
                    return bcast[:, bass.ds(L * H + o, H)].unsqueeze(1).broadcast_to([P, 5, H])

                TT(ax[:, :, :], bt[:, :, H:2 * H], rowb(10), ALU.add).then_inc(t_dve.sem, 1)
                dve.drain()
                V.tensor_scalar(gg[:, :, :], ax[:, :, :], 0.0, None, ALU.max)
                dve.drain()
                dve.wait_ge(t_act.sem, t_act.at("softplus", L))
                TT(gg[:, :, :], gg[:, :, :], sp[:, :, :], ALU.add)
                dve.drain()
                V.scalar_tensor_tensor(out=gg[:, :, :], in0=gg[:, :, :], scalar=-1.0, in1=rowb(2), op0=ALU.mult, op1=ALU.mult
                                       ).then_inc(t_dve.sem, 1)
                dve.wait_ge(t_pe.sem, t_pe.at("gcum", L))
                V.tensor_copy(gcs[:, :, :], ps[:, 3, 0:16].rearrange("p (c h) -> p c h", h=H))
                dve.drain()
                TT(kdx[:, :, :], ps[:, 3, 16:32].rearrange("p (c h) -> p c h", h=H), gcs[:, :, :], ALU.subtract
                   ).then_inc(t_dve.sem, 1)
                dve.wait_ge(t_act.sem, t_act.at("asam", L))
                id8 = CC[0:NSEQ, C_ID:C_ID + NSEQ].unsqueeze(1).broadcast_to([NSEQ, H, NSEQ])
                for n, x in enumerate((sp, beta)):
                    last = TT(sexp[:, n, :, :], x[0:NSEQ, 4, :].unsqueeze(2).broadcast_to([NSEQ, H, NSEQ]), id8, ALU.mult)
                last.then_inc(t_dve.sem, 1)
                dve.wait_ge(t_pe.sem, t_pe.at("sab", L))
                V.tensor_copy(sab[:, :, :, :].rearrange("p a h s -> p (a h s)"), ps[:, 4, 0:64]).then_inc(t_dve.sem, 1)

                def taps(j):
                    return convw[:, bass.ds(L * (CONV * NCONV) + j * NCONV, NCONV)].unsqueeze(2).broadcast_to([P, NCONV, NSEQ])

                dve.wait_ge(t_pe.sem, t_pe.at("states", L))
                TT(csam[:, :, :], rawtail[:, :, 3:11], taps(3), ALU.mult)
                dve.drain()
                for j in range(3):
                    TT(ctmp[:, :, :], ps[:, 0, 0:24 * NCONV].rearrange("p (c s j) -> p c s j", c=NCONV, j=3)[:, :, :, j],
                       taps(j), ALU.mult)
                    dve.drain()
                    last = TT(csam[:, :, :], csam[:, :, :], ctmp[:, :, :], ALU.add)
                    if j < 2:
                        dve.drain()
                last.then_inc(t_dve.sem, 1)
                V.tensor_tensor(gda[:, :], gains[:, bass.ds(L + 74, 1)], CC[:, bass.ds(L + C_OML, 1)], ALU.mult)
                V.tensor_scalar(nlam[:, :], bcast[:, bass.ds(L, 1)], -1.0, None, ALU.mult)
                with dve.Fori(0, H) as i:
                    for p in range(2):
                        dve.wait_ge(l_act.sem, l_act.at(f"rt{p}", L, i))
                        V.reciprocal(ta[:, p, :], ta[:, p, :])
                        dve.drain()
                        V.scalar_tensor_tensor(out=col(U, i + 4 * p), in0=col(U, i + 4 * p), scalar=1.0 if p else P ** -0.5,
                                               in1=ta[:, p, :], op0=ALU.mult, op1=ALU.mult).then_inc(l_dve.sem, 1)
                dve.drain()
                V.tensor_copy(dq[:, 0, :, :], U[:, 0:4, SEQ:T])
                V.tensor_copy(dq[:, 1, :, :], U[:, 4:8, SEQ:T])
                V.tensor_copy(dv[:, :, :], U[:, 8:12, SEQ:T])
                TT(aq[:, :, :], U[:, U_Q:U_Q + 4, SEQ:T], U[:, U_K:U_K + 4, SEQ:T], ALU.mult)
                dve.drain()
                TT(bk[:, :, :], dq[:, 1, :, :], sab[:, 1, :, :], ALU.mult)
                TT(qk[:, :, :], dq[:, 0, :, :], dq[:, 1, :, :], ALU.mult).then_inc(q_dve.sem, 1)
                dve.wait_ge(q_pe.sem, q_pe.at("own", L))
                TT(qk[:, :, :], ps[:, 7, 0:32].rearrange("p (h s) -> p h s", h=H), sab[:, 1, :, :], ALU.mult)
                V.tensor_copy(own[:, :, :, :].rearrange("p m h s -> p (m h s)"), ps[:, 7, 32:96]).then_inc(q_dve.sem, 1)
                dve.drain()
                dve.wait_ge(tail_out, L * 48 + 48)
                V.memset(S[:, :, :], 0.0)
                dve.drain()
                with dve.Fori(0, 4) as c:
                    def pe_(step):
                        dve.wait_ge(d_pe.sem, d_pe.at(step, L, c))

                    def cc(x):
                        return x[:, bass.ds(c, 1), :].rearrange("p o h -> p (o h)").unsqueeze(2).broadcast_to([P, H, P])

                    def con(o):
                        return heads(CM[:, o:o + P])

                    slope = CC[:, bass.ds(c + C_SLOPE, 1)]

                    def att_stage():
                        for t_, o in ((qs, U_Q), (ks, U_K), (vs, U_V)):
                            last = V.tensor_copy(t_[:, :], col(U, c + o))
                        last.then_inc(a_dve.sem, 1)

                    def att_max(q):
                        n = (q + 1) * P
                        dve.wait_ge(a_pe.sem, a_pe.at(f"score{q}", L, c))
                        for m in range(2):
                            V.scalar_tensor_tensor(out=sc[:, m, 0:n], in0=CM[:, M_DIST + SEQ - n:M_DIST + SEQ], scalar=slope,
                                                   in1=ps[:, 4 + m, 0:n], op0=ALU.mult, op1=ALU.add)
                        dve.drain()
                        V.reduce_max(mx[:, :], sc[:, :, 0:n], AXX)
                        dve.drain()
                        V.tensor_scalar(nm[:, :], mx[:, :], -SCALE, None, ALU.mult).then_inc(a_dve.sem, 1)

                    def att_probs(q):
                        n = (q + 1) * P
                        dve.wait_ge(a_act.sem, a_act.at(f"exp{q}", L, c))
                        V.reciprocal(rc[:, :], sm[:, :])
                        dve.drain()
                        TT(rc[:, 1:2], rc[:, 1:2], nlam[:, :], ALU.mult)
                        V.tensor_scalar(sc[:, 0, 0:n], sc[:, 0, 0:n], rc[:, 0:1], None, ALU.mult)
                        dve.drain()
                        V.scalar_tensor_tensor(out=sc[:, 0, 0:n], in0=sc[:, 1, 0:n], scalar=rc[:, 1:2], in1=sc[:, 0, 0:n],
                                               op0=ALU.mult, op1=ALU.add).then_inc(a_dve.sem, 1)

                    def att_out():
                        dve.wait_ge(a_pe.sem, a_pe.at("out", L, c))
                        stand(dve, "dve")
                        V.tensor_copy(U[:, bass.ds(c + U_Q, 1), 0:SEQ].rearrange("p o t -> p (o t)"), ps[:, 4, :]
                                      ).then_inc(a_dve.sem, 1)

                    def delta_cols(s):
                        dve.wait_ge(k_pe.sem, k_pe.at("sm", L, s))
                        skq = ps[:, 7, 0:2 * H].rearrange("p (h a) -> p h a", a=2)
                        TT(ucol[:, :], skq[:, :, 1], at_s(sab[:, 0], s), ALU.mult)
                        TT(ocol[:, :], skq[:, :, 0], at_s(sab[:, 0], s), ALU.mult)
                        dve.drain()
                        TT(ucol[:, :], at_s(dv, s), ucol[:, :], ALU.subtract)
                        dve.drain()
                        TT(diag[:, :, :], heads(ident), eq(ucol[:, :]), ALU.mult).then_inc(k_dve.sem, 1)
                        dve.drain()
                        TT(ucol[:, :], ucol[:, :], at_s(qk, s), ALU.mult)
                        dve.wait_ge(st_out, L * (NSEQ * 16) + s * 16 + 16)
                        TT(stn[:, :, :], st[:, :, :], eq(at_s(sab[:, 0], s)), ALU.mult)
                        dve.drain()

                    def delta_state(s):
                        dve.wait_ge(k_pe.sem, k_pe.at("ub", L, s))
                        TT(U[:, 8:12, bass.ds(s + SEQ, 1)].rearrange("p h o -> p (h o)"), ocol[:, :], ucol[:, :], ALU.add)
                        TT(diag[:, :, :], bank4(7), eq(at_s(bk, s)), ALU.mult)
                        dve.drain()
                        TT(stn[:, :, :], stn[:, :, :], diag[:, :, :], ALU.add).then_inc(k_dve.sem, 1)
                        dve.drain()
                        TT(diag[:, :, :], heads(ident), eq(U[:, U_Q:U_Q + 4, bass.ds(s + SEQ, 1)].rearrange("p h o -> p (h o)")),
                           ALU.mult).then_inc(k_dve.sem, 1)

                    def key_sum(s, half):
                        dve.wait_ge(k_pool.sem, k_pool.at(f"half{half}", L, s))
                        V.reduce_sum(Sall[:, bass.ds(s, 1), 4 * half:4 * half + 4, :].rearrange("p o g m -> p (o g m)"),
                                     kp[half][:, :, :].rearrange("p g (m d) -> p (g m) d", d=HD), AXX).then_inc(kfree, 1)

                    def invert_low(l):
                        pe_(f"w{l}")
                        V.tensor_copy(W1[:, :, :], bank4(3)).then_inc(d_dve.sem, 1)
                        if l < LV - 1:
                            TT(ATl[:, :, :], ATs[:, :, :], con(M_LVT + P * (l + 1)), ALU.mult)

                    def invert(l):
                        pe_(f"p{l}")
                        if l < LV - 1:
                            TT(Ti[:, :, :], Ti[:, :, :], bank4(1), ALU.subtract)
                        TT(Ui[:, :, :], Ui[:, :, :], bank4(0), ALU.subtract).then_inc(d_dve.sem, 1)

                    for t_, o in ((Qs, 0), (Ks, 4), (Vs, 8)):
                        V.tensor_copy(t_[:, :, :], U[:, o:o + 4, bass.ds(c * P, P)])
                    TT(Ds[:, :, :], heads(ident), cc(gcs), ALU.mult).then_inc(d_dve.sem, 1)
                    att_stage()
                    pe_("gram")
                    TT(W1[:, :, :], bank4(0), cc(gcs), ALU.subtract)
                    dve.drain()
                    V.tensor_scalar(W1[:, :, :], W1[:, :, :], 0.0, None, ALU.max).then_inc(d_dve.sem, 1)
                    dve.wait_ge(d_act.sem, d_act.at("exp", L, c))
                    TT(attn[:, :, :], Ds[:, :, :], con(M_INCL), ALU.mult)
                    TT(At[:, :, :], Ds[:, :, :], con(M_STRICT), ALU.mult)
                    dve.drain()
                    TT(attn[:, :, :], attn[:, :, :], bank4(2), ALU.mult)
                    TT(At[:, :, :], At[:, :, :], bank4(1), ALU.mult)
                    dve.drain()
                    TT(At[:, :, :], At[:, :, :], cc(beta), ALU.mult).then_inc(d_dve.sem, 1)
                    att_max(0)
                    dve.drain()
                    dve.wait_ge(d_act.sem, d_act.at("kt", L, c))
                    TT(Qs[:, :, :], Qs[:, :, :], ATs[:, :, :], ALU.mult)
                    TT(Ti[:, :, :], At[:, :, :], con(M_LOW0), ALU.mult)
                    dve.drain()
                    TT(Ti[:, :, :], heads(ident), Ti[:, :, :], ALU.subtract)
                    pe_("at")
                    V.tensor_copy(ATs[:, :, :], bank4(1))
                    V.tensor_copy(attn[:, :, :], bank4(2))
                    dve.drain()
                    TT(Ui[:, :, :], ATs[:, :, :], con(M_LVT), ALU.mult)
                    TT(ATl[:, :, :], ATs[:, :, :], con(M_LVT + P), ALU.mult)
                    dve.drain()
                    TT(Ui[:, :, :], heads(ident), Ui[:, :, :], ALU.subtract).then_inc(d_dve.sem, 1)
                    delta_cols(2 * c)
                    invert_low(1)
                    att_probs(0)
                    invert(1)
                    delta_state(2 * c)
                    att_max(1)
                    invert_low(2)
                    att_probs(1)
                    invert(2)
                    att_max(2)
                    invert_low(3)
                    att_probs(2)
                    invert(3)
                    key_sum(2 * c, 0)
                    att_max(3)
                    invert_low(4)
                    att_probs(3)
                    invert(4)
                    delta_cols(2 * c + 1)
                    invert_low(5)
                    key_sum(2 * c, 1)
                    invert(5)
                    delta_state(2 * c + 1)
                    invert_low(6)
                    att_out()
                    invert(6)
                    pe_("ks")
                    TT(W1[:, :, :], bank4(0), cc(eg), ALU.mult)
                    dve.drain()
                    TT(W1[:, :, :], Vt[:, :, :], W1[:, :, :], ALU.subtract)
                    dve.drain()
                    TT(W1[:, :, :], W1[:, :, :], cc(beta), ALU.mult).then_inc(d_dve.sem, 1)
                    TT(Kt[:, :, :], Kt[:, :, :], cc(ekd), ALU.mult)
                    pe_("vnew")
                    V.tensor_copy(ATl[:, :, :], bank4(2)).then_inc(d_dve.sem, 1)
                    key_sum(2 * c + 1, 0)
                    pe_("out")
                    stand(dve, "dve")
                    V.tensor_copy(U[:, 8:12, bass.ds(c * P, P)], bank4(3)).then_inc(d_dve.sem, 1)
                    TT(S[:, :, :], S[:, :, :], cc(dl), ALU.mult)
                    dve.drain()
                    pe_("state")
                    TT(S[:, :, :], S[:, :, :], bank4(1), ALU.add).then_inc(d_dve.sem, 1)
                    key_sum(2 * c + 1, 1)
                    dve.drain()
                for s in range(NSEQ):
                    TT(Sall[:, s, :, :].rearrange("p g (h m) -> p (g h) m", m=2),
                       Sall[:, s, :, :].rearrange("p g (h m) -> p (g h) m", m=2),
                       CM[:, M_PAST:M_PAST + NPAGE * H].unsqueeze(2).broadcast_to([P, NPAGE * H, 2]), ALU.add)
                dve.drain()
                V.reduce_max(ms[:, :, :], Sall[:, :, :, :].rearrange("p s g m -> p s m g"), AXX).then_inc(q_dve.sem, 1)
                dve.wait_ge(q_pe.sem, q_pe.at("mt", L))
                V.reduce_max(cm64[:, :], ps[0:64, 4, 0:P], AXX)
                dve.drain()
                V.tensor_scalar(dg64[:, :], CC[0:64, C_ID:C_ID + 64], cm64[:, 0:1], None, ALU.mult).then_inc(q_dve.sem, 1)
                dve.wait_ge(q_pe.sem, q_pe.at("mb", L))

                def hm(x):
                    return x[:, :, :].rearrange("p s (h m) -> p s h m", m=2)

                ow = own[:, :, :, :].rearrange("p m h s -> p s h m")
                TT(hm(ms), ps[:, 5, 0:64].rearrange("p (s h m) -> p s h m", s=NSEQ, m=2), ow, ALU.max)
                dve.drain()

                def pages_(x):
                    return x[:, :, :].unsqueeze(2).broadcast_to([P, NSEQ, NPAGE, 2 * H])

                TT(Sall[:, :, :, :], Sall[:, :, :, :], pages_(ms), ALU.subtract)
                TT(hm(eo), ow, hm(ms), ALU.subtract).then_inc(q_dve.sem, 1)
                dve.wait_ge(q_pe.sem, q_pe.at("sum", L))
                V.reduce_sum(ls[:, :, :], ps[:, 6, :].rearrange("p (s g m) -> p s m g", s=NSEQ, g=NPAGE), AXX)
                dve.drain()
                TT(ls[:, :, :], ls[:, :, :], eo[:, :, :], ALU.add)
                dve.drain()
                V.reciprocal(ls[:, :, :], ls[:, :, :])
                dve.drain()
                V.tensor_scalar(hm(ls)[:, :, :, 1], hm(ls)[:, :, :, 1], nlam[:, 0:1], None, ALU.mult)
                dve.drain()
                TT(Sall[:, :, :, :], Sall[:, :, :, :], pages_(ls), ALU.mult)
                TT(eo[:, :, :], eo[:, :, :], ls[:, :, :], ALU.mult)
                dve.drain()
                sv = Sall[:, :, :, :].rearrange("p s g (h m) -> p (s g) h m", m=2)
                TT(Pc[:, :, :, :].rearrange("p s g h -> p (s g) h"), sv[:, :, :, 0], sv[:, :, :, 1], ALU.add)
                TT(po[:, :, :], hm(eo)[:, :, :, 0], hm(eo)[:, :, :, 1], ALU.add).then_inc(q_dve.sem, 1)
                dve.drain()
                with dve.Fori(0, NSEQ // 2) as i:
                    for j in range(2):
                        s, (v0, v1) = 2 * i + j, vp[j]
                        dve.wait_ge(v_load[j][1], L * (NSEQ * 32) + i * 64 + 64)
                        w = Pc[:, bass.ds(s, 1), 4:8, :].rearrange("p o g h -> p (o g h)")
                        kh = v1[:, :, :].rearrange("p g (h d) -> p (g h) d", d=P)
                        TT(kh, kh, w.unsqueeze(2).broadcast_to([P, 4 * H, P]), ALU.mult)
                        dve.drain()
                        TT(v1[:, 0:2, :], v1[:, 0:2, :], v1[:, 2:4, :], ALU.add).then_inc(v_dve.sem, 1)
                        dve.wait_ge(v_pool.sem, v_pool.at("half0", L, s))
                        TT(v0[:, 0:2, :], v0[:, 0:2, :], v0[:, 2:4, :], ALU.add)
                        dve.drain()
                        TT(v0[:, 0:2, :], v0[:, 0:2, :], v1[:, 0:2, :], ALU.add).then_inc(v_dve.sem, 1)
                dve.drain()
                dve.wait_ge(v_pe.sem, v_pe.at("o", L, NSEQ - 1))
                TT(aq[:, :, :], U[:, U_V:U_V + 4, SEQ:T], po[:, :, :].rearrange("p s h -> p h s"), ALU.mult)
                dve.drain()
                TT(U[:, U_Q:U_Q + 4, SEQ:T], aq[:, :, :], ps[:, 7, 0:32].rearrange("p (h s) -> p h s", h=H), ALU.add
                   ).then_inc(q_dve.sem, 1)
                with dve.Fori(0, H) as i:
                    for p, (c, g_) in enumerate(((8, gains[:, bass.ds(L + 72, 1)]), (U_Q, gda[:, 0:1]))):
                        dve.wait_ge(n_act.sem, n_act.at(f"rt{p}", L, i))
                        V.reciprocal(ta[:, p, :], ta[:, p, :])
                        dve.drain()
                        last = V.scalar_tensor_tensor(out=col(U, i + c), in0=col(U, i + c), scalar=g_, in1=ta[:, p, :],
                                                      op0=ALU.mult, op1=ALU.mult)
                        if p == 0:
                            dve.drain()
                            last = TT(col(U, i + c), col(U, i + c), col(U, i + U_Z), ALU.mult)
                        last.then_inc(n_dve.sem, 1)
                    for p, c in enumerate((8, U_Q)):
                        dve.wait_ge(n_act.sem, n_act.at(f"h{p}", L, i))
                        TT(col(Yl, i + 4 * p), col(U, i + c), col(Yh, i + 4 * p).bitcast(F32), ALU.subtract).then_inc(n_dve.sem, 1)
                def gated(i):
                    for j in range(4):
                        done(L, 52 + 4 * i + j)
                        if j >= 2:
                            dve.wait_ge(g_act.sem, g_act.at("sa" if j == 2 else "sb", L, i))
                        for q in range(2):
                            b = halves(R[:, :]) if j < 2 else halves(sg[:, j - 2, q, :])
                            o = (sg[:, j % 2, q, :], sg[:, j % 2, q, :], mt[:, q, :], gt2[:, q, :])[j]
                            last = TT(halves(o), pair(4 * (j % 2) + 2 * q), b, ALU.mult)
                        last.then_inc(evac, 1)
                    dve.drain()
                    TT(mt[:, :, :], mt[:, :, :], gt2[:, :, :], ALU.add).then_inc(g_dve.sem, 1)

                def gated_low(i):
                    dve.wait_ge(g_act.sem, g_act.at("h", L, i))
                    TT(Ml[:, bass.ds(2 * i, 2), :], mt[:, :, :], Mh[:, bass.ds(2 * i, 2), :].bitcast(F32), ALU.subtract
                       ).then_inc(g_dve.sem, 1)

                with dve.Fori(0, 3) as i:
                    gated(i)
                    gated_low(i)
                gated(3)
                dve.wait_ge(p_pe.sem, p_pe.at("t", L))
                V.tensor_copy(PT[:, 0, 0:SEQ], ps[:, 0, :])
                V.tensor_copy(PT[:, 1, 0:SEQ], ps[:, 2, :])
                V.tensor_copy(PT[:, 0, SEQ:T], ps[:, 1, 0:NSEQ])
                V.tensor_copy(PT[:, 1, SEQ:T], ps[:, 3, 0:NSEQ]).then_inc(p_dve.sem, 1)
                gated_low(3)
                with dve.Fori(0, 2) as i:
                    for p in range(2):
                        done(L, 68 + 2 * i + p)
                        for q in range(2):
                            m = 4 * i + 2 * p + q
                            last = TT(halves(Xc(m)), pair(4 * p + 2 * q), halves(Xc(m)), ALU.add)
                        last.then_inc(evac, 1)
                        for q in range(2):
                            split_chunk_dve(dve, L, 2, 4 * i + 2 * p + q, q)
                norm_rec(L, 2)
                ffn(L, 72, 64, 2, 1)
                def low(m):
                    dve.wait_ge(hh_ready, L * NH + KD * 4 + m + 1)
                    V.scalar_tensor_tensor(out=Hl[:, m, :], in0=X[:, m, :], scalar=gain(L, 4, m), in1=Hh[:, m, :].bitcast(F32),
                                           op0=ALU.mult, op1=ALU.subtract).then_inc(h_ready, 1)

                def gate(i):
                    done(L, 110 + 2 * i)
                    for q in range(2):
                        last = TT(halves(pg[:, q, :]), pair(2 * q), halves(R[:, :]), ALU.mult)
                    last.then_inc(evac, 1)

                def update(i):
                    done(L, 111 + 2 * i)
                    dve.wait_ge(e_act.sem, e_act.at("s", L, i))
                    for q in range(2):
                        last = TT(halves(pg[:, q, :]), pair(4 + 2 * q), halves(pg[:, q, :]), ALU.mult)
                    last.then_inc(evac, 1)
                    dve.drain()
                    TT(X[:, bass.ds(2 * i, 2), :], X[:, bass.ds(2 * i, 2), :], pg[:, :, :], ALU.add).then_inc(e_dve.sem, 1)
                    dve.drain()

                def squares(i):
                    for q in range(2):
                        dve.wait_ge(sq_ready, L * NH + KD * 4 + 2 * i + (q + 1))
                        TT(acc[:, :], acc[:, :], ta[:, q, :], ALU.add).then_inc(acc_ready, 1)
                        dve.drain()

                with dve.Fori(0, 3) as i:
                    gate(i)
                    update(i)
                    squares(i)
                gate(3)
                for m in range(2):
                    low(m)
                update(3)
                for m in range(2, KD):
                    low(m)
                squares(3)
                norm_rec(L, 4)
            for m in range(KD):
                last = V.scalar_tensor_tensor(out=yT[:, m, :], in0=X[:, m, :], scalar=gains[:, 64 + m:65 + m], in1=R[:, :],
                                              op0=ALU.mult, op1=ALU.mult)
            last.then_inc(fin_dve, 1)
            dve.wait_ge(start_act, 2)
            dve.wait_ge(fin_pe, 1)
            V.memset(acc[:, :], 0.0).then_inc(fin_dve, 1)
            dve.wait_ge(fin_pe, 2)
            V.tensor_copy(ytok[0:NSEQ, 4, :].rearrange("p (b c) -> p b c", b=2), ps[0:NSEQ, 0:2, :]).then_inc(fin, 1)


_CONST = dict(const_core=core_constants, const_mix=mixer_constants)
_OUTS = [
    ("y_prompt", (1, SEQ, D)), ("y_sample", (NSEQ, 1, D)),
    ("k_prompt", (DEPTH, 1, SEQ, H, P)), ("v_prompt", (DEPTH, 1, SEQ, H, P)),
    ("delta_prompt", (DEPTH, 1, H, P, P)), ("conv_prompt", (DEPTH, 1, CONV - 1, NCONV * P)),
    ("k_sample", (DEPTH, NSEQ, 1, H, P)), ("v_sample", (DEPTH, NSEQ, 1, H, P)),
    ("delta_sample", (DEPTH, NSEQ, H, P, P)), ("conv_sample", (DEPTH, NSEQ, CONV - 1, NCONV * P)),
]


def kernel(**inputs):
    import concourse.bacc as bacc
    from concourse.bass_utils import run_bass_kernel_spmd

    nc = bacc.Bacc("TRN2", target_bir_lowering=False, num_devices=1)
    arrays, ins, outs = {}, {}, {}
    for name, a in [*inputs.items(), *((n, f()) for n, f in _CONST.items())]:
        a = np.ascontiguousarray(a)
        arrays[f"in_{name}"] = a
        ins[name] = nc.dram_tensor(f"in_{name}", a.shape, mybir.dt.from_np(a.dtype), kind="ExternalInput").ap()
    for name, shape in _OUTS:
        outs[name] = nc.dram_tensor(f"out_{name}", shape, F32, kind="ExternalOutput").ap()
    hybrid_trunk(nc, ins, outs)
    r = run_bass_kernel_spmd(nc, [arrays], core_ids=[0])
    return tuple(r.results[0][f"out_{name}"] for name, _ in _OUTS)
```

```python
import math
from contextlib import ExitStack

import numpy as np
import concourse.bass as bass
from concourse import mybir

ALU = mybir.AluOpType
ACT = mybir.ActivationFunctionType
AXX = mybir.AxisListType.X
F32 = mybir.dt.float32
R32 = mybir.dt.float32r
I32 = mybir.dt.int32

P = 128
D = 1024
KD = D // P
SEQ = 512
NSEQ = 8
T = SEQ + NSEQ
HT = T // 2
DEPTH = 2
H = 4
FF = 2816
KF = FF // P
PLE = 256
PAGE = 128
NPAGE = 8
PAST = PAGE * NPAGE
CONV = 4
NCONV = 12
HD = 64
EPS = 1e-6
IN_Z = 1536
IN_BA = 2048
IN_Q = 2056
IN_GA = 3592
IN_GB = 4616
U_CONV, U_Z, U_Q, U_K, U_V, NU = 0, 12, 16, 20, 24, 28
SCALE = HD ** -0.5
NEG = -1.0e30

C_ID, C_ONE, C_SLOPE, C_LI, C_OML, C_EPS, NCC = 0, 128, 256, 260, 262, 264, 266
LV = 7
M_INCL, M_STRICT, M_UP, M_LOW0, M_LVT, M_HALF, M_DIST = 0, 128, 256, 384, 512, 512 + 128 * LV, 768 + 128 * LV
M_PAST = M_DIST + 512
NCM = M_PAST + NPAGE * H


def core_constants():
    c = np.zeros((P, NCC), np.float32)
    c[:, C_ID:C_ID + P] = np.eye(P)
    c[:, C_ONE:C_ONE + P] = 1.0
    for h in range(H):
        c[:, C_SLOPE + h] = 2.0 ** (-8.0 * (h + 1) / H) / SCALE
    for l in range(DEPTH):
        li = 0.8 - 0.6 * math.exp(-0.3 * l)
        c[:, C_LI + l] = li
        c[:, C_OML + l] = 1.0 - li
    c[:, C_EPS] = EPS
    return c


def mixer_constants():
    c = np.zeros((P, NCM), np.float32)
    i, j = np.arange(P)[:, None], np.arange(P)[None, :]
    c[:, M_INCL:M_INCL + P] = i >= j
    c[:, M_STRICT:M_STRICT + P] = i > j
    c[:, M_UP:M_UP + P] = i <= j
    for l in range(LV):
        low = (i >> (l + 1) == j >> (l + 1)) & (i >> l & 1 == 1) & (j >> l & 1 == 0)
        if l == 0:
            c[:, M_LOW0:M_LOW0 + P] = low
        c[:, M_LVT + P * l:M_LVT + P * (l + 1)] = low.T
    c[:HD, M_HALF:M_HALF + P] = 1.0
    c[HD:, M_HALF + P:M_HALF + 2 * P] = 1.0
    x = np.arange(SEQ)[None, :] - (SEQ - P)
    c[:, M_DIST:M_DIST + SEQ] = np.where(x <= i, x - i, NEG)
    for g in range(NPAGE):
        for h in range(H):
            slope = 2.0 ** (-8.0 * (h + 1) / H) / SCALE
            c[:, M_PAST + g * H + h] = -slope * (PAST - g * PAGE - np.arange(P))
    return c


class Track:

    def __init__(self, sem, steps, iters, bias):
        self.sem, self.steps, self.iters, self.bias = sem, steps, iters, bias

    def at(self, step, layer, i=0):
        n = len(self.steps)
        return layer * (self.iters * n) + i * n + (self.bias + self.steps.index(step) + 1)

    def begin(self, layer, i=0):
        n = len(self.steps)
        return layer * (self.iters * n) + i * n + self.bias


def hybrid_trunk(nc, A, O):
    ctx = ExitStack()
    with ctx:
        base = [(nc.sbuf_base + 31) // 32 * 32]

        def at(name, shape, dt, offset):
            return nc.alloc_sbuf_tensor_at(name, shape, dt, offset=offset)

        def size(shape):
            return (int(np.prod(shape[1:])) * 4 + 31) // 32 * 32

        class Region:
            def __init__(self, start):
                self.at = start

            def sb(self, name, shape, dt=F32):
                t = at(name, shape, dt, self.at)
                self.at += size(shape)
                return t

        top = Region(base[0])
        sb = top.sb
        X = sb("X", [P, KD, T])
        Hh = sb("Hh", [P, KD, T], R32)
        Hl = sb("Hl", [P, KD, T], R32)
        ring_at = top.at
        raw = sb("raw", [P, 2, 2048])
        whi = sb("whi", [P, 2, 2048], R32)
        wlo = sb("wlo", [P, 2, 2048], R32)
        ring_end = top.at
        CC = sb("CC", [P, NCC])
        R = sb("R", [P, T])
        acc = sb("acc", [P, T])
        gains = sb("gains", [P, 76])
        convw = sb("convw", [P, 96])
        bcast = sb("bcast", [P, 18])
        gda = sb("gda", [P, 1])
        nlam = sb("nlam", [P, 1])
        pages = sb("pages", [1, NSEQ * NPAGE], I32)
        PT = sb("PT", [P, 2, T])
        PTl = at("PTl", [P, 2, T], R32, top.at - size([P, 2, T]))
        tmp_at = top.at
        ta = sb("ta", [P, 2, T])
        tb = sb("tb", [P, 2, T])
        PTh = at("PTh", [P, 2, T], R32, top.at - size([P, 2, T]))
        g_at = top.at
        Gh = sb("Gh", [P, KF, T], R32)
        Gl = sb("Gl", [P, KF, T], R32)
        assert top.at <= nc.sbuf_usable_end, (top.at, nc.sbuf_usable_end)
        end = nc.sbuf_usable_end

        mix = Region(g_at)
        U = mix.sb("U", [P, NU, T])
        cm_at = mix.at
        CM = mix.sb("CM", [P, NCM])
        beta = mix.sb("beta", [P, 5, H])
        gcs = mix.sb("gcs", [P, 4, H])
        eg = mix.sb("eg", [P, 4, H])
        ekd = mix.sb("ekd", [P, 4, H])
        dl = mix.sb("dl", [P, 4, H])
        sab = mix.sb("sab", [P, 2, H, NSEQ])
        rawtail = mix.sb("rawtail", [P, NCONV, 11])
        scr_at = mix.at
        s0 = Region(scr_at)
        wba = s0.sb("wba", [P, KD, P])
        wbah = s0.sb("wbah", [P, KD, P], R32)
        wbal = s0.sb("wbal", [P, KD, P], R32)
        BA = s0.sb("BA", [2 * H, T])
        assert s0.at <= end
        s1 = Region(scr_at)
        scin = s1.sb("scin", [24, NCONV * P])
        tailtok = s1.sb("tailtok", [11, NCONV * P])
        csam = s1.sb("csam", [P, NCONV, NSEQ])
        ctmp = s1.sb("ctmp", [P, NCONV, NSEQ])
        assert s1.at <= end
        s2 = Region(tmp_at)
        bt = s2.sb("bt", [P, 5, 2 * H])
        ax = s2.sb("ax", [P, 5, H])
        sp = s2.sb("sp", [P, 5, H])
        gg = s2.sb("gg", [P, 5, H])
        kdx = s2.sb("kdx", [P, 4, H])
        sexp = s2.sb("sexp", [NSEQ, 2, H, NSEQ])
        d = Region(scr_at)
        W4 = [P, H, P]
        Qs, Ks, Vs = d.sb("Qs", W4), d.sb("Ks", W4), d.sb("Vs", W4)
        Vt, Ds, At, ATl = d.sb("Vt", W4), d.sb("Ds", W4), d.sb("At", W4), d.sb("ATl", W4)
        ATs, attn, Ti = d.sb("ATs", W4), d.sb("attn", W4), d.sb("Ti", W4)
        assert d.at <= end
        d2 = Region(tmp_at)
        Ui, W1, S, Kt = d2.sb("Ui", W4), d2.sb("W1", W4), d2.sb("S", W4), d2.sb("Kt", W4)
        a = Region(ring_at)
        qs, ks, vs = a.sb("qs", [P, T]), a.sb("ks", [P, T]), a.sb("vs", [P, T])
        ktok, vtok = a.sb("ktok", W4), a.sb("vtok", W4)
        aT = a.sb("aT", [P, 4, SEQ])
        stok = a.sb("stok", [NSEQ, 2, P])
        mx, nm, sm, rc = (a.sb(n, [P, 2]) for n in ("mx", "nm", "sm", "rc"))
        sc = a.sb("sc", [P, 2, SEQ])
        kp = [a.sb(f"kp{n}", [P, 4, SEQ]) for n in range(2)]
        diag = a.sb("diag", W4)
        st = a.sb("st", W4)
        stn = a.sb("stn", W4)
        qb = a.sb("qb", [P, SEQ])
        assert a.at <= ring_end, (a.at, ring_end)
        f = Region(d.at)
        dq = f.sb("dq", [P, 2, H, NSEQ])
        dv = f.sb("dv", [P, H, NSEQ])
        qk = f.sb("qk", [P, H, NSEQ])
        bk = f.sb("bk", [P, H, NSEQ])
        aq = f.sb("aq", [P, H, NSEQ])
        Sall = f.sb("Sall", [P, NSEQ, NPAGE, 2 * H])
        own = f.sb("own", [P, 2, H, NSEQ])
        ms, eo, ls = (f.sb(n, [P, NSEQ, 2 * H]) for n in ("ms", "eo", "ls"))
        po = f.sb("po", [P, NSEQ, H])
        Pc = f.sb("Pc", [P, NSEQ, NPAGE, H])
        cm64 = f.sb("cm64", [64, 1])
        dg64 = f.sb("dg64", [64, 64])
        ucol, ocol = f.sb("ucol", [P, H]), f.sb("ocol", [P, H])
        assert f.at <= end, (f.at, end)
        vr = Region(scr_at)
        vu = Region(g_at)
        vp = [[r.sb(f"vp{j}{n}", [P, 4, SEQ]) for n in range(2)] for j, r in enumerate((vr, vu))]
        vs2 = vr.sb("vs2", [P, 2, SEQ])
        assert vr.at <= d.at and vu.at <= g_at + 8 * T * 4
        Yh = at("Yh", [P, KD, T], R32, g_at)
        Yl = at("Yl", [P, KD, T], R32, g_at + U_K * T * 4)
        Mh = at("Mh", [P, KD, T], R32, g_at + 8 * T * 4)
        gt = Region(cm_at)
        Ml = gt.sb("Ml", [P, KD, T], R32)
        sg = gt.sb("sg", [P, 2, 2, T])
        mt = gt.sb("mt", [P, 2, T])
        gt2 = gt.sb("gt2", [P, 2, T])
        ptok = at("ptok", [P, 5, PLE], F32, g_at + U_Q * T * 4)
        assert gt.at <= end, (gt.at, end)
        z = Region(g_at)
        xtok = z.sb("xtok", [P, 5, D])
        grow = z.sb("grow", [76, P])
        crow = z.sb("crow", [96, P])
        lrow = z.sb("lrow", [1, 8 * HD])
        lpr = z.sb("lpr", [1, 4 * HD])
        row = z.sb("row", [1, 24])
        pg = at("pg", [P, 2, T], F32, g_at)
        yr = Region(g_at)
        yT = yr.sb("yT", [P, KD, T])
        ytok = yr.sb("ytok", [P, 5, D])

        ps = ctx.enter_context(nc.psum_tensor("ps", [P, 8, 512], F32))
        ident = CC[:, C_ID:C_ID + P]
        ones = CC[:, C_ONE:C_ONE + P]
        eps = CC[:, C_EPS:C_EPS + 1]

        def sem(name):
            return ctx.enter_context(nc.semaphore(name))

        NB = 118
        NE = 102
        NH = 32
        FREE = 2
        raw_ready = [sem("raw_ready0"), sem("raw_ready1")]
        hi_done = sem("hi_done")
        split_done = sem("split_done")
        block_done = sem("block_done")
        half_done = sem("half_done")
        half_evac = sem("half_evac")
        evac = sem("evac")
        hh_ready = sem("hh_ready")
        h_ready = sem("h_ready")
        sq_ready = sem("sq_ready")
        acc_ready = sem("acc_ready")
        sum_ready = sem("sum_ready")
        rt_ready = sem("rt_ready")
        ta_ready, silu_done = sem("ta_ready"), sem("silu_done")
        g_ready, gh_done, gl_done = sem("g_ready"), sem("gh_done"), sem("gl_done")
        outs = sem("outs")
        passed = {n: sem(f"passed_{n}") for n in ("sp", "pe", "dve", "act", "pool")}
        NORMS = 4

        def stand(eng, name):
            eng.sem_inc(passed[name], 1)

        def pair(b):
            return ps[:, b:b + 2, 0:HT]

        def halves(t):
            return t.rearrange("p (a c) -> p a c", a=2)

        def track(name, steps, iters=1, bias=0):
            return Track(sem(name), steps.split(), iters, bias)

        levels = range(1, LV)
        loads = sem("loads")
        start_pe, start_dve, start_act = sem("start_pe"), sem("start_dve"), sem("start_act")
        cv_ready = sem("cv_ready")
        cv_done = sem("cv_done")
        cm_load, ba_load, sc_load = sem("cm_load"), sem("ba_load"), sem("sc_load")
        tail_out, s_out, tok_out, st_out = (sem(n) for n in ("tail_out", "s_out", "tok_out", "st_out"))
        st_load, p_load = sem("st_load"), sem("p_load")
        k_load = [sem(f"k_load{n}") for n in range(2)]
        v_load = [[sem(f"v_load{j}{n}") for n in range(2)] for j in range(2)]
        kfree = sem("kfree")
        fin, fin_pe, fin_dve = sem("fin"), sem("fin_pe"), sem("fin_dve")
        t_pe = track("t_pe", "ba tok tails states gcum sab")
        t_dve = track("t_dve", "ba bt ax csam g kdx sexp sab")
        t_act = track("t_act", "w beta tailtok softplus csam decays asam")
        t_pool = track("t_pool", "w")
        l_act = track("l_act", "sq0 sq1 rt0 rt1", 4)
        l_pe = track("l_pe", "sum0 sum1", 4)
        l_dve = track("l_dve", "n0 n1", 4, bias=1)
        d_pe = track("d_pe", "bc gram vt at " + " ".join(f"w{l} t{l} u{l}" for l in levels[:-1]) + " ks w6 u6 vnew out state", 4)
        d_dve = track("d_dve", "diag dm attn at u0 " + " ".join(f"c{l} t{l} u{l}" for l in levels[:-1]) + " c6 w u6 vn o state", 4)
        d_act = track("d_act", "exp qd kt vt", 4)
        a_pe = track("a_pe", "tok " + " ".join(f"score{q} at{q}" for q in range(4)) + " out", 4)
        a_dve = track("a_dve", "staged " + " ".join(f"max{q} attn{q}" for q in range(4)) + " out", 4)
        a_act = track("a_act", "tok " + " ".join(f"exp{q} at{q}" for q in range(4)), 4)
        q_pe = track("q_pe", "own mt mb sum")
        q_dve = track("q_dve", "cols own max col sub done o")
        q_act = track("q_act", "exp")
        k_pe = track("k_pe", "q sm ub", NSEQ)
        k_dve = track("k_dve", "diag ucol st", NSEQ, bias=1)
        k_act = track("k_act", "qb", NSEQ, bias=1)
        k_pool = track("k_pool", "half0 half1", NSEQ, bias=1)
        v_pool = track("v_pool", "s00 s01 s10", NSEQ // 2)
        v_dve = track("v_dve", "sum", NSEQ, bias=2)
        v_pe = track("v_pe", "o", NSEQ, bias=2)
        m_act = track("m_act", "z sq rt", 4)
        m_pe = track("m_pe", "sum", 4)
        m_dve = track("m_dve", "y", 4, bias=1)
        n_act = track("n_act", "sq0 sq1 rt0 rt1 a0 a1 b0 b1", 2)
        n_pe = track("n_pe", "sum0 sum1", 2)
        n_dve = track("n_dve", "y0 y1 a0 a1 b0 b1", 2)
        g_act = track("g_act", "sa sb h", 4)
        g_dve = track("g_dve", "m l", 4)
        p_pe = track("p_pe", "t")
        p_act = track("p_act", "hi")
        p_dve = track("p_dve", "t lo")
        e_act = track("e_act", "s", 4)
        e_dve = track("e_dve", "x", 4)

        block = ctx.enter_context(nc.Block())

        def value_pages(eng, name, L, s, j, half):
            eng.wait_ge(v_dve.sem, v_dve.begin(L, s - 1))
            stand(eng, name)
            for g in range(4):
                pg = eng.value_load(pages[0:1, bass.ds(s * NPAGE + (half * 4 + g), 1)],
                                    min_val=0, max_val=A["cache_v"].shape[1] - 1)
                eng.dma_start(vp[j][half][:, g, :], A["cache_v"][L, bass.ds(pg, 1)].rearrange("o k h c -> k (o h c)")
                              ).then_inc(v_load[j][half], 16)

        @block.sync
        def _(sp_):
            def slot(L, n, p):
                sp_.wait_ge(split_done, L * NB + (n + 1))

            def load(p, dst_k, cols, src):
                sp_.dma_start(raw[:, p, dst_k[0] * cols:dst_k[1] * cols].rearrange("p (k c) -> p k c", c=cols),
                              src).then_inc(raw_ready[p], 16)

            def block8(L, n, p, w, c0, k=KD, cols=256):
                slot(L, n, p)
                src = w[L].rearrange("(k p) c -> p k c", p=P)
                for a0, a1 in ((0, k // 2), (k // 2, k)):
                    load(p, (a0, a1), cols, src[:, a0:a1, bass.ds(c0, cols)])

            def up(L, n, p, w1, w3, layer, c0):
                slot(L, n, p)
                for s, w in enumerate((w1, w3)):
                    sp_.dma_start(raw[:, p, :].rearrange("p (k s c) -> p s k c", s=2, c=P)[:, s],
                                  w[layer].rearrange("(k p) c -> p k c", p=P)[:, :, c0]).then_inc(raw_ready[p], 16)

            def ffn(L, nb, w1, w3, w2, first=0):
                with sp_.Fori(first, KF // 2) as i:
                    for p in range(2):
                        up(L, nb + 2 * i + p, p, w1, w3, L, bass.ds(i * 256 + p * P, P))
                with sp_.Fori(0, KD // 2) as i:
                    for j in range(4):
                        m, hf = j // 2, j % 2
                        slot(L, nb + KF + 4 * i + j, j % 2)
                        src = w2[L, hf * 11 * P:(hf + 1) * 11 * P, :].rearrange("(k p) c -> p k c", p=P)
                        for a0, a1 in ((0, 6), (6, 11)):
                            load(j % 2, (a0, a1), P, src[:, a0:a1, bass.ds(i * 256 + m * P, P)])

            def proj(L, nb, n, c0, first=0):
                with sp_.Fori(first, n) as i:
                    for p in range(2):
                        block8(L, nb + 2 * i + p, p, A["w_in"], i * 512 + (c0 + 256 * p))

            sp_.dma_start(xtok[:, 0:4, :], A["x_prompt"][0].rearrange("(t p) f -> p t f", p=P)).then_inc(loads, 16)
            sp_.dma_start(xtok[0:NSEQ, 4, :], A["x_sample"][:, 0, :]).then_inc(loads, 16)
            sp_.dma_start(CC[:, :], A["const_core"]).then_inc(loads, 16)
            for l in range(DEPTH):
                for n, name in enumerate(("norm_ffn1", "norm_mix", "norm_ffn2", "norm_ple")):
                    r0 = (NORMS * l + n) * KD
                    sp_.dma_start(grow[r0:r0 + KD, :], A[name][l].rearrange("(c p) -> c p", p=P)).then_inc(loads, 16)
            sp_.dma_start(grow[64:72, :], A["norm_final"].rearrange("(c p) -> c p", p=P)).then_inc(loads, 16)
            sp_.dma_start(grow[72:74, :], A["dn_norm"]).then_inc(loads, 16)
            sp_.dma_start(grow[74:76, :], A["da_norm"]).then_inc(loads, 16)
            sp_.dma_start(crow[:, :], A["dn_conv_w"].rearrange("l j (c p) -> (l j c) p", p=P)).then_inc(loads, 16)
            for n, name in enumerate(("da_lambda_q1", "da_lambda_q2", "da_lambda_k1", "da_lambda_k2")):
                sp_.dma_start(lrow[0:1, n * 2 * HD:(n + 1) * 2 * HD],
                              A[name].rearrange("(o l) c -> o (l c)", o=1)).then_inc(loads, 16)
            sp_.dma_start(row[0:1, 2:10], A["dn_a_log"].rearrange("(o l) h -> o (l h)", o=1)).then_inc(loads, 16)
            sp_.dma_start(row[0:1, 10:18], A["dn_dt_bias"].rearrange("(o l) h -> o (l h)", o=1)).then_inc(loads, 16)
            sp_.dma_start(pages[:, :], A["page_table"].rearrange("(o s) g -> o (s g)", o=1)).then_inc(loads, 16)
            for p in range(2):
                up(0, p, p, A["ffn1_w1"], A["ffn1_w3"], 0, slice(p * P, (p + 1) * P))
            with sp_.Fori(0, DEPTH) as L:
                ffn(L, 0, A["ffn1_w1"], A["ffn1_w3"], A["ffn1_w2"], first=1)
                block8(L, 38, 0, A["w_in"], 0)
                block8(L, 39, 1, A["w_in"], 256)
                sp_.wait_ge(evac, L * NE + (FREE + 30))
                sp_.dma_start(CM[:, :], A["const_mix"]).then_inc(cm_load, 16)
                sp_.dma_start(wba[:, :, :], A["w_in"][L].rearrange("(k p) c -> p k c", p=P)[:, :, IN_BA:IN_BA + P]
                              ).then_inc(ba_load, 16)
                proj(L, 38, 3, 0, first=1)
                proj(L, 44, 1, IN_Z)
                proj(L, 46, 2, IN_Q)
                sp_.wait_ge(t_dve.sem, t_dve.at("bt", L))
                sp_.dma_start(scin[:, :], A["state_conv"][L].rearrange("s j c -> (s j) c")).then_inc(sc_load, 16)
                block8(L, 50, 0, A["w_in"], IN_Q + 1024)
                block8(L, 51, 1, A["w_in"], IN_Q + 1280)
                sp_.wait_ge(t_act.sem, t_act.at("tailtok", L))
                sp_.dma_start(O["conv_prompt"][L, 0], tailtok[0:3, :]).then_inc(tail_out, 16)
                sp_.dma_start(O["conv_sample"][L, :, 2, :], tailtok[3:11, :]).then_inc(tail_out, 16)
                sp_.dma_start(O["conv_sample"][L, :, 0:2, :], A["state_conv"][L, :, 1:3, :]).then_inc(tail_out, 16)
                sp_.wait_ge(q_dve.sem, q_dve.at("cols", L))
                stand(sp_, "sp")
                with sp_.Fori(0, H) as c:
                    for j in range(2):
                        s = 2 * c + j
                        sp_.wait_ge(k_dve.sem, k_dve.begin(L, s))
                        sp_.dma_start(st[:, :, :], A["state_delta"][L, bass.ds(s, 1)].rearrange("o h k v -> k (o h) v")
                                      ).then_inc(st_load, 16)
                        for half in range(2):
                            sp_.wait_ge(kfree, L * 16 + s * 2 + (half + 1))
                            stand(sp_, "sp")
                            for g in range(4):
                                pg = sp_.value_load(pages[0:1, bass.ds(s * NPAGE + (half * 4 + g), 1)],
                                                    min_val=0, max_val=A["cache_k"].shape[1] - 1)
                                sp_.dma_start(kp[half][:, g, :],
                                              A["cache_k"][L, bass.ds(pg, 1)].rearrange("o k h c -> k (o h c)")
                                              ).then_inc(k_load[half], 16)
                        if j == 0:
                            sp_.wait_ge(a_act.sem, a_act.at("tok", L, c))
                            for n, (o, t) in enumerate((("k", ktok), ("v", vtok))):
                                sp_.dma_start(O[o + "_prompt"][L, 0, :, bass.ds(c, 1), :].rearrange("(t p) o c -> p t (o c)", p=P),
                                              t[:, :, :]).then_inc(tok_out, 16)
                                sp_.dma_start(O[o + "_sample"][L, :, 0, bass.ds(c, 1), :].rearrange("s o c -> s (o c)"),
                                              stok[:, n, :]).then_inc(tok_out, 16)
                        sp_.wait_ge(k_dve.sem, k_dve.at("st", L, s))
                        sp_.dma_start(O["delta_sample"][L, bass.ds(s, 1)].rearrange("o h k v -> k (o h) v"), stn[:, :, :]
                                      ).then_inc(st_out, 16)
                sp_.wait_ge(d_dve.sem, d_dve.at("state", L, 3))
                sp_.dma_start(O["delta_prompt"][L, 0].rearrange("h k v -> k h v"), S[:, :, :]).then_inc(s_out, 16)

                with sp_.Fori(0, 1) as i:
                    for j in range(2):
                        value_pages(sp_, "sp", L, 2 * i + j, j, 0)
                sp_.wait_ge(kfree, L * 16 + (16 + 2))
                sp_.wait_ge(a_dve.sem, a_dve.at("out", L, 3))
                sp_.wait_ge(st_out, L * (NSEQ * 16) + (NSEQ * 16 + 16))
                sp_.wait_ge(tok_out, L * (H * 64) + (H * 64 + 64))
                stand(sp_, "sp")
                block8(L, 52, 0, A["w_in"], IN_GA)
                block8(L, 53, 1, A["w_in"], IN_GB)
                with sp_.Fori(1, NSEQ // 2) as i:
                    for j in range(2):
                        value_pages(sp_, "sp", L, 2 * i + j, j, 0)
                sp_.wait_ge(n_dve.sem, n_dve.at("b1", L, 1))
                sp_.dma_start(ptok[:, 0:4, :], A["p_prompt"][L, 0].rearrange("(t p) f -> p t f", p=P)).then_inc(p_load, 16)
                sp_.dma_start(ptok[0:NSEQ, 4, :], A["p_sample"][L, :, 0, :]).then_inc(p_load, 16)

                def pair2(i, n, first=False):
                    if not first:
                        block8(L, n, 0, A["w_in"], i * 256 + IN_GA)
                        block8(L, n + 1, 1, A["w_in"], i * 256 + IN_GB)
                    block8(L, n + 2, 0, A["w_a"], i * 256, k=4)
                    block8(L, n + 3, 1, A["w_b"], i * 256, k=4)

                pair2(0, 52, first=True)
                with sp_.Fori(1, 4) as i:
                    pair2(i, 4 * i + 52)
                with sp_.Fori(0, 2) as i:
                    for p in range(2):
                        block8(L, 68 + 2 * i + p, p, A["w_o"], i * 512 + 256 * p)
                ffn(L, 72, A["ffn2_w1"], A["ffn2_w3"], A["ffn2_w2"])
                with sp_.Fori(0, 4) as i:
                    block8(L, 110 + 2 * i, 0, A["w_ple_gate"], i * 256)
                    block8(L, 111 + 2 * i, 1, A["w_ple"], i * 256, k=2)
                for p in range(2):
                    slot(L, NB + p, p)
                    stand(sp_, "sp")
                    for n, w in enumerate((A["ffn1_w1"], A["ffn1_w3"])):
                        sp_.dma_start(raw[:, p, :].rearrange("p (k s c) -> p s k c", s=2, c=P)[:, n],
                                      w[bass.ds(1 - L, 1)].rearrange("o (k p) c -> p (o k) c", p=P)[:, :, p * P:(p + 1) * P]
                                      ).then_inc(raw_ready[p], 16)
            sp_.wait_ge(fin, 1)
            sp_.dma_start(O["y_prompt"][0].rearrange("(t p) f -> p t f", p=P), ytok[:, 0:4, :]).then_inc(outs, 16)
            sp_.dma_start(O["y_sample"][:, 0, :], ytok[0:NSEQ, 4, :]).then_inc(outs, 16)
            sp_.wait_ge(outs, 32)
            sp_.wait_ge(tail_out, DEPTH * 48)
            sp_.wait_ge(s_out, DEPTH * 16)
            sp_.wait_ge(tok_out, (DEPTH * H + 1) * 64)
            sp_.wait_ge(st_out, (DEPTH * NSEQ + 1) * 16)

        def eq(x):
            return x.unsqueeze(2).broadcast_to([x.shape[0], x.shape[1], P])

        def heads(x):
            return x.unsqueeze(1).broadcast_to([P, H, P])

        def bank4(b):
            return ps[:, b, :].rearrange("p (h c) -> p h c", h=H)

        @block.tensor
        def _(pe):
            def product(slot, cols, ks, ms, rh, rl, bank, starts=True, stops=True, before=None, after=None, k0=0):
                for k in range(ks):
                    if before:
                        before(k)
                    for m in range(ms):
                        o = k * cols + m * P
                        h, l = whi[:, slot, o:o + P], wlo[:, slot, o:o + P]
                        for n, (w, x) in enumerate(((h, rh), (h, rl), (l, rh))):
                            for c in range(2):
                                last = nc.tensor.matmul(ps[:, bank + 2 * m + c, 0:HT], w,
                                                        x[:, k0 + k, c * HT:(c + 1) * HT],
                                                        start=starts and k == 0 and n == 0,
                                                        stop=stops and k == ks - 1 and n == 2)
                last.then_inc(block_done, 1)

            def split_ready(L, n):
                pe.wait_ge(split_done, L * NB + n + (FREE + 1))

            def banks_ready(L, u):
                pe.wait_ge(evac, L * NE + u + 1)

            def h_wait(L, nj):
                return lambda k: pe.wait_ge(h_ready, L * NH + (FREE + KD * nj + k + 1))

            def block8(L, n, u, p, nj, k=KD, rh=Hh, rl=Hl, first=False, k0=0):
                split_ready(L, n)
                banks_ready(L, u)
                if p == 1 and nj is not None:
                    pe.wait_ge(rt_ready, L * NORMS + (nj + 1))
                product(p, 256, k, 2, rh, rl, 4 * p, before=h_wait(L, nj) if first else None, k0=k0)

            def block_low(L, n, u, i):
                split_ready(L, n)
                for m in range(2):
                    if m == 0:
                        if i:
                            pe.wait_ge(half_evac, L * 8 + i)
                        else:
                            banks_ready(L, u)
                    elif i:
                        pe.wait_ge(evac, L * NE + u + FREE)
                    for k in range(KD):
                        o = k * 256 + m * P
                        h, l = whi[:, n % 2, o:o + P], wlo[:, n % 2, o:o + P]
                        for t, (w, x) in enumerate(((h, Hh), (h, Hl), (l, Hh))):
                            for c in range(2):
                                last = nc.tensor.matmul(ps[:, 2 * m + c, 0:HT], w, x[:, k, c * HT:(c + 1) * HT],
                                                        start=k == 0 and t == 0, stop=k == KD - 1 and t == 2)
                    last.then_inc(block_done if m else half_done, 1)

            def norm_sum(L, nj):
                pe.wait_ge(acc_ready, L * NH + KD * (nj + 1))
                for c in range(2):
                    last = nc.tensor.matmul(ps[:, 6 + c, 0:HT], ones, acc[:, c * HT:(c + 1) * HT], start=True, stop=True)
                last.then_inc(sum_ready, 1)

            def first_pair(L, n, u, nj, **second):
                block8(L, n, u, 0, nj, first=True)
                norm_sum(L, nj)
                block8(L, n + 1, u + 1, 1, nj, **second)

            def ffn(L, nb, ub, nj, hid):
                first_pair(L, nb, ub, nj)
                with pe.Fori(1, KF // 2) as i:
                    for p in range(2):
                        block8(L, nb + 2 * i + p, ub + 2 * i + p, p, nj)
                with pe.Fori(0, KD // 2) as i:
                    for j in range(4):
                        m, hf = j // 2, j % 2
                        split_ready(L, nb + KF + 4 * i + j)
                        if hf == 0:
                            banks_ready(L, ub + KF + 2 * i + m)
                        pe.wait_ge(gl_done, L * 2 * KF + (hid * KF + 11 * (hf + 1) + FREE))
                        product(hf, P, 11, 1, Gh, Gl, 4 * m, starts=hf == 0, stops=hf == 1, k0=11 * hf)

            def tr(out, in_, rows=P):
                return nc.tensor.transpose(out, in_, CC[0:rows, C_ID:C_ID + rows])

            def to_features(bank, tok, c):
                for t in range(4):
                    tr(ps[:, bank, t * P:(t + 1) * P], tok[:, t, c * P:(c + 1) * P])
                return tr(ps[:, bank + 1, 0:NSEQ], tok[0:NSEQ, 4, c * P:(c + 1) * P], NSEQ)

            pe.wait_ge(loads, 16 * 22)
            tr(ps[:, 0, 0:76], grow[:, :], 76)
            tr(ps[:, 1, 0:96], crow[:, :], 96).then_inc(start_pe, 1)
            pe.wait_ge(start_dve, 2)
            nc.tensor.matmul(ps[:, 2, 0:18], CC[0:1, C_ONE:C_ONE + P], row[0:1, 0:18], start=True, stop=True).then_inc(start_pe, 1)
            for c in range(KD):
                pe.wait_ge(start_dve, max(2, 1 + c))
                to_features(4 * (c % 2), xtok, c).then_inc(start_pe, 1)

            pe.wait_ge(start_dve, 2 + KD)
            with pe.Fori(0, DEPTH) as L:
                ffn(L, 0, 0, 0, 0)
                first_pair(L, 38, 30, 1)
                with pe.Fori(1, 3) as i:
                    for p in range(2):
                        block8(L, 38 + 2 * i + p, 30 + 2 * i + p, p, 1)
                block_low(L, 44, 36, 0)
                pe.wait_ge(t_pool.sem, t_pool.at("w", L))
                pe.wait_ge(evac, L * NE + (36 + FREE))
                for k in range(KD):
                    for n, (w, x) in enumerate(((wbah, Hh), (wbah, Hl), (wbal, Hh))):
                        for c in range(2):
                            last = nc.tensor.matmul(ps[:, 4 + c, 0:HT], w[:, k, :], x[:, k, c * HT:(c + 1) * HT],
                                                    start=k == 0 and n == 0, stop=k == KD - 1 and n == 2)
                last.then_inc(t_pe.sem, 1)
                block_low(L, 45, 37, 1)
                pe.wait_ge(t_dve.sem, t_dve.at("ba", L))
                stand(pe, "pe")
                for t in range(4):
                    tr(ps[:, 6, t * 8:t * 8 + 8], BA[:, t * P:(t + 1) * P], 8)
                tr(ps[0:NSEQ, 6, 32:40], BA[:, SEQ:T], 8).then_inc(t_pe.sem, 1)
                block_low(L, 46, 38, 2)
                pe.wait_ge(t_dve.sem, t_dve.at("bt", L))
                for c in range(NCONV):
                    last = tr(ps[0:11, 5 + c // 4, (c % 4) * P:(c % 4 + 1) * P], rawtail[:, c, :])
                last.then_inc(t_pe.sem, 1)
                pe.wait_ge(sc_load, L * 16 + 16)
                stand(pe, "pe")
                for c in range(NCONV):
                    last = tr(ps[:, 4, c * 24:(c + 1) * 24], scin[:, c * P:(c + 1) * P], 24)
                last.then_inc(t_pe.sem, 1)
                block_low(L, 47, 39, 3)
                pe.wait_ge(t_dve.sem, t_dve.at("g", L))
                pe.wait_ge(t_act.sem, t_act.at("tailtok", L))
                pe.wait_ge(cm_load, L * 16 + 16)
                gv = gg[:, 0:4, :].rearrange("p t h -> p (t h)")
                nc.tensor.matmul(ps[:, 7, 0:16], CM[:, M_UP:M_UP + P], gv, start=True, stop=True)
                nc.tensor.matmul(ps[:, 7, 16:32], ones, gv, start=True, stop=True).then_inc(t_pe.sem, 1)
                block_low(L, 48, 40, 4)
                pe.wait_ge(t_dve.sem, t_dve.at("sexp", L))
                pe.wait_ge(t_act.sem, t_act.at("decays", L))
                nc.tensor.matmul(ps[:, 7, 0:64], CC[0:NSEQ, C_ONE:C_ONE + P], sexp[:, :, :, :].rearrange("p a h s -> p (a h s)"),
                                 start=True, stop=True).then_inc(t_pe.sem, 1)

                def l2_sums(i):
                    for p in range(2):
                        pe.wait_ge(l_act.sem, l_act.at(f"sq{p}", L, i))
                        for c in range(2):
                            last = nc.tensor.matmul(ps[:, 4 + 2 * p + c, 0:HT], ones, tb[:, p, c * HT:(c + 1) * HT],
                                                    start=True, stop=True)
                        last.then_inc(l_pe.sem, 1)

                pe.wait_ge(t_dve.sem, t_dve.at("sab", L))
                l2_sums(0)
                block_low(L, 49, 41, 5)
                l2_sums(1)
                block_low(L, 50, 42, 6)
                l2_sums(2)
                block_low(L, 51, 43, 7)
                l2_sums(3)
                pe.wait_ge(q_dve.sem, q_dve.at("cols", L))
                nc.tensor.matmul(ps[:, 7, 0:32], ones, qk[:, :, :].rearrange("p h s -> p (h s)"), start=True, stop=True)
                for m in range(2):
                    last = nc.tensor.matmul(ps[:, 7, 32 * (m + 1):32 * (m + 2)], CM[:, M_HALF + P * m:M_HALF + P * (m + 1)],
                                            aq[:, :, :].rearrange("p h s -> p (h s)"), start=True, stop=True)
                last.then_inc(q_pe.sem, 1)
                dflat = diag[:, :, :].rearrange("p h c -> p (h c)")
                with pe.Fori(0, 4) as c:
                    def dve(step):
                        pe.wait_ge(d_dve.sem, d_dve.at(step, L, c))

                    def each(bank, lhs, rhs):
                        for h in range(H):
                            last = nc.tensor.matmul(ps[:, bank, h * P:(h + 1) * P], lhs[:, h, :], rhs[:, h, :],
                                                    start=True, stop=True)
                        return last

                    def each_tr(bank, x):
                        for h in range(H):
                            last = tr(ps[:, bank, h * P:(h + 1) * P], x[:, h, :])
                        return last

                    def att_tok():
                        pe.wait_ge(a_dve.sem, a_dve.at("staged", L, c))
                        for t in range(4):
                            tr(ps[:, 4, t * P:(t + 1) * P], ks[:, t * P:(t + 1) * P])
                        for t in range(4):
                            tr(ps[:, 5, t * P:(t + 1) * P], vs[:, t * P:(t + 1) * P])
                        tr(ps[0:NSEQ, 6, 0:P], ks[:, SEQ:T])
                        tr(ps[0:NSEQ, 6, P:2 * P], vs[:, SEQ:T]).then_inc(a_pe.sem, 1)

                    def att_scores(q):
                        if q == 0:
                            pe.wait_ge(a_act.sem, a_act.at("tok", L, c))
                        n = (q + 1) * P
                        for m in range(2):
                            r = slice(HD * m, HD * (m + 1))
                            last = nc.tensor.matmul(ps[:, 4 + m, 0:n], qs[r, q * P:(q + 1) * P], ks[r, 0:n],
                                                    start=True, stop=True)
                        last.then_inc(a_pe.sem, 1)

                    def att_tr(q):
                        pe.wait_ge(a_dve.sem, a_dve.at(f"attn{q}", L, c))
                        if q:
                            pe.wait_ge(a_act.sem, a_act.at(f"at{q - 1}", L, c))
                        for t in range(q + 1):
                            last = tr(ps[:, 6, t * P:(t + 1) * P], sc[:, 0, t * P:(t + 1) * P])
                        last.then_inc(a_pe.sem, 1)

                    def att_out():
                        pe.wait_ge(a_act.sem, a_act.at("at3", L, c))
                        for t in range(4):
                            last = nc.tensor.matmul(ps[:, 4, t * P:SEQ], vtok[:, t, :], aT[:, t, t * P:SEQ],
                                                    start=t == 0, stop=t == 3)
                        last.then_inc(a_pe.sem, 1)

                    def state_cols(s):
                        pe.wait_ge(st_load, L * (NSEQ * 16) + s * 16 + 16)
                        pe.wait_ge(k_act.sem, k_act.at("qb", L, s))
                        for h in range(H):
                            last = nc.tensor.matmul(ps[:, 7, 2 * h:2 * h + 2], st[:, h, :],
                                                    dq[:, :, h, bass.ds(s, 1)].rearrange("p a o -> p (a o)"), start=True, stop=True)
                        last.then_inc(k_pe.sem, 1)

                    def spread(s, step):
                        pe.wait_ge(k_dve.sem, k_dve.at(step, L, s))
                        nc.tensor.matmul(ps[:, 7, :], ones, dflat, start=True, stop=True).then_inc(k_pe.sem, 1)

                    def invert_low(l):
                        dve(f"t{l - 1}" if l > 1 else "at")
                        each(3, ATl, Ti).then_inc(d_pe.sem, 1)

                    def invert(l):
                        dve(f"u{l - 1}")
                        dve(f"c{l}")
                        if l < LV - 1:
                            each(1, Ui, W1).then_inc(d_pe.sem, 1)
                        each(0, W1, Ui).then_inc(d_pe.sem, 1)

                    dve("diag")
                    nc.tensor.matmul(ps[:, 0, :], ones, Ds[:, :, :].rearrange("p h c -> p (h c)"), start=True, stop=True
                                     ).then_inc(d_pe.sem, 1)
                    each(1, Ks, Ks)
                    each(2, Qs, Ks)
                    each_tr(3, Ks).then_inc(d_pe.sem, 1)
                    pe.wait_ge(d_act.sem, d_act.at("qd", L, c))
                    dve("dm")
                    each_tr(0, Vs).then_inc(d_pe.sem, 1)
                    spread(2 * c, "diag")
                    att_tok()
                    state_cols(2 * c)
                    dve("attn")
                    each_tr(1, At)
                    each_tr(2, attn).then_inc(d_pe.sem, 1)
                    att_scores(0)
                    pe.wait_ge(d_act.sem, d_act.at("vt", L, c))
                    invert_low(1)
                    spread(2 * c, "ucol")
                    invert(1)
                    invert_low(2)
                    att_tr(0)
                    att_scores(1)
                    invert(2)
                    invert_low(3)
                    att_tr(1)
                    att_scores(2)
                    invert(3)
                    invert_low(4)
                    spread(2 * c + 1, "diag")
                    att_tr(2)
                    att_scores(3)
                    invert(4)
                    invert_low(5)
                    att_tr(3)
                    state_cols(2 * c + 1)
                    invert(5)
                    each(2, Ks, S).then_inc(d_pe.sem, 1)
                    invert_low(6)
                    spread(2 * c + 1, "ucol")
                    att_out()
                    invert(6)
                    each(3, S, Qs)
                    dve(f"u{LV - 1}")
                    each(1, Ui, At).then_inc(d_pe.sem, 1)
                    dve("vn")
                    each(0, ATl, attn).then_inc(d_pe.sem, 1)
                    each(2, Kt, ATl).then_inc(d_pe.sem, 1)
                pe.wait_ge(q_dve.sem, q_dve.at("max", L))
                stand(pe, "pe")
                tr(ps[0:64, 4, 0:P], ms[:, :, :].rearrange("p s m -> p (s m)")).then_inc(q_pe.sem, 1)
                pe.wait_ge(q_dve.sem, q_dve.at("col", L))
                nc.tensor.matmul(ps[:, 5, 0:64], CC[0:64, C_ONE:C_ONE + P], dg64[:, :], start=True, stop=True).then_inc(q_pe.sem, 1)
                pe.wait_ge(q_act.sem, q_act.at("exp", L))
                nc.tensor.matmul(ps[:, 6, :], ones, Sall[:, :, :, :].rearrange("p s g m -> p (s g m)"), start=True, stop=True
                                 ).then_inc(q_pe.sem, 1)
                def delta_sum(i):
                    pe.wait_ge(m_act.sem, m_act.at("sq", L, i))
                    for c in range(2):
                        last = nc.tensor.matmul(ps[:, c, 0:HT], ones, tb[:, 0, c * HT:(c + 1) * HT], start=True, stop=True)
                    last.then_inc(m_pe.sem, 1)

                def value_sum(s):
                    pe.wait_ge(v_dve.sem, v_dve.at("sum", L, s))
                    for h in range(H):
                        for g in range(2):
                            last = nc.tensor.matmul(ps[:, 7, bass.ds(s + h * NSEQ, 1)], vs2[:, g, h * P:(h + 1) * P],
                                                    CC[:, C_ONE:C_ONE + 1], start=g == 0, stop=g == 1)
                    last.then_inc(v_pe.sem, 1)

                delta_sum(0)
                with pe.Fori(0, NSEQ // 2 - 1) as i:
                    value_sum(2 * i)
                    delta_sum(i + 1)
                    value_sum(2 * i + 1)
                with pe.Fori(NSEQ - 2, NSEQ) as s:
                    value_sum(s)
                with pe.Fori(0, H // 2) as i:
                    for p in range(2):
                        pe.wait_ge(n_act.sem, n_act.at(f"sq{p}", L, i))
                        for c in range(2):
                            last = nc.tensor.matmul(ps[:, 2 * p + c, 0:HT], ones, tb[:, p, c * HT:(c + 1) * HT],
                                                    start=True, stop=True)
                        last.then_inc(n_pe.sem, 1)
                pe.wait_ge(n_act.sem, n_act.at("rt1", L, 1))
                stand(pe, "pe")
                with pe.Fori(0, 4) as i:
                    for j in range(4):
                        y = j >= 2
                        if j == 2:
                            pe.wait_ge(n_dve.sem, n_dve.at("b1", L, 1))
                        block8(L, 52 + 4 * i + j, 44 + 4 * i + j, j % 2, None if y else 1, k=4 if y else KD,
                               rh=Yh if y else Hh, rl=Yl if y else Hl, k0=4 * (j == 3))
                pe.wait_ge(p_load, L * 32 + 32)
                pe.wait_ge(evac, L * NE + (59 + FREE))
                to_features(0, ptok, 0)
                to_features(2, ptok, 1).then_inc(p_pe.sem, 1)
                pe.wait_ge(p_dve.sem, p_dve.at("t", L))
                pe.wait_ge(g_dve.sem, g_dve.at("l", L, 3))
                stand(pe, "pe")
                with pe.Fori(0, 2) as i:
                    for p in range(2):
                        block8(L, 68 + 2 * i + p, 60 + 2 * i + p, p, 1, rh=Mh, rl=Ml)
                ffn(L, 72, 64, 2, 1)
                pe.wait_ge(p_dve.sem, p_dve.at("lo", L))
                stand(pe, "pe")
                first_pair(L, 110, 94, 3, k=2, rh=PTh, rl=PTl)
                with pe.Fori(1, 4) as i:
                    block8(L, 110 + 2 * i, 94 + 2 * i, 0, 3)
                    block8(L, 111 + 2 * i, 95 + 2 * i, 1, 3, k=2, rh=PTh, rl=PTl)
            norm_sum(DEPTH - 1, 4)
            pe.wait_ge(fin_dve, 1)
            for t in range(4):
                for c in range(KD):
                    last = tr(ps[:, 2 * t + c // 4, (c % 4) * P:(c % 4 + 1) * P], yT[:, c, t * P:(t + 1) * P])
            last.then_inc(fin_pe, 1)
            pe.wait_ge(fin_dve, 2)
            for c in range(KD):
                last = tr(ps[0:NSEQ, c // 4, (c % 4) * P:(c % 4 + 1) * P], yT[:, c, SEQ:T])
            last.then_inc(fin_pe, 1)

        def split_chunk_act(act, L, nj, m, par, ready):
            ready()
            act.wait_ge(h_ready, L * NH + KD * nj + m + 1)
            nc.scalar.activation(ta[:, par, :], Xc(m), ACT.Square).then_inc(sq_ready, 1)
            nc.scalar.activation(col(Hh, m), Xc(m), ACT.Copy, scale=gain(L, nj, m)).then_inc(hh_ready, 1)

        def split_chunk_dve(dve, L, nj, m, par):
            dve.drain()
            dve.wait_ge(sq_ready, L * NH + KD * nj + m + 1)
            nc.vector.tensor_tensor(acc[:, :], acc[:, :], ta[:, par, :], ALU.add).then_inc(acc_ready, 1)
            dve.wait_ge(hh_ready, L * NH + KD * nj + m + 1)
            nc.vector.scalar_tensor_tensor(out=col(Hl, m), in0=Xc(m), scalar=gain(L, nj, m), in1=col(Hh, m).bitcast(F32),
                                           op0=ALU.mult, op1=ALU.subtract).then_inc(h_ready, 1)

        def col(t, m):
            return t[:, bass.ds(m, 1), :].rearrange("p o t -> p (o t)")

        def Xc(m):
            return col(X, m)

        def at_s(x, s):
            return x[:, :, bass.ds(s, 1)].rearrange("p h o -> p (h o)")

        def gain(L, nj, m):
            return gains[:, bass.ds((L * NORMS + nj) * KD + m, 1)]

        @block.scalar
        def _(act):
            def A_(out, in_, func, **kw):
                return nc.scalar.activation(out, in_, func, **kw)

            def hi(L, n, p, i_half, cols=2048):
                act.wait_ge(block_done, L * NB + n + 1)
                act.wait_ge(raw_ready[p], L * (NB // 2 * 32) + i_half * 32 + 32)
                A_(whi[:, p, 0:cols], raw[:, p, 0:cols], ACT.Copy).then_inc(hi_done, 1)

            def norm_root(L, nj):
                act.wait_ge(sum_ready, L * NORMS + (nj + 1))
                A_(halves(R[:, :]), pair(6), ACT.Sqrt, scale=1.0 / D, bias=eps).then_inc(rt_ready, 1)

            def x_ready(L, u):
                return lambda: act.wait_ge(evac, L * NE + u + (FREE + 1))

            def ffn(L, nb, ub, nj, hid):
                with act.Fori(0, KF // 2) as i:
                    for p in range(2):
                        m = 2 * i + p
                        hi(L, nb + m + 2, p, i + (nb // 2 + 1))
                        act.wait_ge(ta_ready, L * 2 * KF + m + (hid * KF + 1))
                        A_(ta[:, p, :], ta[:, p, :], ACT.Silu).then_inc(silu_done, 1)
                        act.wait_ge(g_ready, L * 2 * KF + m + (hid * KF + 1))
                        A_(col(Gh, m), tb[:, p, :], ACT.Copy).then_inc(gh_done, 1)
                with act.Fori(0, KD // 2 - 1) as i:
                    for j in range(4):
                        hi(L, nb + KF + 4 * i + j + 2, j % 2, 2 * i + (nb // 2 + 11 + j // 2 + 1))
                        if j % 2:
                            m = 2 * i + j // 2
                            split_chunk_act(act, L, nj + 1, m, j // 2, x_ready(L, ub + KF + m))
                if hid:
                    A_(PTh[:, :, :], PT[:, :, :], ACT.Copy).then_inc(p_act.sem, 1)
                for j in range(3):
                    hi(L, nb + KF + 14 + j, j % 2, nb // 2 + 18 + j // 2)
                    if j == 1:
                        split_chunk_act(act, L, nj + 1, KD - 2, 0, x_ready(L, ub + KF + KD - 2))
                split_chunk_act(act, L, nj + 1, KD - 1, 1, x_ready(L, ub + KF + KD - 1))
                hi(L, nb + KF + 17, 1, nb // 2 + 19, cols=512 if hid else 2048)
                norm_root(L, nj + 1)

            act.wait_ge(loads, 16 * 22)
            A_(row[0:1, 2:10], row[0:1, 2:10], ACT.Exp)
            act.wait_ge(start_dve, 1)
            A_(row[0:1, 18:22], row[0:1, 18:22], ACT.Exp).then_inc(start_act, 1)
            hi(0, 0, 0, 0)
            for m in range(KD):
                split_chunk_act(act, 0, 0, m, m % 2, lambda: act.wait_ge(start_dve, 3 + m))
            hi(0, 1, 1, 0)
            norm_root(0, 0)

            with act.Fori(0, DEPTH) as L:
                ffn(L, 0, 0, 0, 0)
                with act.Fori(0, 3) as i:
                    for p in range(2):
                        hi(L, 40 + 2 * i + p, p, i + 20)
                        for q in range(2):
                            act.wait_ge(cv_ready, L * NCONV + (4 * i + 2 * p + q) + 1)
                            A_(U[:, bass.ds(4 * i + 2 * p + q, 1), 0:SEQ].rearrange("p o t -> p (o t)"), ta[:, q, 0:SEQ],
                               ACT.Silu).then_inc(cv_done, 1)
                act.wait_ge(ba_load, L * 16 + 16)
                A_(wbah[:, :, :], wba[:, :, :], ACT.Copy).then_inc(t_act.sem, 1)
                hi(L, 46, 0, 23)
                hi(L, 47, 1, 23)
                hi(L, 48, 0, 24)
                act.wait_ge(t_dve.sem, t_dve.at("bt", L))
                A_(beta[:, :, :], bt[:, :, 0:H], ACT.Sigmoid).then_inc(t_act.sem, 1)
                act.wait_ge(t_dve.sem, t_dve.at("ax", L))
                A_(sp[:, :, :], ax[:, :, :], ACT.Abs)
                act.drain()
                A_(sp[:, :, :], sp[:, :, :], ACT.Exp, scale=-1.0)
                act.wait_ge(t_pe.sem, t_pe.at("tails", L))
                A_(tailtok[:, :].rearrange("p (b c) -> p b c", b=3), ps[0:11, 5:8, :], ACT.Copy).then_inc(t_act.sem, 1)
                act.drain()
                A_(sp[:, :, :], sp[:, :, :], ACT.Ln, bias=1.0).then_inc(t_act.sem, 1)
                hi(L, 49, 1, 24)
                act.wait_ge(t_dve.sem, t_dve.at("csam", L))
                A_(U[:, 0:NCONV, SEQ:T], csam[:, :, :], ACT.Silu).then_inc(t_act.sem, 1)
                act.wait_ge(t_dve.sem, t_dve.at("kdx", L))
                A_(eg[:, :, :], gcs[:, :, :], ACT.Exp)
                A_(ekd[:, :, :], kdx[:, :, :], ACT.Exp)
                A_(dl[:, :, :], ps[:, 7, 16:32].rearrange("p (c h) -> p c h", h=H), ACT.Exp).then_inc(t_act.sem, 1)
                A_(sp[0:NSEQ, 4, :], gg[0:NSEQ, 4, :], ACT.Exp).then_inc(t_act.sem, 1)
                hi(L, 50, 0, 25)
                act.drain()
                for i in range(H):
                    for p in range(2):
                        A_(tb[:, p, :], U[:, i + 4 * p, :], ACT.Square).then_inc(l_act.sem, 1)
                    for p in range(2):
                        act.wait_ge(l_pe.sem, l_pe.at(f"sum{p}", L, i))
                        act.wait_ge(l_dve.sem, l_dve.begin(L, i))
                        A_(halves(ta[:, p, :]), pair(4 + 2 * p), ACT.Sqrt, bias=eps).then_inc(l_act.sem, 1)
                    if i == 0:
                        hi(L, 51, 1, 25)
                with act.Fori(0, 4) as c:
                    def att_tok():
                        act.wait_ge(tok_out, L * (H * 64) + c * 64 + 64)
                        act.wait_ge(a_pe.sem, a_pe.at("tok", L, c))
                        A_(ktok[:, :, :], bank4(4), ACT.Copy)
                        A_(vtok[:, :, :], bank4(5), ACT.Copy)
                        A_(stok[:, :, :], ps[0:NSEQ, 6, 0:2 * P].rearrange("p (a c) -> p a c", a=2), ACT.Copy
                           ).then_inc(a_act.sem, 1)

                    def att_exp(q):
                        n = (q + 1) * P
                        act.wait_ge(a_dve.sem, a_dve.at(f"max{q}", L, c))
                        for m in range(2):
                            last = A_(sc[:, m, 0:n], sc[:, m, 0:n], ACT.Exp, scale=SCALE, bias=nm[:, m:m + 1],
                                      accum_out=sm[:, m:m + 1])
                        last.then_inc(a_act.sem, 1)

                    def att_tr(q):
                        act.wait_ge(a_pe.sem, a_pe.at(f"at{q}", L, c))
                        A_(aT[:, 0:q + 1, q * P:(q + 1) * P], ps[:, 6, 0:(q + 1) * P].rearrange("p (t c) -> p t c", c=P), ACT.Copy
                           ).then_inc(a_act.sem, 1)

                    def query(s):
                        act.wait_ge(k_pool.sem, k_pool.begin(L, s))
                        act.wait_ge(k_pe.sem, k_pe.at("q", L, s))
                        A_(qb[:, :], ps[:, 7, :], ACT.Copy).then_inc(k_act.sem, 1)

                    act.wait_ge(d_dve.sem, d_dve.at("dm", L, c))
                    A_(Ds[:, :, :], W1[:, :, :], ACT.Exp, scale=-1.0).then_inc(d_act.sem, 1)
                    A_(ATs[:, :, :], bank4(0), ACT.Exp).then_inc(d_act.sem, 1)
                    act.wait_ge(d_pe.sem, d_pe.at("gram", L, c))
                    A_(Kt[:, :, :], bank4(3), ACT.Copy).then_inc(d_act.sem, 1)
                    act.wait_ge(d_pe.sem, d_pe.at("vt", L, c))
                    A_(Vt[:, :, :], bank4(0), ACT.Copy).then_inc(d_act.sem, 1)
                    query(2 * c)
                    att_tok()
                    att_exp(0)
                    att_tr(0)
                    att_exp(1)
                    att_tr(1)
                    att_exp(2)
                    query(2 * c + 1)
                    att_tr(2)
                    att_exp(3)
                    att_tr(3)
                act.wait_ge(d_dve.sem, d_dve.at("state", L, 3))
                stand(act, "act")
                with act.Fori(0, 1) as i:
                    for j in range(2):
                        value_pages(act, "act", L, 2 * i + j, j, 1)
                act.wait_ge(q_dve.sem, q_dve.at("sub", L))
                A_(Sall[:, :, :, :], Sall[:, :, :, :], ACT.Exp, scale=SCALE)
                A_(eo[:, :, :], eo[:, :, :], ACT.Exp, scale=SCALE).then_inc(q_act.sem, 1)
                act.wait_ge(s_out, L * 16 + 16)
                stand(act, "act")
                def delta_norm(i):
                    A_(tb[:, 0, :], col(U, i + 8), ACT.Square)
                    A_(col(U, i + U_Z), col(U, i + U_Z), ACT.Silu).then_inc(m_act.sem, 2)
                    act.wait_ge(m_pe.sem, m_pe.at("sum", L, i))
                    act.wait_ge(m_dve.sem, m_dve.begin(L, i))
                    A_(halves(ta[:, 0, :]), ps[:, 0:2, 0:HT], ACT.Sqrt, scale=1.0 / P, bias=eps).then_inc(m_act.sem, 1)

                delta_norm(0)
                with act.Fori(0, H - 1) as i:
                    value_pages(act, "act", L, 2 * i + 2, 0, 1)
                    delta_norm(i + 1)
                    value_pages(act, "act", L, 2 * i + 3, 1, 1)
                hi(L, 52, 0, 26)
                hi(L, 53, 1, 26)
                act.wait_ge(q_dve.sem, q_dve.at("o", L))
                stand(act, "act")
                with act.Fori(0, H // 2) as i:
                    for p in range(2):
                        A_(tb[:, p, :], col(U, 2 * i + (U_Q + p)), ACT.Square).then_inc(n_act.sem, 1)
                    for p in range(2):
                        act.wait_ge(n_pe.sem, n_pe.at(f"sum{p}", L, i))
                        A_(halves(ta[:, p, :]), pair(2 * p), ACT.Sqrt, scale=1.0 / P, bias=eps).then_inc(n_act.sem, 1)
                    for p in range(2):
                        A_(col(Yh, 2 * i + p), col(U, 2 * i + (8 + p)), ACT.Copy).then_inc(n_act.sem, 1)
                    for p in range(2):
                        act.wait_ge(n_dve.sem, n_dve.at(f"y{p}", L, i))
                        A_(col(Yh, 2 * i + (4 + p)), col(U, 2 * i + (U_Q + p)), ACT.Copy).then_inc(n_act.sem, 1)
                with act.Fori(0, 4) as i:
                    for j in range(4):
                        hi(L, 54 + 4 * i + j, j % 2, 2 * i + (27 + j // 2), cols=1024 if j < 2 else 2048)
                        if j < 2:
                            act.wait_ge(evac, L * NE + (44 + 4 * i + j) + (FREE + 1))
                            A_(sg[:, j, :, :], sg[:, j, :, :], ACT.Sigmoid).then_inc(g_act.sem, 1)
                    act.wait_ge(g_dve.sem, g_dve.at("m", L, i))
                    A_(Mh[:, bass.ds(2 * i, 2), :], mt[:, :, :], ACT.Copy).then_inc(g_act.sem, 1)
                with act.Fori(0, 2) as i:
                    for p in range(2):
                        hi(L, 70 + 2 * i + p, p, i + 35)
                        for q in range(2):
                            split_chunk_act(act, L, 2, 4 * i + 2 * p + q, q, x_ready(L, 60 + 2 * i + p))
                norm_root(L, 2)
                ffn(L, 72, 64, 2, 1)
                def gate(i):
                    hi(L, 112 + 2 * i, 0, i + 56)
                    act.wait_ge(evac, L * NE + (94 + 2 * i) + (FREE + 1))
                    A_(pg[:, :, :], pg[:, :, :], ACT.Sigmoid).then_inc(e_act.sem, 1)

                def squares(i):
                    act.wait_ge(e_dve.sem, e_dve.at("x", L, i))
                    for q in range(2):
                        A_(ta[:, q, :], Xc(2 * i + q), ACT.Square).then_inc(sq_ready, 1)

                with act.Fori(0, 3) as i:
                    gate(i)
                    hi(L, 113 + 2 * i, 1, i + 56, cols=512)
                    squares(i)
                gate(3)
                for m in range(KD):
                    if m == KD - 2:
                        squares(3)
                    A_(Hh[:, m, :], X[:, m, :], ACT.Copy, scale=gain(L, 4, m)).then_inc(hh_ready, 1)
                hi(L, 119, 1, 59)
                norm_root(L, 4)
            act.wait_ge(fin_pe, 1)
            for t in range(4):
                last = A_(ytok[:, t, :].rearrange("p (b c) -> p b c", b=2), ps[:, 2 * t:2 * t + 2, :], ACT.Copy)
            last.then_inc(start_act, 1)

        @block.gpsimd
        def _(pool):
            for s_, v in ((split_done, FREE), (block_done, FREE), (evac, FREE), (h_ready, FREE), (gl_done, FREE),
                          (l_dve.sem, 1), (v_pe.sem, 2), (kfree, 2), (v_dve.sem, 2), (tok_out, 64), (st_out, 16), (cv_done, 2),
                          (k_dve.sem, 1), (m_dve.sem, 1), (k_act.sem, 1), (k_pool.sem, 1)):
                pool.sem_inc(s_, v)

            def lo(L, n, p, cols=2048):
                pool.wait_ge(hi_done, L * NB + n + 1)
                nc.gpsimd.tensor_tensor(wlo[:, p, 0:cols], raw[:, p, 0:cols], whi[:, p, 0:cols].bitcast(F32), ALU.subtract
                                        ).then_inc(split_done, 1)

            def blocks(L, n0, pairs):
                with pool.Fori(0, pairs) as i:
                    for p in range(2):
                        lo(L, n0 + 2 * i + p, p)

            def ffn(L, nb, hid):
                with pool.Fori(0, KF // 2) as i:
                    for p in range(2):
                        lo(L, nb + 2 + 2 * i + p, p)
                        pool.wait_ge(gh_done, L * 2 * KF + 2 * i + (hid * KF + p + 1))
                        nc.gpsimd.tensor_tensor(col(Gl, 2 * i + p), tb[:, p, :], col(Gh, 2 * i + p).bitcast(F32), ALU.subtract
                                                ).then_inc(gl_done, 1)

            lo(0, 0, 0)
            lo(0, 1, 1)
            with pool.Fori(0, DEPTH) as L:
                ffn(L, 0, 0)
                blocks(L, 24, 11)
                pool.wait_ge(t_act.sem, t_act.at("w", L))
                nc.gpsimd.tensor_tensor(wbal[:, :, :], wba[:, :, :], wbah[:, :, :].bitcast(F32), ALU.subtract
                                        ).then_inc(t_pool.sem, 1)
                blocks(L, 46, 3)
                with pool.Fori(0, NSEQ) as s:
                    for half in range(2):
                        pool.wait_ge(k_load[half], L * (NSEQ * 64) + s * 64 + 64)
                        if half == 0:
                            pool.wait_ge(k_act.sem, k_act.at("qb", L, s))
                        nc.gpsimd.tensor_tensor(kp[half][:, :, :], kp[half][:, :, :],
                                                qb[:, :].unsqueeze(1).broadcast_to([P, 4, SEQ]), ALU.mult).then_inc(k_pool.sem, 1)
                pool.wait_ge(q_dve.sem, q_dve.at("done", L))
                stand(pool, "pool")
                with pool.Fori(0, NSEQ // 2) as i:
                    for j in range(2):
                        s = 2 * i + j
                        for half in range(2 - j):
                            pool.wait_ge(v_load[j][half], L * (NSEQ * 32) + i * 64 + 64)
                            kh = vp[j][half][:, :, :].rearrange("p g (h d) -> p (g h) d", d=P)
                            w = Pc[:, bass.ds(s, 1), 4 * half:4 * half + 4, :].rearrange("p o g h -> p (o g h)")
                            nc.gpsimd.tensor_tensor(kh, kh, w.unsqueeze(2).broadcast_to([P, 4 * H, P]), ALU.mult
                                                    ).then_inc(v_pool.sem, 1)
                lo(L, 52, 0)
                lo(L, 53, 1)
                with pool.Fori(0, 4) as i:
                    for j in range(4):
                        lo(L, 54 + 4 * i + j, j % 2, cols=1024 if j < 2 else 2048)
                blocks(L, 70, 2)
                ffn(L, 72, 1)
                blocks(L, 96, 7)
                with pool.Fori(0, 4) as i:
                    lo(L, 110 + 2 * i, 0)
                    lo(L, 111 + 2 * i, 1, cols=512)
                lo(L, 118, 0)
                lo(L, 119, 1)

        @block.vector
        def _(dve):
            V = nc.vector

            def TT(out, a_, b_, op):
                return V.tensor_tensor(out, a_, b_, op)

            def done(L, n):
                dve.wait_ge(block_done, L * NB + n + (FREE + 1))

            def norm_rec(L, nj):
                dve.wait_ge(rt_ready, L * NORMS + (nj + 1))
                V.reciprocal(R[:, :], R[:, :])
                V.memset(acc[:, :], 0.0)
                dve.drain()

            def ffn(L, nb, ub, nj, hid):
                with dve.Fori(0, KF // 2) as i:
                    for p in range(2):
                        m = 2 * i + p
                        done(L, nb + m)
                        dve.wait_ge(gl_done, L * 2 * KF + m + (hid * KF + 1))
                        TT(halves(ta[:, p, :]), pair(4 * p), halves(R[:, :]), ALU.mult).then_inc(ta_ready, 1)
                        TT(halves(tb[:, p, :]), pair(4 * p + 2), halves(R[:, :]), ALU.mult).then_inc(evac, 1)
                        dve.drain()
                        dve.wait_ge(silu_done, L * 2 * KF + m + (hid * KF + 1))
                        TT(tb[:, p, :], tb[:, p, :], ta[:, p, :], ALU.mult).then_inc(g_ready, 1)
                def down(i):
                    for p in range(2):
                        m = 2 * i + p
                        done(L, nb + KF + 1 + 4 * i + 2 * p)
                        V.scalar_tensor_tensor(out=halves(Xc(m)), in0=pair(4 * p), scalar=0.5, in1=halves(Xc(m)),
                                               op0=ALU.mult, op1=ALU.add).then_inc(evac, 1)
                        split_chunk_dve(dve, L, nj + 1, m, p)

                with dve.Fori(0, KD // 2 - 1) as i:
                    down(i)
                if hid:
                    dve.wait_ge(p_act.sem, p_act.at("hi", L))
                    TT(PTl[:, :, :], PT[:, :, :], PTh[:, :, :].bitcast(F32), ALU.subtract).then_inc(p_dve.sem, 1)
                down(KD // 2 - 1)
                norm_rec(L, nj + 1)

            def to_u(L, n, c, p):
                done(L, n)
                for q in range(2):
                    last = TT(halves(col(U, c + q)), pair(4 * p + 2 * q), halves(R[:, :]), ALU.mult)
                last.then_inc(evac, 1)

            dve.wait_ge(loads, 16 * 22)
            V.memset(acc[:, :], 0.0)
            TT(lpr[0:1, :], lrow[0:1, 0:4 * HD], lrow[0:1, 4 * HD:8 * HD], ALU.mult)
            dve.drain()
            V.reduce_sum(row[0:1, 18:22], lpr[0:1, :].rearrange("p (a c) -> p a c", c=HD), AXX).then_inc(start_dve, 1)
            dve.wait_ge(start_pe, 1)
            V.tensor_copy(gains[:, :], ps[:, 0, 0:76])
            V.tensor_copy(convw[:, :], ps[:, 1, 0:96])
            dve.wait_ge(start_act, 1)
            TT(row[0:1, 0:2], row[0:1, 18:20], row[0:1, 20:22], ALU.subtract)
            dve.drain()
            TT(row[0:1, 0:2], row[0:1, 0:2], CC[0:1, C_LI:C_LI + 2], ALU.add).then_inc(start_dve, 1)
            dve.wait_ge(start_pe, 2)
            V.tensor_copy(bcast[:, :], ps[:, 2, 0:18])
            for c in range(KD):
                dve.wait_ge(start_pe, 3 + c)
                V.tensor_copy(X[:, c, 0:SEQ], ps[:, 4 * (c % 2), :])
                V.tensor_copy(X[:, c, SEQ:T], ps[:, 4 * (c % 2) + 1, 0:NSEQ]).then_inc(start_dve, 1)
                if c:
                    split_chunk_dve(dve, 0, 0, c - 1, (c - 1) % 2)
            split_chunk_dve(dve, 0, 0, KD - 1, 1)
            norm_rec(0, 0)

            with dve.Fori(0, DEPTH) as L:
                ffn(L, 0, 0, 0, 0)

                with dve.Fori(0, 3) as i:
                    for p in range(2):
                        c0 = 4 * i + 2 * p
                        to_u(L, 38 + 2 * i + p, c0, p)
                        dve.drain()

                        def tap(j, c):
                            return convw[:, bass.ds(L * (CONV * NCONV) + (j * NCONV) + c, 1)]

                        for j in (3, 2, 1, 0):
                            o = 3 - j
                            for q in range(2):
                                u = col(U, c0 + q)
                                if j == 3:
                                    V.tensor_copy(rawtail[:, bass.ds(c0 + q, 1), :].rearrange("p o t -> p (o t)"), u[:, SEQ - 3:T])
                                    dve.wait_ge(cv_done, L * NCONV + c0 + (q + 1))
                                    V.tensor_scalar(ta[:, q, 0:SEQ], u[:, 0:SEQ], tap(j, c0 + q), None, ALU.mult)
                                else:
                                    last = V.scalar_tensor_tensor(out=ta[:, q, o:SEQ], in0=u[:, 0:SEQ - o], scalar=tap(j, c0 + q),
                                                                  in1=ta[:, q, o:SEQ], op0=ALU.mult, op1=ALU.add)
                                    if j == 0:
                                        last.then_inc(cv_ready, 1)
                            if j:
                                dve.drain()
                def low_u(n, i):
                    for m in range(2):
                        if m:
                            done(L, n)
                        else:
                            dve.wait_ge(half_done, L * 8 + (i + 1))
                        TT(halves(U[:, U_Z + 2 * i + m, :]), pair(2 * m), halves(R[:, :]), ALU.mult
                           ).then_inc(evac if m else half_evac, 1)

                def rowb(o):
                    return bcast[:, bass.ds(L * H + o, H)].unsqueeze(1).broadcast_to([P, 5, H])

                low_u(44, 0)
                dve.wait_ge(t_pe.sem, t_pe.at("ba", L))
                TT(halves(BA[:, :]), ps[0:2 * H, 4:6, 0:HT], halves(R[0:2 * H, :]), ALU.mult).then_inc(t_dve.sem, 1)
                dve.wait_ge(cv_done, L * NCONV + (NCONV + 2))
                V.memset(bt[:, :, :], 0.0)
                dve.drain()
                low_u(45, 1)
                dve.wait_ge(t_pe.sem, t_pe.at("tok", L))
                V.tensor_copy(bt[:, 0:4, :], ps[:, 6, 0:32].rearrange("p (t c) -> p t c", c=8))
                V.tensor_copy(bt[0:NSEQ, 4, :], ps[0:NSEQ, 6, 32:40]).then_inc(t_dve.sem, 1)
                dve.drain()
                TT(ax[:, :, :], bt[:, :, H:2 * H], rowb(10), ALU.add).then_inc(t_dve.sem, 1)
                dve.drain()
                V.tensor_scalar(gg[:, :, :], ax[:, :, :], 0.0, None, ALU.max)
                low_u(46, 2)

                def taps(j):
                    return convw[:, bass.ds(L * (CONV * NCONV) + j * NCONV, NCONV)].unsqueeze(2).broadcast_to([P, NCONV, NSEQ])

                dve.wait_ge(t_pe.sem, t_pe.at("states", L))
                TT(csam[:, :, :], rawtail[:, :, 3:11], taps(3), ALU.mult)
                dve.drain()
                for j in range(3):
                    TT(ctmp[:, :, :], ps[:, 4, 0:24 * NCONV].rearrange("p (c s j) -> p c s j", c=NCONV, j=3)[:, :, :, j],
                       taps(j), ALU.mult)
                    dve.drain()
                    last = TT(csam[:, :, :], csam[:, :, :], ctmp[:, :, :], ALU.add)
                    if j < 2:
                        dve.drain()
                last.then_inc(t_dve.sem, 1)
                dve.wait_ge(t_act.sem, t_act.at("softplus", L))
                TT(gg[:, :, :], gg[:, :, :], sp[:, :, :], ALU.add)
                dve.drain()
                V.scalar_tensor_tensor(out=gg[:, :, :], in0=gg[:, :, :], scalar=-1.0, in1=rowb(2), op0=ALU.mult, op1=ALU.mult
                                       ).then_inc(t_dve.sem, 1)
                V.tensor_tensor(gda[:, :], gains[:, bass.ds(L + 74, 1)], CC[:, bass.ds(L + C_OML, 1)], ALU.mult)
                V.tensor_scalar(nlam[:, :], bcast[:, bass.ds(L, 1)], -1.0, None, ALU.mult)
                low_u(47, 3)
                dve.wait_ge(t_pe.sem, t_pe.at("gcum", L))
                V.tensor_copy(gcs[:, :, :], ps[:, 7, 0:16].rearrange("p (c h) -> p c h", h=H))
                dve.drain()
                TT(kdx[:, :, :], ps[:, 7, 16:32].rearrange("p (c h) -> p c h", h=H), gcs[:, :, :], ALU.subtract
                   ).then_inc(t_dve.sem, 1)
                dve.wait_ge(t_act.sem, t_act.at("asam", L))
                id8 = CC[0:NSEQ, C_ID:C_ID + NSEQ].unsqueeze(1).broadcast_to([NSEQ, H, NSEQ])
                for n, x in enumerate((sp, beta)):
                    last = TT(sexp[:, n, :, :], x[0:NSEQ, 4, :].unsqueeze(2).broadcast_to([NSEQ, H, NSEQ]), id8, ALU.mult)
                last.then_inc(t_dve.sem, 1)
                low_u(48, 4)
                dve.wait_ge(t_pe.sem, t_pe.at("sab", L))
                V.tensor_copy(sab[:, :, :, :].rearrange("p a h s -> p (a h s)"), ps[:, 7, 0:64]).then_inc(t_dve.sem, 1)

                def l2_norms(i):
                    for p in range(2):
                        dve.wait_ge(l_act.sem, l_act.at(f"rt{p}", L, i))
                        V.reciprocal(ta[:, p, :], ta[:, p, :])
                        dve.drain()
                        V.scalar_tensor_tensor(out=U[:, i + 4 * p, :], in0=U[:, i + 4 * p, :], scalar=1.0 if p else P ** -0.5,
                                               in1=ta[:, p, :], op0=ALU.mult, op1=ALU.mult).then_inc(l_dve.sem, 1)

                l2_norms(0)
                low_u(49, 5)
                l2_norms(1)
                low_u(50, 6)
                l2_norms(2)
                low_u(51, 7)
                l2_norms(3)
                dve.drain()
                V.tensor_copy(dq[:, 0, :, :], U[:, 0:4, SEQ:T])
                V.tensor_copy(dq[:, 1, :, :], U[:, 4:8, SEQ:T])
                V.tensor_copy(dv[:, :, :], U[:, 8:12, SEQ:T])
                TT(aq[:, :, :], U[:, U_Q:U_Q + 4, SEQ:T], U[:, U_K:U_K + 4, SEQ:T], ALU.mult)
                dve.drain()
                TT(bk[:, :, :], dq[:, 1, :, :], sab[:, 1, :, :], ALU.mult)
                TT(qk[:, :, :], dq[:, 0, :, :], dq[:, 1, :, :], ALU.mult).then_inc(q_dve.sem, 1)
                dve.wait_ge(q_pe.sem, q_pe.at("own", L))
                TT(qk[:, :, :], ps[:, 7, 0:32].rearrange("p (h s) -> p h s", h=H), sab[:, 1, :, :], ALU.mult)
                V.tensor_copy(own[:, :, :, :].rearrange("p m h s -> p (m h s)"), ps[:, 7, 32:96]).then_inc(q_dve.sem, 1)
                dve.drain()
                dve.wait_ge(tail_out, L * 48 + 48)
                V.memset(S[:, :, :], 0.0)
                dve.drain()
                with dve.Fori(0, 4) as c:
                    def pe_(step):
                        dve.wait_ge(d_pe.sem, d_pe.at(step, L, c))

                    def cc(x):
                        return x[:, bass.ds(c, 1), :].rearrange("p o h -> p (o h)").unsqueeze(2).broadcast_to([P, H, P])

                    def con(o):
                        return heads(CM[:, o:o + P])

                    slope = CC[:, bass.ds(c + C_SLOPE, 1)]

                    def att_stage():
                        for t_, o in ((qs, U_Q), (ks, U_K), (vs, U_V)):
                            last = V.tensor_copy(t_[:, :], col(U, c + o))
                        last.then_inc(a_dve.sem, 1)

                    def att_max(q):
                        n = (q + 1) * P
                        dve.wait_ge(a_pe.sem, a_pe.at(f"score{q}", L, c))
                        for m in range(2):
                            V.scalar_tensor_tensor(out=sc[:, m, 0:n], in0=CM[:, M_DIST + SEQ - n:M_DIST + SEQ], scalar=slope,
                                                   in1=ps[:, 4 + m, 0:n], op0=ALU.mult, op1=ALU.add)
                        dve.drain()
                        V.reduce_max(mx[:, :], sc[:, :, 0:n], AXX)
                        dve.drain()
                        V.tensor_scalar(nm[:, :], mx[:, :], -SCALE, None, ALU.mult).then_inc(a_dve.sem, 1)

                    def att_probs(q):
                        n = (q + 1) * P
                        dve.wait_ge(a_act.sem, a_act.at(f"exp{q}", L, c))
                        V.reciprocal(rc[:, :], sm[:, :])
                        dve.drain()
                        TT(rc[:, 1:2], rc[:, 1:2], nlam[:, :], ALU.mult)
                        V.tensor_scalar(sc[:, 0, 0:n], sc[:, 0, 0:n], rc[:, 0:1], None, ALU.mult)
                        dve.drain()
                        V.scalar_tensor_tensor(out=sc[:, 0, 0:n], in0=sc[:, 1, 0:n], scalar=rc[:, 1:2], in1=sc[:, 0, 0:n],
                                               op0=ALU.mult, op1=ALU.add).then_inc(a_dve.sem, 1)

                    def att_out():
                        dve.wait_ge(a_pe.sem, a_pe.at("out", L, c))
                        stand(dve, "dve")
                        V.tensor_copy(U[:, bass.ds(c + U_Q, 1), 0:SEQ].rearrange("p o t -> p (o t)"), ps[:, 4, :]
                                      ).then_inc(a_dve.sem, 1)

                    def delta_cols(s):
                        dve.wait_ge(k_pe.sem, k_pe.at("sm", L, s))
                        skq = ps[:, 7, 0:2 * H].rearrange("p (h a) -> p h a", a=2)
                        TT(ucol[:, :], skq[:, :, 1], at_s(sab[:, 0], s), ALU.mult)
                        TT(ocol[:, :], skq[:, :, 0], at_s(sab[:, 0], s), ALU.mult)
                        dve.drain()
                        TT(ucol[:, :], at_s(dv, s), ucol[:, :], ALU.subtract)
                        dve.drain()
                        TT(diag[:, :, :], heads(ident), eq(ucol[:, :]), ALU.mult).then_inc(k_dve.sem, 1)
                        dve.drain()
                        TT(ucol[:, :], ucol[:, :], at_s(qk, s), ALU.mult)
                        dve.wait_ge(st_out, L * (NSEQ * 16) + s * 16 + 16)
                        TT(stn[:, :, :], st[:, :, :], eq(at_s(sab[:, 0], s)), ALU.mult)
                        dve.drain()

                    def delta_state(s):
                        dve.wait_ge(k_pe.sem, k_pe.at("ub", L, s))
                        TT(U[:, 8:12, bass.ds(s + SEQ, 1)].rearrange("p h o -> p (h o)"), ocol[:, :], ucol[:, :], ALU.add)
                        TT(diag[:, :, :], bank4(7), eq(at_s(bk, s)), ALU.mult)
                        dve.drain()
                        TT(stn[:, :, :], stn[:, :, :], diag[:, :, :], ALU.add).then_inc(k_dve.sem, 1)

                    def query_diag(s):
                        dve.drain()
                        TT(diag[:, :, :], heads(ident), eq(U[:, U_Q:U_Q + 4, bass.ds(s + SEQ, 1)].rearrange("p h o -> p (h o)")),
                           ALU.mult).then_inc(k_dve.sem, 1)

                    def key_sum(s, half):
                        dve.wait_ge(k_pool.sem, k_pool.at(f"half{half}", L, s))
                        V.reduce_sum(Sall[:, bass.ds(s, 1), 4 * half:4 * half + 4, :].rearrange("p o g m -> p (o g m)"),
                                     kp[half][:, :, :].rearrange("p g (m d) -> p (g m) d", d=HD), AXX).then_inc(kfree, 1)

                    def invert_low(l):
                        pe_(f"w{l}")
                        V.tensor_copy(W1[:, :, :], bank4(3)).then_inc(d_dve.sem, 1)
                        if l < LV - 1:
                            TT(ATl[:, :, :], ATs[:, :, :], con(M_LVT + P * (l + 1)), ALU.mult)
                            pe_(f"t{l}")
                            TT(Ti[:, :, :], Ti[:, :, :], bank4(1), ALU.subtract).then_inc(d_dve.sem, 1)

                    def invert(l):
                        pe_(f"u{l}")
                        TT(Ui[:, :, :], Ui[:, :, :], bank4(0), ALU.subtract).then_inc(d_dve.sem, 1)

                    for t_, o in ((Qs, 0), (Ks, 4), (Vs, 8)):
                        V.tensor_copy(t_[:, :, :], U[:, o:o + 4, bass.ds(c * P, P)])
                    TT(Ds[:, :, :], heads(ident), cc(gcs), ALU.mult).then_inc(d_dve.sem, 1)
                    query_diag(2 * c)
                    att_stage()
                    pe_("bc")
                    TT(W1[:, :, :], bank4(0), cc(gcs), ALU.subtract)
                    dve.drain()
                    V.tensor_scalar(W1[:, :, :], W1[:, :, :], 0.0, None, ALU.max).then_inc(d_dve.sem, 1)
                    dve.wait_ge(d_act.sem, d_act.at("exp", L, c))
                    TT(At[:, :, :], Ds[:, :, :], con(M_STRICT), ALU.mult)
                    TT(attn[:, :, :], Ds[:, :, :], con(M_INCL), ALU.mult)
                    dve.drain()
                    pe_("gram")
                    TT(At[:, :, :], At[:, :, :], bank4(1), ALU.mult)
                    TT(attn[:, :, :], attn[:, :, :], bank4(2), ALU.mult)
                    dve.drain()
                    TT(At[:, :, :], At[:, :, :], cc(beta), ALU.mult).then_inc(d_dve.sem, 1)
                    dve.drain()
                    TT(Ti[:, :, :], At[:, :, :], con(M_LOW0), ALU.mult)
                    dve.drain()
                    TT(Ti[:, :, :], heads(ident), Ti[:, :, :], ALU.subtract)
                    dve.wait_ge(d_act.sem, d_act.at("kt", L, c))
                    TT(Qs[:, :, :], Qs[:, :, :], ATs[:, :, :], ALU.mult)
                    dve.drain()
                    pe_("at")
                    V.tensor_copy(ATs[:, :, :], bank4(1))
                    dve.drain()
                    TT(ATl[:, :, :], ATs[:, :, :], con(M_LVT + P), ALU.mult).then_inc(d_dve.sem, 1)
                    TT(Ui[:, :, :], ATs[:, :, :], con(M_LVT), ALU.mult)
                    V.tensor_copy(attn[:, :, :], bank4(2))
                    dve.drain()
                    TT(Ui[:, :, :], heads(ident), Ui[:, :, :], ALU.subtract).then_inc(d_dve.sem, 1)
                    att_max(0)
                    delta_cols(2 * c)
                    invert_low(1)
                    key_sum(2 * c, 0)
                    invert(1)
                    att_probs(0)
                    delta_state(2 * c)
                    invert_low(2)
                    att_max(1)
                    invert(2)
                    att_probs(1)
                    key_sum(2 * c, 1)
                    invert_low(3)
                    att_max(2)
                    query_diag(2 * c + 1)
                    invert(3)
                    att_probs(2)
                    invert_low(4)
                    att_max(3)
                    invert(4)
                    att_probs(3)
                    invert_low(5)
                    delta_cols(2 * c + 1)
                    invert(5)
                    pe_("ks")
                    TT(At[:, :, :], bank4(2), cc(eg), ALU.mult)
                    dve.drain()
                    TT(At[:, :, :], Vt[:, :, :], At[:, :, :], ALU.subtract)
                    invert_low(6)
                    key_sum(2 * c + 1, 0)
                    dve.drain()
                    TT(At[:, :, :], At[:, :, :], cc(beta), ALU.mult).then_inc(d_dve.sem, 1)
                    invert(6)
                    TT(Kt[:, :, :], Kt[:, :, :], cc(ekd), ALU.mult)
                    pe_("vnew")
                    V.tensor_copy(ATl[:, :, :], bank4(1)).then_inc(d_dve.sem, 1)
                    delta_state(2 * c + 1)
                    pe_("out")
                    stand(dve, "dve")
                    V.tensor_copy(U[:, 8:12, bass.ds(c * P, P)], bank4(3))
                    dve.drain()
                    TT(U[:, 8:12, bass.ds(c * P, P)], U[:, 8:12, bass.ds(c * P, P)], bank4(0), ALU.add).then_inc(d_dve.sem, 1)
                    TT(S[:, :, :], S[:, :, :], cc(dl), ALU.mult)
                    dve.drain()
                    pe_("state")
                    TT(S[:, :, :], S[:, :, :], bank4(2), ALU.add).then_inc(d_dve.sem, 1)
                    att_out()
                    key_sum(2 * c + 1, 1)
                    dve.drain()
                for s in range(NSEQ):
                    TT(Sall[:, s, :, :].rearrange("p g (h m) -> p (g h) m", m=2),
                       Sall[:, s, :, :].rearrange("p g (h m) -> p (g h) m", m=2),
                       CM[:, M_PAST:M_PAST + NPAGE * H].unsqueeze(2).broadcast_to([P, NPAGE * H, 2]), ALU.add)
                dve.drain()
                V.reduce_max(ms[:, :, :], Sall[:, :, :, :].rearrange("p s g m -> p s m g"), AXX).then_inc(q_dve.sem, 1)
                dve.wait_ge(q_pe.sem, q_pe.at("mt", L))
                V.reduce_max(cm64[:, :], ps[0:64, 4, 0:P], AXX)
                dve.drain()
                V.tensor_scalar(dg64[:, :], CC[0:64, C_ID:C_ID + 64], cm64[:, 0:1], None, ALU.mult).then_inc(q_dve.sem, 1)
                dve.wait_ge(q_pe.sem, q_pe.at("mb", L))

                def hm(x):
                    return x[:, :, :].rearrange("p s (h m) -> p s h m", m=2)

                ow = own[:, :, :, :].rearrange("p m h s -> p s h m")
                TT(hm(ms), ps[:, 5, 0:64].rearrange("p (s h m) -> p s h m", s=NSEQ, m=2), ow, ALU.max)
                dve.drain()

                def pages_(x):
                    return x[:, :, :].unsqueeze(2).broadcast_to([P, NSEQ, NPAGE, 2 * H])

                TT(Sall[:, :, :, :], Sall[:, :, :, :], pages_(ms), ALU.subtract)
                TT(hm(eo), ow, hm(ms), ALU.subtract).then_inc(q_dve.sem, 1)
                dve.wait_ge(q_pe.sem, q_pe.at("sum", L))
                V.reduce_sum(ls[:, :, :], ps[:, 6, :].rearrange("p (s g m) -> p s m g", s=NSEQ, g=NPAGE), AXX)
                dve.drain()
                TT(ls[:, :, :], ls[:, :, :], eo[:, :, :], ALU.add)
                dve.drain()
                V.reciprocal(ls[:, :, :], ls[:, :, :])
                dve.drain()
                V.tensor_scalar(hm(ls)[:, :, :, 1], hm(ls)[:, :, :, 1], nlam[:, 0:1], None, ALU.mult)
                dve.drain()
                TT(Sall[:, :, :, :], Sall[:, :, :, :], pages_(ls), ALU.mult)
                TT(eo[:, :, :], eo[:, :, :], ls[:, :, :], ALU.mult)
                dve.drain()
                sv = Sall[:, :, :, :].rearrange("p s g (h m) -> p (s g) h m", m=2)
                TT(Pc[:, :, :, :].rearrange("p s g h -> p (s g) h"), sv[:, :, :, 0], sv[:, :, :, 1], ALU.add)
                TT(po[:, :, :], hm(eo)[:, :, :, 0], hm(eo)[:, :, :, 1], ALU.add).then_inc(q_dve.sem, 1)
                dve.drain()
                with dve.Fori(0, NSEQ // 2) as i:
                    dve.wait_ge(m_act.sem, m_act.at("rt", L, i))
                    V.reciprocal(ta[:, 0, :], ta[:, 0, :])
                    dve.drain()
                    V.scalar_tensor_tensor(out=col(U, i + 8), in0=col(U, i + 8), scalar=gains[:, bass.ds(L + 72, 1)],
                                           in1=ta[:, 0, :], op0=ALU.mult, op1=ALU.mult)
                    dve.drain()
                    TT(col(U, i + 8), col(U, i + 8), col(U, i + U_Z), ALU.mult).then_inc(m_dve.sem, 1)
                    for j in range(2):
                        s, (v0, v1) = 2 * i + j, vp[j]
                        if j:
                            dve.wait_ge(v_load[j][1], L * (NSEQ * 32) + i * 64 + 64)
                            w = Pc[:, bass.ds(s, 1), 4:8, :].rearrange("p o g h -> p (o g h)")
                            kh = v1[:, :, :].rearrange("p g (h d) -> p (g h) d", d=P)
                            TT(kh, kh, w.unsqueeze(2).broadcast_to([P, 4 * H, P]), ALU.mult)
                            dve.drain()
                        for half, v in ((1, v1), (0, v0)) if j else ((0, v0), (1, v1)):
                            if not (j and half):
                                dve.wait_ge(v_pool.sem, v_pool.at(f"s{j}{half}", L, i))
                            last = TT(v[:, 0:2, :], v[:, 0:2, :], v[:, 2:4, :], ALU.add)
                        dve.drain()
                        dve.wait_ge(v_pe.sem, v_pe.begin(L, s))
                        TT(vs2[:, :, :], v0[:, 0:2, :], v1[:, 0:2, :], ALU.add).then_inc(v_dve.sem, 1)
                dve.drain()
                dve.wait_ge(v_pe.sem, v_pe.at("o", L, NSEQ - 1))
                TT(aq[:, :, :], U[:, U_V:U_V + 4, SEQ:T], po[:, :, :].rearrange("p s h -> p h s"), ALU.mult)
                dve.drain()
                TT(U[:, U_Q:U_Q + 4, SEQ:T], aq[:, :, :], ps[:, 7, 0:32].rearrange("p (h s) -> p h s", h=H), ALU.add
                   ).then_inc(q_dve.sem, 1)
                with dve.Fori(0, H // 2) as i:
                    for p in range(2):
                        y = col(U, 2 * i + (U_Q + p))
                        dve.wait_ge(n_act.sem, n_act.at(f"rt{p}", L, i))
                        V.reciprocal(ta[:, p, :], ta[:, p, :])
                        dve.drain()
                        V.scalar_tensor_tensor(out=y, in0=y, scalar=gda[:, 0:1], in1=ta[:, p, :],
                                               op0=ALU.mult, op1=ALU.mult).then_inc(n_dve.sem, 1)
                    for c, u in ((0, 8), (4, U_Q)):
                        for p in range(2):
                            dve.wait_ge(n_act.sem, n_act.at(f"{'b' if c else 'a'}{p}", L, i))
                            TT(col(Yl, 2 * i + (c + p)), col(U, 2 * i + (u + p)), col(Yh, 2 * i + (c + p)).bitcast(F32),
                               ALU.subtract).then_inc(n_dve.sem, 1)
                def gated(i):
                    for j in range(4):
                        done(L, 52 + 4 * i + j)
                        if j >= 2:
                            dve.wait_ge(g_act.sem, g_act.at("sa" if j == 2 else "sb", L, i))
                        for q in range(2):
                            b = halves(R[:, :]) if j < 2 else halves(sg[:, j - 2, q, :])
                            o = (sg[:, j % 2, q, :], sg[:, j % 2, q, :], mt[:, q, :], gt2[:, q, :])[j]
                            last = TT(halves(o), pair(4 * (j % 2) + 2 * q), b, ALU.mult)
                        last.then_inc(evac, 1)
                    dve.drain()
                    TT(mt[:, :, :], mt[:, :, :], gt2[:, :, :], ALU.add).then_inc(g_dve.sem, 1)

                def gated_low(i):
                    dve.wait_ge(g_act.sem, g_act.at("h", L, i))
                    TT(Ml[:, bass.ds(2 * i, 2), :], mt[:, :, :], Mh[:, bass.ds(2 * i, 2), :].bitcast(F32), ALU.subtract
                       ).then_inc(g_dve.sem, 1)

                with dve.Fori(0, 3) as i:
                    gated(i)
                    gated_low(i)
                gated(3)
                dve.wait_ge(p_pe.sem, p_pe.at("t", L))
                V.tensor_copy(PT[:, 0, 0:SEQ], ps[:, 0, :])
                V.tensor_copy(PT[:, 1, 0:SEQ], ps[:, 2, :])
                V.tensor_copy(PT[:, 0, SEQ:T], ps[:, 1, 0:NSEQ])
                V.tensor_copy(PT[:, 1, SEQ:T], ps[:, 3, 0:NSEQ]).then_inc(p_dve.sem, 1)
                gated_low(3)
                with dve.Fori(0, 2) as i:
                    for p in range(2):
                        done(L, 68 + 2 * i + p)
                        for q in range(2):
                            m = 4 * i + 2 * p + q
                            last = TT(halves(Xc(m)), pair(4 * p + 2 * q), halves(Xc(m)), ALU.add)
                        last.then_inc(evac, 1)
                        for q in range(2):
                            split_chunk_dve(dve, L, 2, 4 * i + 2 * p + q, q)
                norm_rec(L, 2)
                ffn(L, 72, 64, 2, 1)
                def low(m):
                    dve.wait_ge(hh_ready, L * NH + KD * 4 + m + 1)
                    V.scalar_tensor_tensor(out=Hl[:, m, :], in0=X[:, m, :], scalar=gain(L, 4, m), in1=Hh[:, m, :].bitcast(F32),
                                           op0=ALU.mult, op1=ALU.subtract).then_inc(h_ready, 1)

                def gate(i):
                    done(L, 110 + 2 * i)
                    for q in range(2):
                        last = TT(halves(pg[:, q, :]), pair(2 * q), halves(R[:, :]), ALU.mult)
                    last.then_inc(evac, 1)

                def update(i):
                    done(L, 111 + 2 * i)
                    dve.wait_ge(e_act.sem, e_act.at("s", L, i))
                    for q in range(2):
                        last = TT(halves(pg[:, q, :]), pair(4 + 2 * q), halves(pg[:, q, :]), ALU.mult)
                    last.then_inc(evac, 1)
                    dve.drain()
                    TT(X[:, bass.ds(2 * i, 2), :], X[:, bass.ds(2 * i, 2), :], pg[:, :, :], ALU.add).then_inc(e_dve.sem, 1)
                    dve.drain()

                def squares(i):
                    for q in range(2):
                        dve.wait_ge(sq_ready, L * NH + KD * 4 + 2 * i + (q + 1))
                        TT(acc[:, :], acc[:, :], ta[:, q, :], ALU.add).then_inc(acc_ready, 1)
                        dve.drain()

                with dve.Fori(0, 3) as i:
                    gate(i)
                    update(i)
                    squares(i)
                gate(3)
                for m in range(2):
                    low(m)
                update(3)
                for m in range(2, KD):
                    low(m)
                squares(3)
                norm_rec(L, 4)
            for m in range(KD):
                last = V.scalar_tensor_tensor(out=yT[:, m, :], in0=X[:, m, :], scalar=gains[:, 64 + m:65 + m], in1=R[:, :],
                                              op0=ALU.mult, op1=ALU.mult)
            last.then_inc(fin_dve, 1)
            dve.wait_ge(start_act, 2)
            dve.wait_ge(fin_pe, 1)
            V.memset(acc[:, :], 0.0).then_inc(fin_dve, 1)
            dve.wait_ge(fin_pe, 2)
            V.tensor_copy(ytok[0:NSEQ, 4, :].rearrange("p (b c) -> p b c", b=2), ps[0:NSEQ, 0:2, :]).then_inc(fin, 1)


_CONST = dict(const_core=core_constants, const_mix=mixer_constants)
_OUTS = [
    ("y_prompt", (1, SEQ, D)), ("y_sample", (NSEQ, 1, D)),
    ("k_prompt", (DEPTH, 1, SEQ, H, P)), ("v_prompt", (DEPTH, 1, SEQ, H, P)),
    ("delta_prompt", (DEPTH, 1, H, P, P)), ("conv_prompt", (DEPTH, 1, CONV - 1, NCONV * P)),
    ("k_sample", (DEPTH, NSEQ, 1, H, P)), ("v_sample", (DEPTH, NSEQ, 1, H, P)),
    ("delta_sample", (DEPTH, NSEQ, H, P, P)), ("conv_sample", (DEPTH, NSEQ, CONV - 1, NCONV * P)),
]


def kernel(**inputs):
    import concourse.bacc as bacc
    from concourse.bass_utils import run_bass_kernel_spmd

    nc = bacc.Bacc("TRN2", target_bir_lowering=False, num_devices=1)
    arrays, ins, outs = {}, {}, {}
    for name, a in [*inputs.items(), *((n, f()) for n, f in _CONST.items())]:
        a = np.ascontiguousarray(a)
        arrays[f"in_{name}"] = a
        ins[name] = nc.dram_tensor(f"in_{name}", a.shape, mybir.dt.from_np(a.dtype), kind="ExternalInput").ap()
    for name, shape in _OUTS:
        outs[name] = nc.dram_tensor(f"out_{name}", shape, F32, kind="ExternalOutput").ap()
    hybrid_trunk(nc, ins, outs)
    r = run_bass_kernel_spmd(nc, [arrays], core_ids=[0])
    return tuple(r.results[0][f"out_{name}"] for name, _ in _OUTS)
```
